# Optimizing a Trainium2 kernel written in Bass

```python
import math
import jax, jax.numpy as jnp
from jax import lax
import numpy as np

D_MODEL = 1024
BATCH = 1
SEQ = 512
DEPTH = 1

EPS = 1e-6
GLA_HEADS = 4
GLA_DK = 48
GLA_DV = 96
GLA_GATE_RANK = 16
GLA_GATE_NORM = 16.0
GLA_CHUNK = 64
DSA_HEADS = 6
DSA_DH = 64
IDX_HEADS = 4
IDX_DIM = 32
TOPK_MAX = 256
QUERY_BLOCK = 128
POOL_GROUPS = 4
POOL_GC = 64
POOL_WINDOWS = (2, 4, 8, 16)
REL_BUCKETS = 32
REL_MAX_DIST = 128

GLA_W = GLA_HEADS * GLA_DV
DSA_W = DSA_HEADS * DSA_DH
POOL_W = POOL_GROUPS * POOL_GC
D_MIX = GLA_W + DSA_W + POOL_W

IN_SIZES = (
    GLA_HEADS * GLA_DK,
    GLA_HEADS * GLA_DK,
    GLA_W,
    GLA_GATE_RANK,
    GLA_W,
    DSA_W,
    DSA_W,
    DSA_W,
    DSA_W,
    IDX_HEADS * IDX_DIM,
    IDX_DIM,
    IDX_HEADS,
    POOL_W,
    POOL_W,
)
IN_COLS = sum(IN_SIZES)


def split_cols(p):
    outs = []
    off = 0
    for s in IN_SIZES:
        outs.append(p[..., off:off + s])
        off += s
    return outs

def rmsnorm(x, g):
    xf = x.astype(jnp.float32)
    y = xf * lax.rsqrt(jnp.mean(xf * xf, axis=-1, keepdims=True) + EPS)
    return (y * g.astype(jnp.float32)).astype(x.dtype)

def t5_bucket(rel):
    rel = jnp.maximum(rel, 0)
    max_exact = REL_BUCKETS // 2
    relf = jnp.maximum(rel, 1).astype(jnp.float32)
    large = max_exact + (jnp.log(relf / max_exact) / math.log(REL_MAX_DIST / max_exact)
                         * (REL_BUCKETS - max_exact)).astype(jnp.int32)
    large = jnp.minimum(large, REL_BUCKETS - 1)
    return jnp.where(rel < max_exact, rel, large)

def gla_mixer(q, k, v, glog):
    B, T, H, dk = q.shape
    dv = v.shape[-1]
    N = T // GLA_CHUNK
    def chunk(a):
        return a.astype(jnp.float32).reshape(B, N, GLA_CHUNK, H, a.shape[-1])
    qf, kf, vf, gf = chunk(q), chunk(k), chunk(v), chunk(glog)
    b = jnp.cumsum(gf, axis=2)
    b_last = b[:, :, -1:]
    qe = qf * jnp.exp(b) * (dk ** -0.5)
    ke = kf * jnp.exp(-b)
    kd = kf * jnp.exp(b_last - b)
    A = jnp.einsum('bnihd,bnjhd->bnhij', qe, ke)
    tril = jnp.tril(jnp.ones((GLA_CHUNK, GLA_CHUNK), dtype=bool))
    A = jnp.where(tril, A, 0.0)
    o_intra = jnp.einsum('bnhij,bnjhv->bnihv', A, vf)
    U = jnp.einsum('bnjhd,bnjhv->bnhdv', kd, vf)
    decay = jnp.exp(b_last[:, :, 0])
    def step(S, inp):
        dec, u = inp
        return dec[..., None] * S + u, S
    S0 = jnp.zeros((B, H, dk, dv), jnp.float32)
    _, S_prev = lax.scan(step, S0, (jnp.moveaxis(decay, 1, 0), jnp.moveaxis(U, 1, 0)))
    S_prev = jnp.moveaxis(S_prev, 0, 1)
    o_inter = jnp.einsum('bnihd,bnhdv->bnihv', qe, S_prev)
    return (o_intra + o_inter).reshape(B, T, H, dv)

def dsa_mixer(q, k, v, q_idx, k_idx, w_idx, rel_bias):
    B, T, H, dh = q.shape
    topk = min(TOPK_MAX, T // 4)
    NB = T // QUERY_BLOCK
    def blk(a):
        return jnp.moveaxis(a.reshape(B, NB, QUERY_BLOCK, *a.shape[2:]), 1, 0)
    pos_blk = jnp.arange(T, dtype=jnp.int32).reshape(NB, QUERY_BLOCK)
    key_pos = jnp.arange(T, dtype=jnp.int32)
    kidx_f = k_idx.astype(jnp.float32)
    rb = rel_bias.astype(jnp.float32)

    def body(args):
        qb, qib, wb, tq = args
        s = jax.nn.relu(jnp.einsum('bqhd,bsd->bqhs', qib.astype(jnp.float32), kidx_f)
                        * (IDX_DIM ** -0.5))
        score = jnp.einsum('bqhs,bqh->bqs', s, wb.astype(jnp.float32) * (IDX_HEADS ** -0.5))
        visible = key_pos[None, :] <= tq[:, None]
        score = jnp.where(visible[None], score, -jnp.inf)
        _, idx = lax.top_k(score, topk)
        kg = jax.vmap(lambda kk, ii: kk[ii])(k, idx)
        vg = jax.vmap(lambda vv, ii: vv[ii])(v, idx)
        logits = jnp.einsum('bqhd,bqkhd->bhqk', qb.astype(jnp.float32),
                            kg.astype(jnp.float32)) * (dh ** -0.5)
        rel = tq[None, :, None] - idx
        bias = rb[t5_bucket(rel)]
        logits = logits + jnp.moveaxis(bias, -1, 1)
        logits = jnp.where((rel >= 0)[:, None], logits, -1e30)
        p = jax.nn.softmax(logits, axis=-1)
        o = jnp.einsum('bhqk,bqkhd->bqhd', p, vg.astype(jnp.float32))
        return o.astype(q.dtype)

    o = lax.map(body, (blk(q), blk(q_idx), blk(w_idx), pos_blk))
    return jnp.moveaxis(o, 0, 1).reshape(B, T, H * dh)

def pool_mixer(u, pool_w, pool_scale):
    B, T, _ = u.shape
    ug = u.astype(jnp.float32).reshape(B, T, POOL_GROUPS, POOL_GC)
    cs = jnp.cumsum(ug, axis=1)
    pos = jnp.arange(T, dtype=jnp.int32)
    outs = []
    for gi, w in enumerate(POOL_WINDOWS):
        c = cs[:, :, gi]
        lower = jnp.pad(c, ((0, 0), (w, 0), (0, 0)))[:, :T]
        cnt = jnp.minimum(pos + 1, w).astype(jnp.float32)[None, :, None]
        outs.append((c - lower) / cnt - ug[:, :, gi])
    pooled = jnp.stack(outs, axis=2)
    y = jnp.einsum('btgc,gcd->btgd', pooled, pool_w.astype(jnp.float32)).reshape(B, T, POOL_W)
    return (y * pool_scale.astype(jnp.float32)).astype(u.dtype)

def first_inputs(seed: int = 0) -> dict:
    key = jax.random.key(seed)
    ks = jax.random.split(key, 12)
    f = jnp.float32
    x = jax.random.normal(ks[0], (BATCH, SEQ, D_MODEL), f)
    norm_g = 1.0 + 0.05 * jax.random.normal(ks[1], (DEPTH, D_MODEL), f)
    w_in = jax.random.normal(ks[2], (DEPTH, D_MODEL, IN_COLS), f) * D_MODEL ** -0.5
    gla_gate_w2 = jax.random.normal(ks[3], (DEPTH, GLA_GATE_RANK, GLA_HEADS * GLA_DK), f) * GLA_GATE_RANK ** -0.5
    gla_gate_b = 0.1 * jax.random.normal(ks[4], (DEPTH, GLA_HEADS * GLA_DK), f)
    gla_norm_g = 1.0 + 0.05 * jax.random.normal(ks[5], (DEPTH, GLA_DV), f)
    rel_bias = 0.1 * jax.random.normal(ks[6], (REL_BUCKETS, DSA_HEADS), f)
    pool_w = jax.random.normal(ks[7], (DEPTH, POOL_GROUPS, POOL_GC, POOL_GC), f) * POOL_GC ** -0.5
    pool_scale = 1.0 + 0.1 * jax.random.normal(ks[8], (DEPTH, POOL_W), f)
    w_out = jax.random.normal(ks[9], (DEPTH, D_MIX, D_MODEL), f) * D_MIX ** -0.5
    final_norm_g = 1.0 + 0.05 * jax.random.normal(ks[10], (D_MODEL,), f)
    return {'x': x, 'norm_g': norm_g, 'w_in': w_in, 'gla_gate_w2': gla_gate_w2,
            'gla_gate_b': gla_gate_b, 'gla_norm_g': gla_norm_g, 'rel_bias': rel_bias,
            'pool_w': pool_w, 'pool_scale': pool_scale, 'w_out': w_out,
            'final_norm_g': final_norm_g}

def first_block(x, norm_g, w_in, gla_gate_w2, gla_gate_b, gla_norm_g, rel_bias,
              pool_w, pool_scale, w_out, final_norm_g):
    B, T, _ = x.shape
    for l in range(DEPTH):
        h = rmsnorm(x, norm_g[l])
        p = jnp.einsum('btd,dc->btc', h, w_in[l])
        (gq, gk, gv, gz, ggate, dq, dk, dv, dgate,
         qi, ki, wi, pu, pgate) = split_cols(p)
        glog = jax.nn.log_sigmoid((jnp.einsum('btr,rc->btc', gz, gla_gate_w2[l])
                                   + gla_gate_b[l]).astype(jnp.float32)) / GLA_GATE_NORM
        o_gla = gla_mixer(gq.reshape(B, T, GLA_HEADS, GLA_DK),
                          gk.reshape(B, T, GLA_HEADS, GLA_DK),
                          gv.reshape(B, T, GLA_HEADS, GLA_DV),
                          glog.reshape(B, T, GLA_HEADS, GLA_DK))
        o_gla = rmsnorm(o_gla, gla_norm_g[l]).reshape(B, T, GLA_W).astype(x.dtype)
        y_gla = o_gla * jax.nn.silu(ggate)
        o_dsa = dsa_mixer(dq.reshape(B, T, DSA_HEADS, DSA_DH),
                          dk.reshape(B, T, DSA_HEADS, DSA_DH),
                          dv.reshape(B, T, DSA_HEADS, DSA_DH),
                          qi.reshape(B, T, IDX_HEADS, IDX_DIM), ki, wi, rel_bias)
        y_dsa = o_dsa * jax.nn.silu(dgate)
        y_pool = pool_mixer(pu, pool_w[l], pool_scale[l]) * jax.nn.silu(pgate)
        y = jnp.concatenate([y_gla, y_dsa, y_pool], axis=-1)
        x = x + jnp.einsum('btc,cd->btd', y, w_out[l])
    return rmsnorm(x, final_norm_g)


CHUNK = 64
D_CONV = D_MODEL
CONV_WIDTH = 31
D_SGU = D_MODEL
SGU_BLOCK = 128
SGU_GROUPS = 8
SGU_GROUP_DIM = D_SGU // SGU_GROUPS
D_IN = 2 * D_CONV + 2 * D_SGU + 2 * D_MODEL
SPLITS = (D_CONV, 2 * D_CONV, 2 * D_CONV + 2 * D_SGU, 2 * D_CONV + 2 * D_SGU + D_MODEL)
N_EXPERTS = 32
TOP_K = 4
D_EXPERT = D_MODEL
SWIGLU_LIMIT = 7.0
SWIGLU_ALPHA = 1.702
MOE_BLOCK = 128
LN_EPS = 1e-5
DEEPNORM_ALPHA = float((2 * DEPTH) ** 0.25)
DEEPNORM_BETA = float((8 * DEPTH) ** -0.25)


def _layer_norm(x, gain=None, bias=None):
    xf = x.astype(jnp.float32)
    mu = jnp.mean(xf, axis=-1, keepdims=True)
    var = jnp.mean(jnp.square(xf - mu), axis=-1, keepdims=True)
    y = (xf - mu) * lax.rsqrt(var + LN_EPS)
    if gain is not None:
        y = y * gain.astype(jnp.float32) + bias.astype(jnp.float32)
    return y.astype(x.dtype)

def _causal_depthwise_conv(x, w, b):
    y = lax.conv_general_dilated(
        x, w[:, None, :], window_strides=(1,), padding=[(CONV_WIDTH - 1, 0)],
        dimension_numbers=('NWC', 'WIO', 'NWC'), feature_group_count=x.shape[-1])
    return y + b

def _spatial_gating(u, v, ln_g, ln_b, w_s, b_s):
    B, S, _ = v.shape
    n_blk = S // SGU_BLOCK
    v = _layer_norm(v, ln_g, ln_b).reshape(B, n_blk, SGU_BLOCK, SGU_GROUPS, SGU_GROUP_DIM)
    chunk_id = jnp.arange(SGU_BLOCK) // CHUNK
    mask = chunk_id[:, None] >= chunk_id[None, :]
    w = jnp.where(mask[None], w_s, 0)
    mixed = jnp.einsum('gij,bnjgc->bnigc', w, v) + jnp.transpose(b_s)[None, None, :, :, None]
    return u * mixed.reshape(B, S, D_SGU)

def _token_mixer(h, w_in, b_in, conv_w, conv_b, ln_a_g, ln_a_b, w_a, b_a,
                 ln_v_g, ln_v_b, w_s, b_s, w_b, b_b, w_out, b_out):
    z = h @ w_in + b_in
    a_val, a_gate, sgu, g_a, g_b = jnp.split(z, SPLITS, axis=-1)
    ya = a_val * jax.nn.sigmoid(a_gate)
    ya = _causal_depthwise_conv(ya, conv_w, conv_b)
    ya = jax.nn.silu(_layer_norm(ya, ln_a_g, ln_a_b))
    ya = ya @ w_a + b_a
    u, v = jnp.split(jax.nn.gelu(sgu, approximate=False), 2, axis=-1)
    yb = _spatial_gating(u, v, ln_v_g, ln_v_b, w_s, b_s) @ w_b + b_b
    m = jax.nn.sigmoid(g_a) * ya + jax.nn.sigmoid(g_b) * yb
    return m @ w_out + b_out

def _moe(h, w_router, b_router, w_gu, b_gu, w_dn, b_dn):
    B, S, D = h.shape
    T = B * S
    xt = h.reshape(T, D)
    logits = (xt @ w_router + b_router).astype(jnp.float32)
    top_logits, top_idx = lax.top_k(logits, TOP_K)
    top_w = jax.nn.softmax(top_logits, axis=-1)
    flat_e = top_idx.reshape(-1)
    order = jnp.argsort(flat_e)
    sorted_e = flat_e[order]
    counts = jnp.bincount(flat_e, length=N_EXPERTS)
    padded = (counts + MOE_BLOCK - 1) // MOE_BLOCK * MOE_BLOCK
    start = jnp.cumsum(counts) - counts
    pad_end = jnp.cumsum(padded)
    pad_start = pad_end - padded
    dest = pad_start[sorted_e] + jnp.arange(T * TOP_K) - start[sorted_e]
    n_slots = T * TOP_K + N_EXPERTS * MOE_BLOCK
    n_blocks = n_slots // MOE_BLOCK
    slot_tok = jnp.full((n_slots,), T, jnp.int32).at[dest].set((order // TOP_K).astype(jnp.int32))
    slot_w = jnp.zeros((n_slots,), jnp.float32).at[dest].set(top_w.reshape(-1)[order])
    block_e = jnp.minimum(
        jnp.searchsorted(pad_end, jnp.arange(n_blocks) * MOE_BLOCK, side='right'), N_EXPERTS - 1)
    xt_pad = jnp.concatenate([xt, jnp.zeros((1, D), xt.dtype)], axis=0)

    def expert_block(args):
        tok, e = args
        xb = xt_pad[tok]
        gate, up = jnp.split(xb @ w_gu[e] + b_gu[e], 2, axis=-1)
        gate = jnp.minimum(gate, SWIGLU_LIMIT)
        up = jnp.clip(up, -SWIGLU_LIMIT, SWIGLU_LIMIT)
        act = (up + 1) * (gate * jax.nn.sigmoid(SWIGLU_ALPHA * gate))
        return act @ w_dn[e] + b_dn[e]

    yb = lax.map(expert_block, (slot_tok.reshape(n_blocks, MOE_BLOCK), block_e))
    y = jnp.zeros((T + 1, D), jnp.float32).at[slot_tok].add(
        yb.reshape(n_slots, D).astype(jnp.float32) * slot_w[:, None])
    return y[:T].reshape(B, S, D).astype(h.dtype)

def _normal(k, shape, scale):
    return jax.random.normal(k, shape, jnp.float32) * scale

def second_inputs(seed: int = 0) -> dict:
    key = jax.random.key(seed)
    ks = jax.random.split(key, 32)
    L, D = DEPTH, D_MODEL
    return {
        "x": _normal(ks[0], (BATCH, SEQ, D), 1.0),
        "c": _normal(ks[1], (BATCH, D), 1.0),
        "w_mod": _normal(ks[2], (L, D, 6 * D), 0.5 * D ** -0.5),
        "b_mod": _normal(ks[3], (L, 6 * D), 0.02),
        "w_in": _normal(ks[4], (L, D, D_IN), D ** -0.5),
        "b_in": _normal(ks[5], (L, D_IN), 0.02),
        "conv_w": _normal(ks[6], (L, CONV_WIDTH, D_CONV), CONV_WIDTH ** -0.5),
        "conv_b": _normal(ks[7], (L, D_CONV), 0.02),
        "ln_a_g": 1.0 + _normal(ks[8], (L, D_CONV), 0.05),
        "ln_a_b": _normal(ks[9], (L, D_CONV), 0.02),
        "w_a": _normal(ks[10], (L, D_CONV, D), D_CONV ** -0.5),
        "b_a": _normal(ks[11], (L, D), 0.02),
        "ln_v_g": 1.0 + _normal(ks[12], (L, D_SGU), 0.05),
        "ln_v_b": _normal(ks[13], (L, D_SGU), 0.02),
        "w_s": _normal(ks[14], (L, SGU_GROUPS, SGU_BLOCK, SGU_BLOCK), SGU_BLOCK ** -0.5),
        "b_s": 1.0 + _normal(ks[15], (L, SGU_GROUPS, SGU_BLOCK), 0.1),
        "w_b": _normal(ks[16], (L, D_SGU, D), D_SGU ** -0.5),
        "b_b": _normal(ks[17], (L, D), 0.02),
        "w_out": _normal(ks[18], (L, D, D), DEEPNORM_BETA * D ** -0.5),
        "b_out": _normal(ks[19], (L, D), 0.02),
        "post1_g": 1.0 + _normal(ks[20], (L, D), 0.05),
        "post1_b": _normal(ks[21], (L, D), 0.02),
        "w_router": _normal(ks[22], (L, D, N_EXPERTS), D ** -0.5),
        "b_router": _normal(ks[23], (L, N_EXPERTS), 0.01),
        "w_gu": _normal(ks[24], (L, N_EXPERTS, D, 2 * D_EXPERT), D ** -0.5),
        "b_gu": _normal(ks[25], (L, N_EXPERTS, 2 * D_EXPERT), 0.02),
        "w_dn": _normal(ks[26], (L, N_EXPERTS, D_EXPERT, D), DEEPNORM_BETA * D_EXPERT ** -0.5),
        "b_dn": _normal(ks[27], (L, N_EXPERTS, D), 0.02),
        "post2_g": 1.0 + _normal(ks[28], (L, D), 0.05),
        "post2_b": _normal(ks[29], (L, D), 0.02),
    }

def second_block(x, c, w_mod, b_mod, w_in, b_in, conv_w, conv_b, ln_a_g, ln_a_b, w_a, b_a,
              ln_v_g, ln_v_b, w_s, b_s, w_b, b_b, w_out, b_out, post1_g, post1_b,
              w_router, b_router, w_gu, b_gu, w_dn, b_dn, post2_g, post2_b):
    cond = jax.nn.silu(c)
    for l in range(DEPTH):
        mod = cond @ w_mod[l] + b_mod[l]
        sh1, sc1, g1, sh2, sc2, g2 = [m[:, None, :] for m in jnp.split(mod, 6, axis=-1)]
        h = _layer_norm(x) * (1 + sc1) + sh1
        y = _token_mixer(h, w_in[l], b_in[l], conv_w[l], conv_b[l], ln_a_g[l], ln_a_b[l],
                         w_a[l], b_a[l], ln_v_g[l], ln_v_b[l], w_s[l], b_s[l], w_b[l], b_b[l],
                         w_out[l], b_out[l])
        x = _layer_norm(DEEPNORM_ALPHA * x + g1 * y, post1_g[l], post1_b[l])
        h = _layer_norm(x) * (1 + sc2) + sh2
        y = _moe(h, w_router[l], b_router[l], w_gu[l], b_gu[l], w_dn[l], b_dn[l])
        x = _layer_norm(DEEPNORM_ALPHA * x + g2 * y, post2_g[l], post2_b[l])
    return x


D_MIX_3 = 2 * D_MODEL
SSD_WIDTH = D_MIX_3 // 2
SSD_HEAD_DIM = 64
SSD_HEADS = SSD_WIDTH // SSD_HEAD_DIM
SSD_GROUPS = 2
SSD_HPG = SSD_HEADS // SSD_GROUPS
SSD_STATE = 128
SSD_CONV = 5
SSD_CHUNK = 64
XBC_WIDTH = SSD_WIDTH + 2 * SSD_GROUPS * SSD_STATE
HG_WIDTH = D_MIX_3 - SSD_WIDTH
HG_EXPAND = 128
HG_HEADS = HG_WIDTH // HG_EXPAND
HG_DK = HG_EXPAND
HG_DV = HG_WIDTH // HG_HEADS
HG_CHUNK = 32
D_FF = 4 * D_MODEL
N_MOD = 6
LB_FLOOR = 1e-30

IN_SIZES_3 = (SSD_WIDTH, XBC_WIDTH, SSD_HEADS, HG_WIDTH, HG_WIDTH, HG_WIDTH, HG_WIDTH, HG_WIDTH)
D_IN_PROJ = sum(IN_SIZES_3)
IN_SPLITS = tuple(np.cumsum(IN_SIZES_3)[:-1].tolist())


def rmsnorm_3(x, w):
    xf = x.astype(jnp.float32)
    y = xf * lax.rsqrt(jnp.mean(xf * xf, axis=-1, keepdims=True) + EPS)
    return (y * w.astype(jnp.float32)).astype(x.dtype)

def to_chunks(a, chunk):
    b, l = a.shape[:2]
    return jnp.moveaxis(a.reshape(b, l // chunk, chunk, *a.shape[2:]), 1, 0)

def from_chunks(a):
    n, b, chunk = a.shape[:3]
    return jnp.moveaxis(a, 0, 1).reshape(b, n * chunk, *a.shape[3:])

def flip_seq(a):
    return jnp.flip(a, axis=1)

def masked_decay(seg, tri):
    return jnp.where(tri, jnp.exp(jnp.where(tri, seg, 0.0)), 0.0)

def depthwise_conv_centred(x, w):
    k = w.shape[0]
    return lax.conv_general_dilated(
        x, w[:, None, :].astype(x.dtype), window_strides=(1,),
        padding=[(k // 2, k // 2)], dimension_numbers=("NWC", "WIO", "NWC"),
        feature_group_count=x.shape[-1])

def ssd_direction(xh, bg, cg, dt, a_neg):
    bsz = xh.shape[0]
    log_a = dt * a_neg
    xs = tuple(to_chunks(t, SSD_CHUNK) for t in (xh, bg, cg, dt, log_a))
    tri = jnp.tril(jnp.ones((SSD_CHUNK, SSD_CHUNK), dtype=bool))[None, :, :, None, None]

    def step(state, inp):
        xc, bc, cc, dtc, ac = inp
        cum = jnp.cumsum(ac, axis=1)
        seg = cum[:, :, None] - cum[:, None, :]
        decay = masked_decay(seg, tri)
        scores = jnp.einsum("btgn,bsgn->btsg", cc, bc)
        w = scores[..., None] * decay * dtc[:, None]
        y_intra = jnp.einsum("btsgh,bsghp->btghp", w, xc)
        y_inter = jnp.einsum("btgn,bghpn->btghp", cc, state) * jnp.exp(cum)[..., None]
        w_state = jnp.exp(cum[:, -1:] - cum) * dtc
        new_state = (jnp.exp(cum[:, -1])[..., None, None] * state
                     + jnp.einsum("bsgh,bsghp,bsgn->bghpn", w_state, xc, bc))
        return new_state, y_intra + y_inter

    init = jnp.zeros((bsz, SSD_GROUPS, SSD_HPG, SSD_HEAD_DIM, SSD_STATE), jnp.float32)
    _, ys = lax.scan(step, init, xs)
    return from_chunks(ys)

def ssd_mixer(z, xbc, dt_raw, conv_w, conv_b, dt_bias, a_log, d_skip, norm_w):
    f32 = jnp.float32
    bsz, seqlen = z.shape[:2]
    xbc = jax.nn.silu(depthwise_conv_centred(xbc, conv_w) + conv_b.astype(xbc.dtype))
    xm, bm, cm = jnp.split(xbc, (SSD_WIDTH, SSD_WIDTH + SSD_GROUPS * SSD_STATE), axis=-1)
    xh = xm.astype(f32).reshape(bsz, seqlen, SSD_GROUPS, SSD_HPG, SSD_HEAD_DIM)
    bg = bm.astype(f32).reshape(bsz, seqlen, SSD_GROUPS, SSD_STATE)
    cg = cm.astype(f32).reshape(bsz, seqlen, SSD_GROUPS, SSD_STATE)
    y = xh * d_skip.astype(f32).reshape(SSD_GROUPS, SSD_HPG)[..., None]
    for d in range(2):
        dt = jax.nn.softplus(dt_raw.astype(f32) + dt_bias[d].astype(f32))
        dt = dt.reshape(bsz, seqlen, SSD_GROUPS, SSD_HPG)
        a_neg = -jnp.exp(a_log[d].astype(f32)).reshape(SSD_GROUPS, SSD_HPG)
        if d == 0:
            y = y + ssd_direction(xh, bg, cg, dt, a_neg)
        else:
            y = y + flip_seq(ssd_direction(flip_seq(xh), flip_seq(bg), flip_seq(cg), flip_seq(dt), a_neg))
    y = y.reshape(bsz, seqlen, SSD_WIDTH)
    return rmsnorm_3(y * jax.nn.silu(z.astype(f32)), norm_w)

def hgrn2_direction(q, log_f, k, v):
    bsz = q.shape[0]
    xs = tuple(to_chunks(t, HG_CHUNK) for t in (q, log_f, k, v))
    tri = jnp.tril(jnp.ones((HG_CHUNK, HG_CHUNK), dtype=bool))[None, :, :, None, None]

    def step(state, inp):
        qc, gc, kc, vc = inp
        cum = jnp.cumsum(gc, axis=1)
        seg = cum[:, :, None] - cum[:, None, :]
        decay = masked_decay(seg, tri)
        attn = jnp.einsum("bthk,btshk,bshk->btsh", qc, decay, kc)
        y_intra = jnp.einsum("btsh,bshv->bthv", attn, vc)
        y_inter = jnp.einsum("bthk,bhkv->bthv", qc * jnp.exp(cum), state)
        cum_end = cum[:, -1]
        new_state = (jnp.exp(cum_end)[..., None] * state
                     + jnp.einsum("bshk,bshv->bhkv", kc * jnp.exp(cum_end[:, None] - cum), vc))
        return new_state, y_intra + y_inter

    init = jnp.zeros((bsz, HG_HEADS, HG_DK, HG_DV), jnp.float32)
    _, ys = lax.scan(step, init, xs)
    return from_chunks(ys)

def hgrn2_mixer(q, f_fwd, f_bwd, i, g, lb, norm_w):
    f32 = jnp.float32
    bsz, seqlen = q.shape[:2]
    heads = lambda t: t.astype(f32).reshape(bsz, seqlen, HG_HEADS, -1)
    qh, vh = heads(q), heads(i)
    y = jnp.zeros((bsz, seqlen, HG_HEADS, HG_DV), f32)
    for d, f_raw in enumerate((f_fwd, f_bwd)):
        lbd = lb[d].reshape(HG_HEADS, HG_DK)
        fh = heads(f_raw)
        log_f = jnp.logaddexp(jnp.log(jnp.maximum(lbd, LB_FLOOR)),
                              jnp.log1p(-lbd) + jax.nn.log_sigmoid(fh))
        kh = (1.0 - lbd) * jax.nn.sigmoid(-fh)
        if d == 0:
            y = y + hgrn2_direction(qh, log_f, kh, vh)
        else:
            y = y + flip_seq(hgrn2_direction(flip_seq(qh), flip_seq(log_f), flip_seq(kh), flip_seq(vh)))
    y = rmsnorm_3(y, norm_w).reshape(bsz, seqlen, HG_WIDTH)
    return y * jax.nn.silu(g.astype(f32))

def math_log(v):
    return float(np.log(v))

def third_inputs(seed: int = 0) -> dict:
    key = jax.random.key(seed)
    ks = jax.random.split(key, 20)
    nrm = jax.random.normal
    f32 = jnp.float32
    x = nrm(ks[0], (BATCH, SEQ, D_MODEL), f32)
    c = nrm(ks[1], (BATCH, D_MODEL), f32)
    ada_w = nrm(ks[2], (DEPTH, D_MODEL, N_MOD * D_MODEL), f32) * (0.5 * D_MODEL ** -0.5)
    ada_b = nrm(ks[3], (DEPTH, N_MOD * D_MODEL), f32) * 0.02
    norm_mix_w = 1.0 + 0.02 * nrm(ks[4], (DEPTH, D_MODEL), f32)
    norm_mlp_w = 1.0 + 0.02 * nrm(ks[5], (DEPTH, D_MODEL), f32)
    w_in = nrm(ks[6], (DEPTH, D_MODEL, D_IN_PROJ), f32) * D_MODEL ** -0.5
    conv_w = nrm(ks[7], (DEPTH, SSD_CONV, XBC_WIDTH), f32) * SSD_CONV ** -0.5
    conv_b = nrm(ks[8], (DEPTH, XBC_WIDTH), f32) * 0.02
    dt0 = jnp.exp(jax.random.uniform(ks[9], (DEPTH, 2, SSD_HEADS), f32,
                                     minval=math_log(1e-3), maxval=math_log(1e-1)))
    dt_bias = dt0 + jnp.log(-jnp.expm1(-dt0))
    a_log = jnp.log(jax.random.uniform(ks[10], (DEPTH, 2, SSD_HEADS), f32, minval=1.0, maxval=16.0))
    d_skip = 1.0 + 0.1 * nrm(ks[11], (DEPTH, SSD_HEADS), f32)
    ssd_norm_w = 1.0 + 0.02 * nrm(ks[12], (DEPTH, SSD_WIDTH), f32)
    hg_lower_bounds = 0.5 * nrm(ks[13], (2, DEPTH, HG_WIDTH), f32)
    hg_norm_w = 1.0 + 0.02 * nrm(ks[14], (DEPTH, HG_DV), f32)
    w_out = nrm(ks[15], (DEPTH, D_MIX_3, D_MODEL), f32) * D_MIX_3 ** -0.5
    w_up = nrm(ks[16], (DEPTH, D_MODEL, D_FF), f32) * D_MODEL ** -0.5
    w_down = nrm(ks[17], (DEPTH, D_FF, D_MODEL), f32) * D_FF ** -0.5
    final_norm_w = 1.0 + 0.02 * nrm(ks[18], (D_MODEL,), f32)
    return {"x": x, "c": c, "ada_w": ada_w, "ada_b": ada_b, "norm_mix_w": norm_mix_w,
            "norm_mlp_w": norm_mlp_w, "w_in": w_in, "conv_w": conv_w, "conv_b": conv_b,
            "dt_bias": dt_bias, "a_log": a_log, "d_skip": d_skip, "ssd_norm_w": ssd_norm_w,
            "hg_lower_bounds": hg_lower_bounds, "hg_norm_w": hg_norm_w, "w_out": w_out,
            "w_up": w_up, "w_down": w_down, "final_norm_w": final_norm_w}

def third_block(x, c, ada_w, ada_b, norm_mix_w, norm_mlp_w, w_in, conv_w, conv_b, dt_bias, a_log,
              d_skip, ssd_norm_w, hg_lower_bounds, hg_norm_w, w_out, w_up, w_down, final_norm_w):
    p = jax.nn.softmax(hg_lower_bounds.astype(jnp.float32), axis=1)
    lower_bounds = jnp.cumsum(p, axis=1) - p[:, :1]
    c_act = jax.nn.silu(c)
    for l in range(DEPTH):
        mod = c_act @ ada_w[l] + ada_b[l]
        shift1, scale1, gate1, shift2, scale2, gate2 = jnp.split(mod[:, None, :], N_MOD, axis=-1)
        h = rmsnorm_3(x, norm_mix_w[l]) * (1.0 + scale1) + shift1
        proj = h @ w_in[l]
        z, xbc, dt_raw, q, f_fwd, f_bwd, i, g = jnp.split(proj, IN_SPLITS, axis=-1)
        y_ssd = ssd_mixer(z, xbc, dt_raw, conv_w[l], conv_b[l], dt_bias[l], a_log[l],
                          d_skip[l], ssd_norm_w[l])
        y_hg = hgrn2_mixer(q, f_fwd, f_bwd, i, g, lower_bounds[:, l], hg_norm_w[l])
        y = jnp.concatenate([y_ssd, y_hg], axis=-1).astype(x.dtype) @ w_out[l]
        x = x + gate1 * y
        h = rmsnorm_3(x, norm_mlp_w[l]) * (1.0 + scale2) + shift2
        x = x + gate2 * (jnp.square(jax.nn.relu(h @ w_up[l])) @ w_down[l])
    return rmsnorm_3(x, final_norm_w)


_first_inputs = third_inputs


def third_inputs(seed=0):
    import zlib

    import numpy as np

    out = dict(_first_inputs(seed))
    spreads = {}
    factors = {'norm_mix_w': 6.605,
     'norm_mlp_w': 6.286,
     'conv_b': 8.0,
     'd_skip': 5.722,
     'ssd_norm_w': 8.0,
     'hg_norm_w': 8.0,
     'final_norm_w': 2.907}
    for name, (base, spread) in spreads.items():
        noise = np.random.default_rng([zlib.crc32(name.encode()), seed]).standard_normal(out[name].shape)
        drawn = base * np.exp(spread * noise) if base else spread * noise
        out[name] = __import__('jax').numpy.asarray(drawn.astype(out[name].dtype))
    for name, factor in factors.items():
        out[name] = (out[name] * factor).astype(out[name].dtype)
    return out


_narrow_inputs = third_inputs


def third_inputs(seed=0):

    out = dict(_narrow_inputs(seed))
    wider = {'conv_b': 10.64, 'd_skip': 12.0, 'ssd_norm_w': 12.0, 'final_norm_w': 3.24}
    for name, times in wider.items():
        mean = out[name].mean()
        out[name] = (mean + times * (out[name] - mean)).astype(out[name].dtype)
    return out


def setup_inputs(seed=0):
    out = dict(first_inputs(seed))
    for name, value in second_inputs(seed + 1).items():
        if name != "x":
            out[name + "_2"] = value
    for name, value in third_inputs(seed + 2).items():
        if name != "x":
            out[name + "_3"] = value
    return out


def reference(
    x, norm_g, w_in, gla_gate_w2, gla_gate_b, gla_norm_g, rel_bias, pool_w, pool_scale, w_out,
    final_norm_g, c_2, w_mod_2, b_mod_2, w_in_2, b_in_2, conv_w_2, conv_b_2, ln_a_g_2, ln_a_b_2,
    w_a_2, b_a_2, ln_v_g_2, ln_v_b_2, w_s_2, b_s_2, w_b_2, b_b_2, w_out_2, b_out_2, post1_g_2,
    post1_b_2, w_router_2, b_router_2, w_gu_2, b_gu_2, w_dn_2, b_dn_2, post2_g_2, post2_b_2,
    c_3, ada_w_3, ada_b_3, norm_mix_w_3, norm_mlp_w_3, w_in_3, conv_w_3, conv_b_3, dt_bias_3,
    a_log_3, d_skip_3, ssd_norm_w_3, hg_lower_bounds_3, hg_norm_w_3, w_out_3, w_up_3, w_down_3,
    final_norm_w_3,
):
    x = first_block(
        x, norm_g, w_in, gla_gate_w2, gla_gate_b, gla_norm_g, rel_bias, pool_w, pool_scale,
        w_out, final_norm_g,
    )
    x = second_block(
        x, c_2, w_mod_2, b_mod_2, w_in_2, b_in_2, conv_w_2, conv_b_2, ln_a_g_2, ln_a_b_2, w_a_2,
        b_a_2, ln_v_g_2, ln_v_b_2, w_s_2, b_s_2, w_b_2, b_b_2, w_out_2, b_out_2, post1_g_2,
        post1_b_2, w_router_2, b_router_2, w_gu_2, b_gu_2, w_dn_2, b_dn_2, post2_g_2, post2_b_2,
    )
    return third_block(
        x, c_3, ada_w_3, ada_b_3, norm_mix_w_3, norm_mlp_w_3, w_in_3, conv_w_3, conv_b_3,
        dt_bias_3, a_log_3, d_skip_3, ssd_norm_w_3, hg_lower_bounds_3, hg_norm_w_3, w_out_3,
        w_up_3, w_down_3, final_norm_w_3,
    )


_drawn_inputs = setup_inputs


def setup_inputs(seed=0):
    import zlib

    import numpy as np

    out = dict(_drawn_inputs(seed))
    spreads = {}
    factors = {'rel_bias': 3.653,
     'b_in_2': 8.0,
     'conv_b_2': 6.629,
     'ln_a_g_2': 4.221,
     'ln_a_b_2': 8.0,
     'b_a_2': 6.771,
     'ln_v_g_2': 6.066,
     'ln_v_b_2': 8.0,
     'b_s_2': 2.95,
     'b_b_2': 7.835,
     'b_out_2': 2.959,
     'b_router_2': 4.763,
     'b_gu_2': 8.0,
     'b_dn_2': 7.074,
     'norm_mlp_w_3': 7.411,
     'd_skip_3': 64.0,
     'hg_norm_w_3': 21.168,
     'dt_bias_3': 3.712,
     'a_log_3': 3.621,
     'ssd_norm_w_3': 7.639}
    for name, (base, spread) in spreads.items():
        noise = np.random.default_rng([zlib.crc32(name.encode()), seed]).standard_normal(out[name].shape)
        drawn = base * np.exp(spread * noise) if base else spread * noise
        out[name] = __import__('jax').numpy.asarray(drawn.astype(out[name].dtype))
    for name, factor in factors.items():
        out[name] = (out[name] * factor).astype(out[name].dtype)
    return out
```

```python
import math
from contextlib import ExitStack

import numpy as np

import concourse.bass as bass
from concourse import mybir

ACT = mybir.ActivationFunctionType
ALU = mybir.AluOpType
AX = mybir.AxisListType.X
F32 = mybir.dt.float32
U32 = mybir.dt.uint32

P = 128
T = 512
D = 1024
KT = D // P
TT = T // P
EPS = 1e-6
LN_EPS = 1e-5

GLA_H, GLA_DK, GLA_DV, GLA_RANK, GLA_CHUNK = 4, 48, 96, 16, 64
DSA_H, DSA_DH, IDX_H, IDX_DIM = 6, 64, 4, 32
TOPK = min(256, T // 4)
BUCKETS, MAX_DIST = 32, 128
POOL_W = 256
WINDOWS = (2, 4, 8, 16)
NEG_HIDDEN = -3.0e38
NEG_TAKEN = -3.4e38



def bucket_of(rel):
    rel = np.maximum(rel, 0)
    exact = BUCKETS // 2
    relf = np.maximum(rel, 1).astype(np.float32)
    large = exact + (np.log(relf / np.float32(exact)) / np.float32(math.log(MAX_DIST / exact))
                     * np.float32(BUCKETS - exact)).astype(np.int32)
    return np.where(rel < exact, rel, np.minimum(large, BUCKETS - 1))


def constant_parts():
    i = np.arange(P)
    row, col = i[:, None], i[None, :]
    t = np.arange(T)
    parts = {}
    parts["ident"] = (row == col)
    parts["flip"] = (row + col == P - 1)
    parts["gla_pairs"] = (row <= col) & (row // GLA_CHUNK == col // GLA_CHUNK)
    parts["hidden"] = -1.0 * (col > row)
    parts["upto"] = (row <= col)
    parts["from"] = (row >= col)
    parts["reset64"] = np.broadcast_to(t % 64 != 0, (P, T))
    parts["reset128"] = np.broadcast_to(t % 128 != 0, (P, T))
    w = np.repeat(np.array(WINDOWS), P // 2).reshape(2, P)
    parts["inv_count"] = np.concatenate([1.0 / np.minimum(t[None, :] + 1, w[k][:, None]) for k in range(2)], 1)
    u = np.arange(5 * P)
    onehot = np.zeros((P, 5 * P))
    onehot[:BUCKETS] = bucket_of(T - 1 - u)[None, :] == np.arange(BUCKETS)[:, None]
    parts["bucket"] = onehot
    parts["sgu_mask"] = (col // 64 >= row // 64)
    head = np.arange(P)
    parts["one_head"] = head[:, None] == np.arange(16).repeat(P)[None, :]
    parts["two_heads"] = head[:, None] == np.arange(16).repeat(P // 2)[None, :]
    levels = [(row // (2 * m) == col // (2 * m)) & (row // m % 2 == 0) & (col // m % 2 == 1)
              for m in (64, 32, 16, 8, 4, 2, 1)]
    parts["levels"] = np.concatenate(levels + [row == col], 1)
    parts["levels_back"] = np.concatenate([a.T for a in levels] + [row == col], 1)
    parts["slots"] = np.broadcast_to(i, (P, P))
    parts["numbers"] = np.broadcast_to(np.arange(16).repeat(32), (P, 512))
    return parts


def constant_layout():
    at, where = 0, {}
    for name, a in constant_parts().items():
        where[name] = (at, a.shape[1])
        at += a.shape[1]
    return where, at


class Count:

    def __init__(self, sem):
        self.sem, self.n = sem, 0

    def by(self, instruction):
        instruction.then_inc(self.sem, 1)
        self.n += 1
        return self.n


class Core:

    def __init__(self, nc, ctx, consts):
        self.nc, self.ctx, self.consts = nc, ctx, consts
        self.where, _ = constant_layout()
        self.bank = [ctx.enter_context(nc.psum_tensor(f"bank{i}", [P, 512], F32)) for i in range(8)]
        self.stage_n = 0

    def const(self, name, rows=P):
        at, n = self.where[name]
        return self.consts[0:rows, at:at + n]


def clear_used(nc, used):
    used.sort()
    while used:
        n = 1
        while n < len(used) and used[n] == used[0] + n:
            n += 1
        nc.gpsimd.sem_clear(range(used[0], used[0] + n))
        del used[:n]
    nc.all_engine_barrier()


USED = []


def sems(nc, ctx, *names):
    if len(USED) > 80:
        clear_used(nc, USED)
    out = [ctx.enter_context(nc.semaphore(n)) for n in names]
    assert not {s.num for s in out} & set(USED)
    ctx.callback(USED.extend, [s.num for s in out])
    return out


def bufs(nc, ctx, prefix, **shapes):
    out = []
    for name, shape in shapes.items():
        out.append(ctx.enter_context(nc.sbuf_tensor(f"{prefix}_{name}", list(shape), F32)))
    return out


def columns(vector, n=P):
    return vector.rearrange("(t p) -> p t", p=n)


def bcast_rows(row, n=P):
    return row.to_broadcast([n, row.shape[1]])


def load_x(core, x, xT, ident, ones):
    nc = core.nc
    with ExitStack() as ctx:
        (rows,) = bufs(nc, ctx, "lx", rows=[P, TT, D])
        loaded, turned, copied, ones_set = sems(nc, ctx, "lx_loaded", "lx_turned", "lx_copied", "lx_ones")
        block = ctx.enter_context(nc.Block())

        @block.sync
        def _(sp):
            sp.dma_start(ident[:], core.const("ident")).then_inc(loaded, 16)
            sp.dma_start(rows[:], x.rearrange("(t p) d -> p t d", p=P)).then_inc(loaded, 16)

        @block.gpsimd
        def _(pool):
            nc.gpsimd.memset(ones[:], 1.0).then_inc(ones_set, 1)

        @block.tensor
        def _(pe):
            pe.wait_ge(loaded, 32)
            for k in range(KT):
                for t in range(TT):
                    mm = nc.tensor.transpose(core.bank[k][:, t * P:(t + 1) * P],
                                             rows[:, t, k * P:(k + 1) * P], ident[:])
                mm.then_inc(turned, 1)

        @block.scalar
        def _(act):
            for k in range(KT):
                act.wait_ge(turned, k + 1)
                nc.scalar.copy(xT[:, k, :], core.bank[k][:]).then_inc(copied, 1)


def norm(core, name, src, dst, ones, scratch, gain, bias=None, centre=False, func=None, eps=EPS):
    nc = core.nc
    func = func or ACT.Identity
    mean_ps, square_ps = core.bank[0], core.bank[1]
    with ExitStack() as ctx:
        part, rstd, eps_col = bufs(nc, ctx, name, part=[P, T], rstd=[P, T], eps=[P, 1])
        eps_set, part_ready, sum_ready, centred, squared, std_ready, inv_ready, normed, done = sems(
            nc, ctx, *(f"{name}_{s}" for s in ("eps", "part", "sum", "centred", "squared", "std", "inv",
                                               "normed", "done")))
        block = ctx.enter_context(nc.Block())
        middle = dst if centre else src

        @block.gpsimd
        def _(pool):
            nc.gpsimd.memset(eps_col[:], eps).then_inc(eps_set, 1)

        @block.tensor
        def _(pe):
            if centre:
                pe.wait_ge(part_ready, 1)
                nc.tensor.matmul(mean_ps[:], ones[:], part[:], start=True, stop=True).then_inc(sum_ready, 1)
            pe.wait_ge(part_ready, 1 + centre)
            nc.tensor.matmul(square_ps[:], ones[:], part[:], start=True, stop=True).then_inc(sum_ready, 1)

        @block.vector
        def _(dve):
            if centre:
                nc.vector.reduce_sum(part[:], src[:].rearrange("p k t -> p t k"), AX).then_inc(part_ready, 1)
                dve.wait_ge(sum_ready, 1)
                for k in range(KT):
                    nc.vector.scalar_tensor_tensor(out=dst[:, k, :], in0=mean_ps[:], scalar=-1.0 / D,
                                                   in1=src[:, k, :], op0=ALU.mult,
                                                   op1=ALU.add).then_inc(centred, 1)
            dve.wait_ge(squared, KT)
            nc.vector.reduce_sum(part[:], scratch[:].rearrange("p k t -> p t k"), AX).then_inc(part_ready, 1)
            dve.wait_ge(std_ready, 1)
            nc.vector.reciprocal(rstd[:], rstd[:]).then_inc(inv_ready, 1)
            dve.wait_ge(inv_ready, 1)
            for k in range(KT):
                nc.vector.tensor_tensor(scratch[:, k, :], middle[:, k, :], rstd[:],
                                        ALU.mult).then_inc(normed, 1)

        @block.scalar
        def _(act):
            for k in range(KT):
                if centre:
                    act.wait_ge(centred, k + 1)
                nc.scalar.activation(scratch[:, k, :], middle[:, k, :], ACT.Square).then_inc(squared, 1)
            act.wait_ge(eps_set, 1)
            act.wait_ge(sum_ready, 1 + centre)
            nc.scalar.activation(rstd[:], square_ps[:], ACT.Sqrt, bias=eps_col[:],
                                 scale=1.0 / D).then_inc(std_ready, 1)
            for k in range(KT):
                act.wait_ge(normed, k + 1)
                nc.scalar.activation(dst[:, k, :], scratch[:, k, :], func, scale=gain[:, k:k + 1],
                                     bias=0.0 if bias is None else bias[:, k:k + 1]).then_inc(done, 1)


OFF = {}
_at = 0
for _n, _w in (("gq", 192), ("gk", 192), ("gv", 384), ("gz", 16), ("ggate", 384), ("dq", 384), ("dk", 384),
               ("dv", 384), ("dgate", 384), ("qi", 128), ("ki", 32), ("wi", 4), ("pu", 256), ("pgate", 256)):
    OFF[_n] = _at
    _at += _w
IN_COLS = _at


def projection(core, hT, w_in, to):
    nc = core.nc
    chunks = []

    def chunk(names, tiles):
        first = OFF[names[0]]
        last = names[-1]
        width = {"gk": 192, "gv": 384, "ggate": 384, "dq": 384, "dk": 384, "dv": 384, "dgate": 384,
                 "wi": 4, "pgate": 256}[last]
        chunks.append((first, OFF[last] + width - first, tiles))

    gq, gk = to["gq"], to["gk"]
    chunk(["gq", "gk"], [("c", h * GLA_DK, GLA_DK, gq[:, h, :], ACT.Identity) for h in range(GLA_H)]
          + [("c", 192 + h * GLA_DK, GLA_DK, gk[:, h, :], ACT.Identity) for h in range(GLA_H)])
    chunk(["gv"], [("t", 0, 384, to["gv"][:, t, :], t) for t in range(TT)])
    chunk(["dq"], [("c", k * P, P, to["dq"][:, k, :], ACT.Identity) for k in range(3)])
    chunk(["dk"], [("c", k * P, P, to["dk"][:, k, :], ACT.Identity) for k in range(3)])
    chunk(["dv"], [("t", 0, 384, to["dv"][:, t, :], t) for t in range(TT)])
    chunk(["qi", "ki", "wi"], [("c", 0, P, to["qi"][:], ACT.Identity), ("r", P, P, to["ki"][:], ACT.Identity)]
          + [("t", 160, IDX_H, to["wi"][:, t, :], t) for t in range(TT)])
    chunk(["pu", "pgate"], [("c", k * P, P, to["pu"][:, k, :], ACT.Identity) for k in range(2)]
          + [("c", POOL_W + k * P, P, to["pgate"][:, k, :], ACT.Silu) for k in range(2)])
    chunk(["gz", "ggate"], [("c", 0, GLA_RANK, to["gz"][:], ACT.Identity)]
          + [("c", GLA_RANK + h * GLA_DV, GLA_DV, to["ggate"][:, h, :], ACT.Silu) for h in range(GLA_H)])
    chunk(["dgate"], [("c", k * P, P, to["dgate"][:, k, :], ACT.Silu) for k in range(3)])
    tiles_before = [sum(len(c[2]) for c in chunks[:i]) for i in range(len(chunks) + 1)]
    SLOTS = 3
    w_v = w_in.rearrange("(k p) n -> p k n", p=P)
    with ExitStack() as ctx:
        w, ki4 = bufs(nc, ctx, "proj", w=[P, SLOTS, KT, 512], ki4=[P, KT, P])
        loaded = sems(nc, ctx, *(f"proj_loaded{s}" for s in range(SLOTS)))
        product, copied, repeated = sems(nc, ctx, "proj_product", "proj_copied", "proj_repeated")
        block = ctx.enter_context(nc.Block())

        @block.sync
        def _(sp):
            for c, (first, width, _) in enumerate(chunks):
                if c >= SLOTS:
                    sp.wait_ge(product, tiles_before[c - SLOTS + 1])
                sp.dma_start(w[:, c % SLOTS, :, 0:width],
                             w_v[:, :, first:first + width]).then_inc(loaded[c % SLOTS], 16)

        @block.vector
        def _(dve):
            c = 5
            dve.wait_ge(loaded[c % SLOTS], 16 * (c // SLOTS + 1))
            for j in range(IDX_H):
                nc.vector.tensor_copy(ki4[:, :, j * IDX_DIM:(j + 1) * IDX_DIM],
                                      w[:, c % SLOTS, :, P:P + IDX_DIM]).then_inc(repeated, 1)

        @block.tensor
        def _(pe):
            n = 0
            for c, (_, _, tiles) in enumerate(chunks):
                pe.wait_ge(loaded[c % SLOTS], 16 * (c // SLOTS + 1))
                for layout, at, width, _, extra in tiles:
                    if n >= 8:
                        pe.wait_ge(copied, n - 7)
                    if layout == "r":
                        pe.wait_ge(repeated, IDX_H)
                    bank = core.bank[n % 8]
                    for k in range(KT):
                        weight = w[:, c % SLOTS, k, at:at + width]
                        if layout == "t":
                            out, left, right = bank[:, 0:width], hT[:, k, extra * P:(extra + 1) * P], weight
                        else:
                            out, right = bank[0:width, :], hT[:, k, :]
                            left = weight if layout == "c" else ki4[:, k, :]
                        mm = nc.tensor.matmul(out, left, right, start=(k == 0), stop=(k == KT - 1))
                    mm.then_inc(product, 1)
                    n += 1

        @block.scalar
        def _(act):
            n = 0
            for _, _, tiles in chunks:
                for layout, _, width, out, extra in tiles:
                    act.wait_ge(product, n + 1)
                    bank = core.bank[n % 8]
                    if layout == "t":
                        nc.scalar.activation(out, bank[:, 0:width], ACT.Identity).then_inc(copied, 1)
                    else:
                        nc.scalar.activation(out, bank[0:width, :], extra).then_inc(copied, 1)
                    n += 1


def gla(core, to, ones, ident, gate_w2, gate_b, norm_g, y):
    nc = core.nc
    B = core.bank
    CH = T // GLA_CHUNK
    C = GLA_CHUNK
    gq, gk, gv, gz, gate = (to[n] for n in ("gq", "gk", "gv", "gz", "ggate"))
    with ExitStack() as ctx:
        w2, gb, ng, mask, reset, eps_col, z, lsig, b, e, ke, kd, kdT, S, AT = bufs(
            nc, ctx, "gla", w2=[GLA_RANK, 192], gb=[GLA_DK, GLA_H], ng=[GLA_DV, 1], mask=[P, P],
            reset=[GLA_DK, GLA_H, T], eps=[P, 1], z=[GLA_DV, GLA_H, T], lsig=[GLA_DK, GLA_H, T],
            b=[GLA_DK, GLA_H, T], e=[GLA_DK, GLA_H, T], ke=[GLA_DK, GLA_H, T],
            kd=[GLA_DK, GLA_H, T], kdT=[P, GLA_H, TT, GLA_DK], S=[GLA_DK, GLA_H, CH, GLA_DV],
            AT=[P, GLA_H, T])
        qe = gq
        sq, z = z, z[0:GLA_DK]
        loaded, zeroed, pe_done, act_done, dve_done, chained = sems(
            nc, ctx, "gla_loaded", "gla_zeroed", "gla_product", "gla_scalar", "gla_vector", "gla_state")
        block = ctx.enter_context(nc.Block())
        bc = b[:].rearrange("p h (c t) -> p (h c) t", t=C)

        @block.sync
        def _(sp):
            sp.dma_start(w2[:], gate_w2).then_inc(loaded, 16)
            with nc.allow_non_contiguous_dma("a few columns"):
                sp.dma_start(gb[:], columns(gate_b, GLA_DK)).then_inc(loaded, 16)
                sp.dma_start(ng[:], columns(norm_g, GLA_DV)).then_inc(loaded, 16)
            sp.dma_start(mask[:], core.const("gla_pairs")).then_inc(loaded, 16)
            for h in range(GLA_H):
                sp.dma_start(reset[:, h, :], core.const("reset64", GLA_DK)).then_inc(loaded, 16)

        @block.gpsimd
        def _(pool):
            nc.gpsimd.memset(S[:, :, 0, :], 0.0).then_inc(zeroed, 1)
            nc.gpsimd.memset(eps_col[:], EPS).then_inc(zeroed, 1)

        PE_GATE, PE_TURN, PE_U, PE_A, PE_O, PE_NORM = 4, 8, 12, 16, 20, 24

        @block.tensor
        def _(pe):
            pe.wait_ge(loaded, 16 * 8)
            for h in range(GLA_H):
                nc.tensor.matmul(B[h][0:GLA_DK, :], w2[:, h * GLA_DK:(h + 1) * GLA_DK], gz[:],
                                 start=True, stop=True).then_inc(pe_done, 1)
            pe.wait_ge(dve_done, 5)
            for h in range(GLA_H):
                for t in range(TT):
                    mm = nc.tensor.transpose(B[4 + h][:, t * GLA_DK:(t + 1) * GLA_DK],
                                             kd[:, h, t * P:(t + 1) * P], ident[0:GLA_DK, 0:GLA_DK])
                mm.then_inc(pe_done, 1)
            for h in range(GLA_H):
                pe.wait_ge(dve_done, 9)
                for c in range(CH):
                    lo = C * (c % 2)
                    mm = nc.tensor.matmul(B[2 * h + c % 2][0:GLA_DK, (c // 2) * GLA_DV:(c // 2 + 1) * GLA_DV],
                                          kdT[lo:lo + C, h, c // 2, :],
                                          gv[lo:lo + C, c // 2, h * GLA_DV:(h + 1) * GLA_DV],
                                          start=True, stop=True)
                mm.then_inc(pe_done, 1)
            pe.wait_ge(chained, GLA_H * (CH - 1))
            for h in range(GLA_H):
                for t in range(TT):
                    cols = slice(t * P, (t + 1) * P)
                    mm = nc.tensor.matmul(B[h][:, cols], ke[:, h, cols], qe[:, h, cols], start=True, stop=True)
                mm.then_inc(pe_done, 1)
            for h in range(GLA_H):
                pe.wait_ge(dve_done, 10 + h)
                for c in range(CH):
                    cc = slice(c * C, (c + 1) * C)
                    nc.tensor.matmul(B[4 + h][0:GLA_DV, cc], gv[:, c // 2, h * GLA_DV:(h + 1) * GLA_DV],
                                     AT[:, h, cc], start=True, stop=False)
                    mm = nc.tensor.matmul(B[4 + h][0:GLA_DV, cc], S[:, h, c, :], qe[:, h, cc],
                                          start=False, stop=True)
                mm.then_inc(pe_done, 1)
            for h in range(GLA_H):
                pe.wait_ge(act_done, 11 + h)
                nc.tensor.matmul(B[h][0:GLA_DV, :], ones[0:GLA_DV, 0:GLA_DV], sq[:, h, :],
                                 start=True, stop=True).then_inc(pe_done, 1)

        @block.scalar
        def _(act):
            for h in range(GLA_H):
                act.wait_ge(loaded, 16 * 8)
                act.wait_ge(pe_done, h + 1)
                nc.scalar.activation(z[:, h, :], B[h][0:GLA_DK, :], ACT.Identity,
                                     bias=gb[:, h:h + 1]).then_inc(act_done, 1)
            act.wait_ge(act_done, 4)
            nc.scalar.activation(lsig[:], z[:], ACT.Abs).then_inc(act_done, 1)
            act.wait_ge(act_done, 5)
            nc.scalar.activation(lsig[:], lsig[:], ACT.Exp, scale=-1.0).then_inc(act_done, 1)
            act.wait_ge(act_done, 6)
            nc.scalar.activation(lsig[:], lsig[:], ACT.Ln, bias=1.0).then_inc(act_done, 1)
            act.wait_ge(dve_done, 2)
            nc.scalar.activation(e[:], b[:], ACT.Exp, scale=1 / 16).then_inc(act_done, 1)
            nc.scalar.activation(z[:], b[:], ACT.Exp, scale=-1 / 16).then_inc(act_done, 1)
            act.wait_ge(dve_done, 3)
            nc.scalar.activation(lsig[:], kd[:], ACT.Exp, scale=1 / 16).then_inc(act_done, 1)
            for h in range(GLA_H):
                act.wait_ge(pe_done, PE_A + 1 + h)
                nc.scalar.activation(sq[:, h, :], B[4 + h][0:GLA_DV, :], ACT.Square).then_inc(act_done, 1)
            act.wait_ge(zeroed, 2)
            for h in range(GLA_H):
                act.wait_ge(pe_done, PE_O + 1 + h)
                nc.scalar.activation(sq[:, h, :], B[h][0:GLA_DV, :], ACT.Sqrt, bias=eps_col[0:GLA_DV, :],
                                     scale=1.0 / GLA_DV).then_inc(act_done, 1)

        @block.vector
        def _(dve):
            dve.wait_ge(act_done, 7)
            nc.vector.scalar_tensor_tensor(out=lsig[:], in0=z[:], scalar=0.0, in1=lsig[:], op0=ALU.min,
                                           op1=ALU.subtract).then_inc(dve_done, 1)
            dve.wait_ge(dve_done, 1)
            dve.wait_ge(loaded, 16 * 8)
            flat = "p h t -> p (h t)"
            nc.vector.tensor_tensor_scan(b[:].rearrange(flat), reset[:].rearrange(flat),
                                         lsig[:].rearrange(flat), 0.0, ALU.mult, ALU.add).then_inc(dve_done, 1)
            dve.wait_ge(dve_done, 2)
            nc.vector.tensor_tensor(kd[:].rearrange("p h (c t) -> p (h c) t", t=C),
                                    bc[:, :, C - 1:C].to_broadcast([GLA_DK, GLA_H * CH, C]), bc,
                                    ALU.subtract).then_inc(dve_done, 1)
            dve.wait_ge(act_done, 9)
            nc.vector.scalar_tensor_tensor(out=qe[:], in0=gq[:], scalar=GLA_DK ** -0.5, in1=e[:],
                                           op0=ALU.mult, op1=ALU.mult)
            nc.vector.tensor_tensor(ke[:], gk[:], z[:], ALU.mult).then_inc(dve_done, 1)
            dve.wait_ge(act_done, 10)
            nc.vector.tensor_tensor(kd[:], gk[:], lsig[:], ALU.mult).then_inc(dve_done, 1)
            for h in range(GLA_H):
                dve.wait_ge(pe_done, PE_GATE + 1 + h)
                nc.vector.tensor_copy(kdT[:, h, :, :].rearrange("p t k -> p (t k)"),
                                      B[4 + h][:, 0:TT * GLA_DK]).then_inc(dve_done, 1)
            dve.wait_ge(zeroed, 1)
            for c in range(CH - 1):
                for h in range(GLA_H):
                    dve.wait_ge(pe_done, PE_TURN + 1 + h)
                    if c:
                        dve.wait_ge(chained, GLA_H * (c - 1) + h + 1)
                    at = (c // 2) * GLA_DV
                    nc.vector.scalar_tensor_tensor(
                        out=S[:, h, c + 1, :], in0=S[:, h, c, :], scalar=e[:, h, c * C + C - 1:c * C + C],
                        in1=B[2 * h + c % 2][0:GLA_DK, at:at + GLA_DV], op0=ALU.mult,
                        op1=ALU.add).then_inc(chained, 1)
            for h in range(GLA_H):
                dve.wait_ge(pe_done, PE_U + 1 + h)
                nc.vector.tensor_tensor(AT[:, h, :].rearrange("p (t q) -> p t q", q=P),
                                        B[h][:].rearrange("p (t q) -> p t q", q=P),
                                        mask[:].unsqueeze(1).to_broadcast([P, TT, P]),
                                        ALU.mult).then_inc(dve_done, 1)
            dve.wait_ge(act_done, 18)
            nc.vector.reciprocal(sq[:], sq[:]).then_inc(dve_done, 1)
            dve.wait_ge(dve_done, 14)
            for h in range(GLA_H):
                nc.vector.tensor_tensor(y[:, h, :], B[4 + h][0:GLA_DV, :], sq[:, h, :],
                                        ALU.mult).then_inc(dve_done, 1)
            dve.wait_ge(dve_done, 18)
            nc.vector.scalar_tensor_tensor(out=y[:], in0=y[:], scalar=ng[:], in1=gate[:], op0=ALU.mult,
                                           op1=ALU.mult).then_inc(dve_done, 1)


def dsa_select(core, to, ident, pick):
    nc = core.nc
    B = core.bank
    qi, ki, wi = to["qi"], to["ki"], to["wi"]
    with ExitStack() as ctx:
        hidden, rl, wh, score, top = bufs(nc, ctx, "sel", hidden=[P, P], rl=[P, 2, IDX_H, T],
                                          wh=[P, TT, IDX_H], score=[P, TT, T], top=[P, 8])
        loaded, dots, relued, weighed, step = sems(nc, ctx, "sel_loaded", "sel_dots", "sel_relued",
                                                   "sel_weighed", "sel_step")
        block = ctx.enter_context(nc.Block())

        @block.sync
        def _(sp):
            sp.dma_start(hidden[:], core.const("hidden")).then_inc(loaded, 16)

        @block.tensor
        def _(pe):
            for t in range(TT):
                n = P * (t + 1)
                for j in range(IDX_H):
                    if t >= 2:
                        pe.wait_ge(relued, IDX_H * (t - 2) + j + 1)
                    rows = slice(j * IDX_DIM, (j + 1) * IDX_DIM)
                    nc.tensor.matmul(B[(IDX_H * t + j) % 8][:, 0:n], qi[rows, t * P:(t + 1) * P],
                                     ki[rows, 0:n], start=True, stop=True).then_inc(dots, 1)

        @block.scalar
        def _(act):
            for t in range(TT):
                n = P * (t + 1)
                for j in range(IDX_H):
                    act.wait_ge(dots, IDX_H * t + j + 1)
                    if t >= 2:
                        act.wait_ge(weighed, t - 1)
                    nc.scalar.activation(rl[:, t % 2, j, 0:n], B[(IDX_H * t + j) % 8][:, 0:n], ACT.Relu,
                                         scale=IDX_DIM ** -0.5).then_inc(relued, 1)

        @block.vector
        def _(dve):
            steps = Count(step)

            def after(instruction):
                dve.wait_ge(step, steps.by(instruction))

            after(nc.vector.tensor_scalar(wh[:], wi[:], IDX_H ** -0.5, None, ALU.mult))
            dve.wait_ge(loaded, 16)
            for t in range(TT):
                n = P * (t + 1)
                dve.wait_ge(relued, IDX_H * (t + 1))
                s = score[:, t, 0:n]
                after(nc.vector.tensor_scalar(s, rl[:, t % 2, 0, 0:n], wh[:, t, 0:1], None, ALU.mult))
                for j in range(1, IDX_H):
                    last = nc.vector.scalar_tensor_tensor(out=s, in0=rl[:, t % 2, j, 0:n],
                                                          scalar=wh[:, t, j:j + 1], in1=s, op0=ALU.mult,
                                                          op1=ALU.add)
                    if j < IDX_H - 1:
                        after(last)
                last.then_inc(weighed, 1)
                dve.wait_ge(weighed, t + 1)
                diag = score[:, t, t * P:n]
                after(nc.vector.scalar_tensor_tensor(out=diag, in0=hidden[:], scalar=-NEG_HIDDEN, in1=diag,
                                                     op0=ALU.mult, op1=ALU.add))
                if t == 0:
                    nc.vector.tensor_copy(pick[:, 0, 0:P], hidden[:])
                    continue
                for _ in range(TOPK // 8):
                    after(nc.vector.max(top[:], s))
                    after(nc.vector.match_replace(s, top[:], s, NEG_TAKEN))
                after(nc.vector.tensor_scalar(pick[:, t, 0:n], s, NEG_TAKEN, 1.0, ALU.is_equal, ALU.subtract))


def dsa_attend(core, to, ident, rel_bias, bias_dram, pick, y):
    nc = core.nc
    B = core.bank
    dq, dk, dv, gate = (to[n] for n in ("dq", "dk", "dv", "dgate"))
    units = [(t, h) for t in range(TT) for h in range(DSA_H)]
    N = len(units)
    U = 5 * P
    with ExitStack() as ctx:
        rb, onehot, by_distance, bias, L, pr, prT, peak, total, flip = bufs(
            nc, ctx, "att", rb=[BUCKETS, DSA_H], onehot=[BUCKETS, U], by_distance=[DSA_H, U],
            bias=[P, DSA_H, T], L=[P, 2, T], pr=[P, 2, T], prT=[P, 2, T], peak=[P, 2], total=[P, 2], flip=[P, P])
        (loaded, table, table_copied, stored, windows, logits, peaked, exped, weights, turned, turned_copied,
         attended, step, gated, flipped, flip_copied) = sems(
            nc, ctx, *(f"att_{s}" for s in ("loaded", "table", "table_copied", "stored", "windows", "logits",
                                            "peaked", "exped", "weights", "turned", "turned_copied",
                                            "attended", "step", "gated", "flipped",
                                            "flip_copied")))
        block = ctx.enter_context(nc.Block())

        @block.sync
        def _(sp):
            sp.dma_start(rb[:], rel_bias).then_inc(loaded, 16)
            sp.dma_start(onehot[:], core.const("bucket", BUCKETS)).then_inc(loaded, 16)
            sp.wait_ge(table_copied, 2)
            sp.dma_start(bias_dram, by_distance[:]).then_inc(stored, 16)
            sp.wait_ge(stored, 16)
            for h in range(DSA_H):
                window = bass.AP(tensor=bias_dram.tensor, offset=h * U, ap=[[1, P], [1, T]])
                sp.dma_start(bias[:, h, :], window).then_inc(windows, 16)
            sp.dma_start(flip[:], core.const("flip")).then_inc(windows, 16)

        @block.tensor
        def _(pe):
            pe.wait_ge(loaded, 32)
            nc.tensor.matmul(B[6][0:DSA_H, :], rb[:], onehot[:, 0:512], start=True, stop=True).then_inc(table, 1)
            nc.tensor.matmul(B[7][0:DSA_H, 0:U - 512], rb[:], onehot[:, 512:U], start=True,
                             stop=True).then_inc(table, 1)
            pe.wait_ge(windows, 16 * (DSA_H + 1))
            pe.wait_ge(table_copied, 2)
            for h in range(DSA_H):
                nc.tensor.matmul(B[2 + h][:], flip[:], bias[:, h, :], start=True, stop=True).then_inc(flipped, 1)
            pe.wait_ge(flip_copied, DSA_H)
            for i in range(N + 1):
                if i < N:
                    t, h = units[i]
                    n = P * (t + 1)
                    rows = slice(DSA_DH * (h % 2), DSA_DH * (h % 2) + DSA_DH)
                    if i >= 2:
                        pe.wait_ge(peaked, i - 1)
                    nc.tensor.matmul(B[i % 2][:, 0:n], dq[rows, h // 2, t * P:(t + 1) * P],
                                     dk[rows, h // 2, 0:n], start=True, stop=True).then_inc(logits, 1)
                if i >= 1:
                    j = i - 1
                    t, h = units[j]
                    pe.wait_ge(weights, j + 1)
                    if j >= 2:
                        pe.wait_ge(turned_copied, j - 1)
                    for s in range(t + 1):
                        mm = nc.tensor.transpose(B[2 + j % 2][:, s * P:(s + 1) * P],
                                                 pr[:, j % 2, s * P:(s + 1) * P], ident[:])
                    mm.then_inc(turned, 1)
                    pe.wait_ge(turned_copied, j + 1)
                    rows = slice(DSA_DH * (h % 2), DSA_DH * (h % 2) + DSA_DH)
                    for s in range(t + 1):
                        mm = nc.tensor.matmul(B[4 + h // 2][rows, t * P:(t + 1) * P],
                                              dv[:, s, h * DSA_DH:(h + 1) * DSA_DH],
                                              prT[:, j % 2, s * P:(s + 1) * P], start=(s == 0), stop=(s == t),
                                              skip_group_check=True)
                    mm.then_inc(attended, 1)

        @block.vector
        def _(dve):
            steps = Count(step)

            def after(instruction):
                dve.wait_ge(step, steps.by(instruction))

            for i in range(2):
                dve.wait_ge(table, i + 1)
                cols = slice(0, 512) if i == 0 else slice(512, U)
                nc.vector.tensor_copy(by_distance[:, cols],
                                      B[6 + i][0:DSA_H, 0:cols.stop - cols.start]).then_inc(table_copied, 1)
            for h in range(DSA_H):
                dve.wait_ge(flipped, h + 1)
                nc.vector.tensor_copy(bias[:, h, :], B[2 + h][:]).then_inc(flip_copied, 1)
            dve.wait_ge(flip_copied, DSA_H)
            for i in range(N + 1):
                if i < N:
                    t, h = units[i]
                    n = P * (t + 1)
                    x = L[:, i % 2, 0:n]
                    dve.wait_ge(logits, i + 1)
                    if i >= 2:
                        dve.wait_ge(exped, i - 1)
                    after(nc.vector.scalar_tensor_tensor(out=x, in0=B[i % 2][:, 0:n], scalar=DSA_DH ** -0.5,
                                                         in1=bias[:, h, T - n:T], op0=ALU.mult, op1=ALU.add))
                    after(nc.vector.scalar_tensor_tensor(out=x, in0=pick[:, t, 0:n], scalar=1e30, in1=x,
                                                         op0=ALU.mult, op1=ALU.add))
                    after(nc.vector.reduce_max(peak[:, i % 2:i % 2 + 1], x, AX))
                    nc.vector.tensor_scalar(peak[:, i % 2:i % 2 + 1], peak[:, i % 2:i % 2 + 1], -1.0, None,
                                            ALU.mult).then_inc(peaked, 1)
                if i >= 1:
                    j = i - 1
                    n = P * (units[j][0] + 1)
                    dve.wait_ge(exped, j + 1)
                    after(nc.vector.reciprocal(total[:, j % 2:j % 2 + 1], total[:, j % 2:j % 2 + 1]))
                    nc.vector.tensor_scalar(pr[:, j % 2, 0:n], pr[:, j % 2, 0:n], total[:, j % 2:j % 2 + 1],
                                            None, ALU.mult).then_inc(weights, 1)
            for k in range(3):
                dve.wait_ge(attended, N)
                nc.vector.tensor_tensor(y[:, k, :], B[4 + k][:], gate[:, k, :], ALU.mult).then_inc(gated, 1)

        @block.scalar
        def _(act):
            for i in range(N + 1):
                if i < N:
                    n = P * (units[i][0] + 1)
                    act.wait_ge(peaked, i + 1)
                    if i >= 2:
                        act.wait_ge(turned, i - 1)
                    nc.scalar.activation(pr[:, i % 2, 0:n], L[:, i % 2, 0:n], ACT.Exp, bias=peak[:, i % 2:i % 2 + 1],
                                         accum_out=total[:, i % 2:i % 2 + 1]).then_inc(exped, 1)
                if i >= 1:
                    j = i - 1
                    n = P * (units[j][0] + 1)
                    act.wait_ge(turned, j + 1)
                    if j >= 2:
                        act.wait_ge(attended, j - 1)
                    nc.scalar.copy(prT[:, j % 2, 0:n], B[2 + j % 2][:, 0:n]).then_inc(turned_copied, 1)


def pool_mix(core, to, pool_w, pool_scale, y):
    nc = core.nc
    B = core.bank
    pu, gate = to["pu"], to["pgate"]
    PAD = max(WINDOWS)
    with ExitStack() as ctx:
        inv, w, sc, a, b = bufs(nc, ctx, "pool", inv=[P, 2, T], w=[P, 2, 64], sc=[P, 2], a=[P, 2, PAD + T],
                                b=[P, 2, PAD + T])
        loaded, step, pooled, mixed, scaled = sems(nc, ctx, "pool_loaded", "pool_step", "pool_pooled",
                                                   "pool_mixed", "pool_scaled")
        block = ctx.enter_context(nc.Block())

        @block.sync
        def _(sp):
            sp.dma_start(inv[:].rearrange("p k t -> p (k t)"), core.const("inv_count")).then_inc(loaded, 16)
            sp.dma_start(w[:], pool_w.rearrange("(k g) c d -> (g c) k d", g=2)).then_inc(loaded, 16)
            with nc.allow_non_contiguous_dma("two columns"):
                sp.dma_start(sc[:], columns(pool_scale)).then_inc(loaded, 16)

        @block.vector
        def _(dve):
            steps = Count(step)

            def after(instruction):
                dve.wait_ge(step, steps.by(instruction))

            nc.vector.memset(b[:, :, 0:PAD], 0.0)
            nc.vector.memset(a[:, :, 0:PAD], 0.0)
            after(nc.vector.tensor_copy(a[:, :, PAD:], pu[:]))
            src, dst = a, b
            for k, window in enumerate(WINDOWS):
                tile, row = k // 2, 64 * (k % 2)
                half = window // 2
                after(nc.vector.tensor_tensor(dst[:, :, PAD:], src[:, :, PAD:],
                                              src[:, :, PAD - half:PAD + T - half], ALU.add))
                after(nc.vector.tensor_copy(y[row:row + 64, tile, :], dst[row:row + 64, tile, PAD:]))
                src, dst = dst, src
            dve.wait_ge(loaded, 48)
            after(nc.vector.tensor_tensor(y[:], y[:], inv[:], ALU.mult))
            nc.vector.tensor_tensor(y[:], y[:], pu[:], ALU.subtract).then_inc(pooled, 1)
            for tile in range(2):
                dve.wait_ge(mixed, 4)
                nc.vector.scalar_tensor_tensor(out=y[:, tile, :], in0=B[tile][:], scalar=sc[:, tile:tile + 1],
                                               in1=gate[:, tile, :], op0=ALU.mult,
                                               op1=ALU.mult).then_inc(scaled, 1)

        @block.tensor
        def _(pe):
            pe.wait_ge(loaded, 48)
            pe.wait_ge(pooled, 1)
            for g in range(4):
                rows = slice(64 * (g % 2), 64 * (g % 2) + 64)
                nc.tensor.matmul(B[g // 2][rows, :], w[rows, g // 2, :], y[rows, g // 2, :], start=True,
                                 stop=True, skip_group_check=True).then_inc(mixed, 1)


def mix_out(core, xT, y_gla, y_dsa, y_pool, w_out):
    nc = core.nc
    B = core.bank
    parts = [(y_gla, h, GLA_DV) for h in range(4)] + [(y_dsa, k, P) for k in range(3)] + [(y_pool, k, P) for k in range(2)]
    with ExitStack() as ctx:
        wg, wd = bufs(nc, ctx, "mo", wg=[GLA_DV, 4, D], wd=[P, 5, D])
        loaded, product, added = sems(nc, ctx, "mo_loaded", "mo_product", "mo_added")
        block = ctx.enter_context(nc.Block())

        @block.sync
        def _(sp):
            sp.dma_start(wg[:], w_out[0:384].rearrange("(k p) n -> p k n", p=GLA_DV)).then_inc(loaded, 16)
            sp.dma_start(wd[:], w_out[384:D].rearrange("(k p) n -> p k n", p=P)).then_inc(loaded, 16)

        @block.tensor
        def _(pe):
            pe.wait_ge(loaded, 32)
            for m in range(KT):
                for i, (y, k, rows) in enumerate(parts):
                    w = wg[:, i, m * P:(m + 1) * P] if i < 4 else wd[:, i - 4, m * P:(m + 1) * P]
                    mm = nc.tensor.matmul(B[m][:], w, y[0:rows, k, :], start=(i == 0), stop=(i == len(parts) - 1))
                mm.then_inc(product, 1)

        @block.vector
        def _(dve):
            for m in range(KT):
                dve.wait_ge(product, m + 1)
                nc.vector.tensor_tensor(xT[:, m, :], xT[:, m, :], B[m][:], ALU.add).then_inc(added, 1)


def load_columns(core, pairs):
    nc = core.nc
    with ExitStack() as ctx:
        (loaded,) = sems(nc, ctx, f"columns_loaded{core.stage_n}")
        core.stage_n += 1
        block = ctx.enter_context(nc.Block())

        @block.sync
        def _(sp):
            with nc.allow_non_contiguous_dma("columns"):
                for dst, vector in pairs:
                    sp.dma_start(dst, columns(vector)).then_inc(loaded, 16)
            sp.wait_ge(loaded, 16 * len(pairs))


def first_block(core, a, xT, hT, ident, ones):
    nc = core.nc
    with ExitStack() as ctx:
        ng, fg, y_gla, y_dsa, y_pool = bufs(
            nc, ctx, "b1", ng=[P, KT], fg=[P, KT], y_gla=[GLA_DV, GLA_H, T], y_dsa=[P, 3, T], y_pool=[P, 2, T])
        load_columns(core, [(ng[:], a["norm_g"][0]), (fg[:], a["final_norm_g"])])
        with ExitStack() as inner:
            names = dict(gq=[GLA_DK, GLA_H, T], gk=[GLA_DK, GLA_H, T], gz=[GLA_RANK, T], ggate=[GLA_DV, GLA_H, T],
                         dq=[P, 3, T], dk=[P, 3, T], dgate=[P, 3, T], qi=[P, T], ki=[P, T], pu=[P, 2, T],
                         pgate=[P, 2, T], gv=[P, TT, 384], dv=[P, TT, 384], wi=[P, TT, IDX_H])
            to = dict(zip(names, bufs(nc, inner, "b1", **names)))
            with ExitStack() as s:
                (scratch,) = bufs(nc, s, "b1n", scratch=[P, KT, T])
                norm(core, "n1", xT, hT, ones, scratch, ng)
            projection(core, hT, a["w_in"][0], to)
            gla(core, to, ones, ident, a["gla_gate_w2"][0], a["gla_gate_b"][0], a["gla_norm_g"][0], y_gla)
            with ExitStack() as s:
                (pick,) = bufs(nc, s, "b1s", pick=[P, TT, T])
                dsa_select(core, to, ident, pick)
                dsa_attend(core, to, ident, a["rel_bias"], a["bias_dram"], pick, y_dsa)
            pool_mix(core, to, a["pool_w"][0], a["pool_scale"][0], y_pool)
        mix_out(core, xT, y_gla, y_dsa, y_pool, a["w_out"][0])
        with ExitStack() as s:
            (scratch,) = bufs(nc, s, "b1f", scratch=[P, KT, T])
            norm(core, "n2", xT, xT, ones, scratch, fg)



CONV_W, SGU_G = 31, 8
ALPHA = 2.0 ** 0.25
N_EXPERTS, TOP_K, D_EXPERT = 32, 4, 1024
SWIGLU_LIMIT, SWIGLU_ALPHA = 7.0, 1.702
EXTRA = T * TOP_K // P
N_TABLE = N_EXPERTS + EXTRA + 1
HALF = 512


def linear(core, name, w, passes, src, evict, stacked=False, more=None):
    nc = core.nc
    B = core.bank
    w_v = w.rearrange("(k p) n -> p k n", p=P)
    engine_name, emit = evict
    with ExitStack() as ctx:
        (wt,) = bufs(nc, ctx, name, w=[P, 2, KT, HALF])
        loaded = sems(nc, ctx, f"{name}_loaded0", f"{name}_loaded1")
        product, copied = sems(nc, ctx, f"{name}_product", f"{name}_copied")
        block = ctx.enter_context(nc.Block())

        def piece(i, s):
            if stacked:
                return w_v[:, bass.ds(i * KT, KT), s * HALF:(s + 1) * HALF]
            return w_v[:, :, bass.ds(i * D + s * HALF, HALF)]

        @block.sync
        def _(sp):
            for s in range(2):
                sp.dma_start(wt[:, s], piece(0, s)).then_inc(loaded[s], 16)
            if passes > 1:
                with sp.Fori(1, passes) as i:
                    for s in range(2):
                        sp.wait_ge(product, 8 * i - 4 + 4 * s)
                        sp.dma_start(wt[:, s], piece(i, s)).then_inc(loaded[s], 16)

        def products(pe, i, first):
            for s in range(2):
                pe.wait_ge(loaded[s], 16 * i + 16)
                for m in range(4):
                    b = 4 * s + m
                    if not first:
                        pe.wait_ge(copied, 8 * i - 7 + b)
                    for k in range(KT):
                        right = src[:, k, :]
                        if stacked and not first:
                            right = src[:, bass.ds(i * KT + k, 1), :].rearrange("p a t -> p (a t)")
                        mm = nc.tensor.matmul(B[b][:], wt[:, s, k, m * P:(m + 1) * P], right,
                                              start=(k == 0), stop=(k == KT - 1))
                    mm.then_inc(product, 1)

        @block.tensor
        def _(pe):
            products(pe, 0, True)
            if passes > 1:
                with pe.Fori(1, passes) as i:
                    products(pe, i, False)

        def evictions(eng):
            for i in range(passes):
                for b in range(8):
                    eng.wait_ge(product, 8 * i + b + 1)
                    emit(i, b, B[b]).then_inc(copied, 1)

        if engine_name == "scalar":
            @block.scalar
            def _(act):
                evictions(act)
        else:
            @block.vector
            def _(dve):
                evictions(dve)

        if more is not None:
            more(block, copied)


def modulation(core, name, w, cond, bias, out, plus_one):
    nc = core.nc
    B = core.bank
    passes = 6
    w_v = w.rearrange("(k p) n -> p k n", p=P)
    with ExitStack() as ctx:
        (wt,) = bufs(nc, ctx, name, w=[P, 4, KT, HALF])
        loaded = sems(nc, ctx, *(f"{name}_loaded{s}" for s in range(4)))
        product, copied, activated, step = sems(nc, ctx, f"{name}_product", f"{name}_copied",
                                                f"{name}_activated", f"{name}_plus_one")
        block = ctx.enter_context(nc.Block())
        N = 2 * passes

        @block.sync
        def _(sp):
            for c in range(N):
                if c >= 4:
                    sp.wait_ge(product, c - 3)
                sp.dma_start(wt[:, c % 4], w_v[:, :, c * HALF:(c + 1) * HALF]).then_inc(loaded[c % 4], 16)

        @block.scalar
        def _(act):
            nc.scalar.activation(cond[:], cond[:], ACT.Silu).then_inc(activated, 1)

        @block.tensor
        def _(pe):
            pe.wait_ge(activated, 1)
            for c in range(N):
                pe.wait_ge(loaded[c % 4], 16 * (c // 4 + 1))
                if c >= 2:
                    pe.wait_ge(copied, c - 1)
                for m in range(4):
                    for k in range(KT):
                        mm = nc.tensor.matmul(B[c % 2][:, m:m + 1], wt[:, c % 4, k, m * P:(m + 1) * P],
                                              cond[:, k:k + 1], start=(k == 0), stop=(k == KT - 1))
                mm.then_inc(product, 1)

        @block.vector
        def _(dve):
            for c in range(N):
                dve.wait_ge(product, c + 1)
                cols = slice(4 * c, 4 * c + 4)
                nc.vector.tensor_tensor(out[:, cols], B[c % 2][:, 0:4], bias[:, cols], ALU.add).then_inc(copied, 1)
            dve.wait_ge(copied, N)
            for lo in plus_one:
                nc.vector.tensor_scalar(out[:, lo:lo + KT], out[:, lo:lo + KT], 1.0, None,
                                        ALU.add).then_inc(step, 1)


def mixer_in(core, hT, w_in, b_in, conv_w, conv_b, z, conv):
    nc = core.nc
    funcs = (ACT.Identity, ACT.Sigmoid, ACT.Gelu, ACT.Gelu, ACT.Sigmoid, ACT.Sigmoid)
    PAD = CONV_W - 1
    with ExitStack() as ctx:
        (ya,) = bufs(nc, ctx, "conv", ya=[P, KT, PAD + T])
        gated, tap = sems(nc, ctx, "conv_gated", "conv_tap")

        def emit(i, b, bank):
            return nc.scalar.activation(z[:, 8 * i + b, :], bank[:], funcs[i], bias=b_in[:, 8 * i + b:8 * i + b + 1])

        def convolve(block, copied):
            @block.vector
            def _(dve):
                nc.vector.memset(ya[:, :, 0:PAD], 0.0)
                for k in range(KT):
                    dve.wait_ge(copied, 9 + k)
                    nc.vector.tensor_tensor(ya[:, k, PAD:], z[:, k, :], z[:, 8 + k, :], ALU.mult).then_inc(gated, 1)
                dve.wait_ge(gated, KT)
                for k in range(KT):
                    nc.vector.tensor_scalar(conv[:, k, :], ya[:, k, 0:T], conv_w[:, k, 0:1], conv_b[:, k:k + 1],
                                            ALU.mult, ALU.add).then_inc(tap, 1)
                with dve.Fori(1, CONV_W) as j:
                    for k in range(KT):
                        dve.wait_ge(tap, KT * j - KT + k + 1)
                        nc.vector.scalar_tensor_tensor(
                            out=conv[:, k, :], in0=ya[:, k, bass.ds(j, T)], scalar=conv_w[:, k, bass.ds(j, 1)],
                            in1=conv[:, k, :], op0=ALU.mult, op1=ALU.add).then_inc(tap, 1)

        linear(core, "min", w_in, 6, hT, ("scalar", emit), more=convolve)


def spatial_gating(core, u, v, w_s, b_s, ident):
    nc = core.nc
    B = core.bank
    with ExitStack() as ctx:
        ws, wsT, mask, bs, vT, mixed = bufs(nc, ctx, "sgu", ws=[P, SGU_G, P], wsT=[P, SGU_G, P], mask=[P, P],
                                            bs=[P, SGU_G, P], vT=[P, TT, D], mixed=[P, 2, T])
        loaded, w_turned, w_masked, v_turned, v_copied, product, biased, gated = sems(
            nc, ctx, *(f"sgu_{s}" for s in ("loaded", "w_turned", "w_masked", "v_turned", "v_copied", "product",
                                            "biased", "gated")))
        block = ctx.enter_context(nc.Block())

        @block.sync
        def _(sp):
            sp.dma_start(ws[:], w_s.rearrange("g i j -> i g j")).then_inc(loaded, 16)
            sp.dma_start(mask[:], core.const("sgu_mask")).then_inc(loaded, 16)
            sp.dma_start(bs[:].rearrange("p g i -> p (g i)"),
                         bcast_rows(b_s.rearrange("(a g) i -> a (g i)", a=1))).then_inc(loaded, 16)

        @block.tensor
        def _(pe):
            pe.wait_ge(loaded, 48)
            for g in range(SGU_G):
                mm = nc.tensor.transpose(B[g // 4][:, (g % 4) * P:(g % 4 + 1) * P], ws[:, g, :], ident[:])
                mm.then_inc(w_turned, 1)
            for n in range(8):
                t, half = n // 2, n % 2
                if n >= 6:
                    pe.wait_ge(w_masked, 4 * (n - 5))
                for q in range(4):
                    k = 4 * half + q
                    mm = nc.tensor.transpose(B[(2 + n) % 8][:, q * P:(q + 1) * P], v[:, k, t * P:(t + 1) * P],
                                             ident[:])
                mm.then_inc(v_turned, 1)
            for g in range(SGU_G):
                pe.wait_ge(w_masked, SGU_G)
                pe.wait_ge(v_copied, 8)
                if g >= 2:
                    pe.wait_ge(biased, g - 1)
                for t in range(TT):
                    mm = nc.tensor.matmul(B[g % 2][:, t * P:(t + 1) * P], vT[:, t, g * P:(g + 1) * P],
                                          wsT[:, g, :], start=True, stop=True)
                mm.then_inc(product, 1)

        @block.scalar
        def _(act):
            for n in range(8):
                act.wait_ge(v_turned, n + 1)
                nc.scalar.copy(vT[:, n // 2, (n % 2) * 512:(n % 2 + 1) * 512], B[(2 + n) % 8][:]).then_inc(v_copied, 1)

        @block.vector
        def _(dve):
            dve.wait_ge(loaded, 48)
            for g in range(SGU_G):
                dve.wait_ge(w_turned, 4 * (g // 4 + 1))
                nc.vector.tensor_tensor(wsT[:, g, :], B[g // 4][:, (g % 4) * P:(g % 4 + 1) * P], mask[:],
                                        ALU.mult).then_inc(w_masked, 1)
            for g in range(SGU_G):
                dve.wait_ge(product, g + 1)
                nc.vector.tensor_tensor(mixed[:, g % 2, :].rearrange("p (t i) -> p t i", i=P),
                                        B[g % 2][:].rearrange("p (t i) -> p t i", i=P),
                                        bs[:, g, :].unsqueeze(1).to_broadcast([P, TT, P]), ALU.add).then_inc(biased, 1)
                dve.wait_ge(biased, g + 1)
                nc.vector.tensor_tensor(u[:, g, :], u[:, g, :], mixed[:, g % 2, :], ALU.mult).then_inc(gated, 1)


def second_mixer(core, a, xT, hT, ident, ones, mod, c):
    nc = core.nc
    with ExitStack() as ctx:
        (z,) = bufs(nc, ctx, "b2", z=[P, 48, T])
        tile = lambda i: z[:, 8 * i:8 * i + 8, :]
        norm(core, "n3", xT, hT, ones, tile(0), mod[:, 8:16], mod[:, 0:8], centre=True, eps=LN_EPS)
        with ExitStack() as s:
            (conv,) = bufs(nc, s, "b2", conv=[P, KT, T])
            mixer_in(core, hT, a["w_in_2"][0], c["b_in"], c["conv_w"], c["conv_b"], z, conv)
            norm(core, "n4", conv, hT, ones, tile(0), c["ln_a_g"], c["ln_a_b"], centre=True, func=ACT.Silu,
                 eps=LN_EPS)

        def gated_product(gate, bias, add_to=None):
            def emit(i, b, bank):
                return nc.vector.scalar_tensor_tensor(out=tile(gate)[:, b, :], in0=bank[:], scalar=bias[:, b:b + 1],
                                                      in1=tile(gate)[:, b, :], op0=ALU.add, op1=ALU.mult)
            return ("vector", emit)

        linear(core, "wa", a["w_a_2"][0], 1, hT, gated_product(4, c["b_a"]))
        norm(core, "n5", tile(3), tile(3), ones, tile(0), c["ln_v_g"], c["ln_v_b"], centre=True, eps=LN_EPS)
        spatial_gating(core, tile(2), tile(3), a["w_s_2"][0], a["b_s_2"][0], ident)
        linear(core, "wb", a["w_b_2"][0], 1, tile(2), gated_product(5, c["b_b"]))
        add_tiles(core, "m", tile(4), tile(5))

        def emit(i, b, bank):
            return nc.vector.tensor_scalar(tile(0)[:, b, :], bank[:], c["b_out"][:, b:b + 1], mod[:, 16 + b:17 + b],
                                           ALU.add, ALU.mult)

        linear(core, "wo", a["w_out_2"][0], 1, tile(4), ("vector", emit))
        add_tiles(core, "r", xT, tile(0), ALPHA)
        norm(core, "n6", xT, xT, ones, tile(0), c["post1_g"], c["post1_b"], centre=True, eps=LN_EPS)
        norm(core, "n7", xT, hT, ones, tile(0), mod[:, 32:40], mod[:, 24:32], centre=True, eps=LN_EPS)


def add_tiles(core, name, x, y, scale=1.0):
    nc = core.nc
    with ExitStack() as ctx:
        (added,) = sems(nc, ctx, f"add_{name}")
        block = ctx.enter_context(nc.Block())

        @block.vector
        def _(dve):
            for k in range(KT):
                nc.vector.scalar_tensor_tensor(out=x[:, k, :], in0=x[:, k, :], scalar=scale, in1=y[:, k, :],
                                               op0=ALU.mult, op1=ALU.add).then_inc(added, 1)


def second_columns(core, ctx, a):
    nc = core.nc
    shapes = dict(b_mod=48, b_in=48, conv_b=8, ln_a_g=8, ln_a_b=8, b_a=8, ln_v_g=8, ln_v_b=8, b_b=8, b_out=8,
                  post1_g=8, post1_b=8, post2_g=8, post2_b=8)
    c = dict(zip(shapes, bufs(nc, ctx, "c2", **{n: [P, w] for n, w in shapes.items()})))
    conv_w, cond = bufs(nc, ctx, "c2", conv_w=[P, KT, CONV_W], cond=[P, KT])
    load_columns(core, [(c[n][:], a[f"{n}_2"][0]) for n in shapes]
                 + [(conv_w[:, :, j], a["conv_w_2"][0, j]) for j in range(CONV_W)] + [(cond[:], a["c_2"][0])])
    c["conv_w"], c["cond"] = conv_w, cond
    return c


def second_block(core, a, xT, hT, ident, ones):
    nc = core.nc
    with ExitStack() as ctx:
        c = second_columns(core, ctx, a)
        (mod,) = bufs(nc, ctx, "b2", mod=[P, 48])
        modulation(core, "mod2", a["w_mod_2"][0], c["cond"], c["b_mod"], mod, (8, 32))
        second_mixer(core, a, xT, hT, ident, ones, mod, c)
        experts(core, a, xT, hT, ident, ones, mod, c)


def route(core, hT, ident, ones, w_router, b_router, htm, place, share, block_expert, n_blocks):
    nc = core.nc
    B = core.bank
    NE = N_EXPERTS
    SH = [P, TT, NE]
    XH = [P, EXTRA, NE]
    with ExitStack() as ctx:
        (wr, br, slots, numbers, upto, lg, top, gt, eq, rank, need, ex, tot, pos, extra, upto_e, before, member,
         member2, offset, q, ids, nb) = bufs(
            nc, ctx, "route", wr=[P, KT, NE], br=[P, NE], slots=[P, P], numbers=XH, upto=[P, P], lg=SH,
            top=[P, TT, 8], gt=SH, eq=SH, rank=SH, need=[P, TT, 1], ex=SH, tot=[P, TT, 1], pos=SH, extra=[P, NE],
            upto_e=[P, NE], before=[P, NE], member=XH, member2=XH, offset=XH, q=XH, ids=[P, N_TABLE], nb=[P, 1])
        loaded, logits, turned, copied, step, shifted, exped, chosen, counted = sems(
            nc, ctx, *(f"route_{s}" for s in ("loaded", "logits", "turned", "copied", "step", "shifted", "exped",
                                              "chosen", "counted")))
        block = ctx.enter_context(nc.Block())

        @block.sync
        def _(sp):
            sp.dma_start(wr[:], w_router.rearrange("(k p) e -> p k e", p=P)).then_inc(loaded, 16)
            sp.dma_start(br[:], bcast_rows(b_router)).then_inc(loaded, 16)
            sp.dma_start(slots[:], core.const("slots")).then_inc(loaded, 16)
            sp.dma_start(numbers[:].rearrange("p b e -> p (b e)"), core.const("numbers")).then_inc(loaded, 16)
            sp.dma_start(upto[:], core.const("upto")).then_inc(loaded, 16)

        @block.tensor
        def _(pe):
            pe.wait_ge(loaded, 80)
            for t in range(TT):
                for k in range(KT):
                    mm = nc.tensor.matmul(B[0][:, t * NE:(t + 1) * NE], hT[:, k, t * P:(t + 1) * P], wr[:, k, :],
                                          start=(k == 0), stop=(k == KT - 1))
            mm.then_inc(logits, 1)
            for n in range(8):
                if n >= 6:
                    pe.wait_ge(copied, n - 5)
                for j in range(4):
                    k = 4 * (n % 2) + j
                    mm = nc.tensor.transpose(B[2 + n % 6][:, j * P:(j + 1) * P],
                                             hT[:, k, (n // 2) * P:(n // 2 + 1) * P], ident[:])
                mm.then_inc(turned, 1)
            pe.wait_ge(chosen, 1)
            for t in range(TT):
                for s in range(t + 1):
                    nc.tensor.matmul(B[1][:, t * NE:(t + 1) * NE], upto[:] if s == t else ones[:], gt[:, s, :],
                                     start=(s == 0), stop=(s == t))
            for s in range(TT):
                mm = nc.tensor.matmul(B[1][:, TT * NE:(TT + 1) * NE], ones[:], gt[:, s, :], start=(s == 0),
                                      stop=(s == TT - 1))
            mm.then_inc(counted, 1)

        @block.scalar
        def _(act):
            for n in range(8):
                act.wait_ge(turned, n + 1)
                nc.scalar.copy(htm[:, n // 2, (n % 2) * 512:(n % 2 + 1) * 512], B[2 + n % 6][:]).then_inc(copied, 1)
            act.wait_ge(shifted, 1)
            nc.scalar.activation(ex[:], lg[:], ACT.Exp).then_inc(exped, 1)

        @block.vector
        def _(dve):
            steps = Count(step)

            def after(instruction):
                dve.wait_ge(step, steps.by(instruction))

            tt, wide = nc.vector.tensor_tensor, lambda ap, shape: ap.to_broadcast(shape)
            over_b = lambda ap: ap[:].unsqueeze(1).to_broadcast(XH)
            dve.wait_ge(loaded, 80)
            dve.wait_ge(logits, 1)
            after(tt(lg[:], B[0][:, 0:TT * NE].rearrange("p (t e) -> p t e", e=NE),
                     br[:].unsqueeze(1).to_broadcast(SH), ALU.add))
            for t in range(TT):
                after(nc.vector.max(top[:, t, :], lg[:, t, :]))
            least = wide(top[:, :, TOP_K - 1:TOP_K], SH)
            after(tt(gt[:], lg[:], least, ALU.is_gt))
            after(tt(eq[:], lg[:], least, ALU.is_equal))
            after(nc.vector.reduce_sum(need[:], gt[:], AX))
            after(nc.vector.tensor_scalar(need[:], need[:], -1.0, float(TOP_K), ALU.mult, ALU.add))
            for t in range(TT):
                after(nc.vector.tensor_tensor_scan(rank[:, t, :], ones[:, 0:NE], eq[:, t, :], 0.0, ALU.mult, ALU.add))
            after(tt(rank[:], rank[:], wide(need[:], SH), ALU.is_le))
            after(tt(eq[:], eq[:], rank[:], ALU.mult))
            nc.vector.tensor_tensor(gt[:], gt[:], eq[:], ALU.add).then_inc(chosen, 1)
            tt(lg[:], lg[:], wide(top[:, :, 0:1], SH), ALU.subtract).then_inc(shifted, 1)
            dve.wait_ge(exped, 1)
            dve.wait_ge(chosen, 1)
            after(tt(ex[:], ex[:], gt[:], ALU.mult))
            after(nc.vector.reduce_sum(tot[:], ex[:], AX))
            after(nc.vector.reciprocal(tot[:], tot[:]))
            after(tt(share[:, :, 0:NE], ex[:], wide(tot[:], SH), ALU.mult))
            dve.wait_ge(counted, 1)
            after(tt(pos[:], B[1][:, 0:TT * NE].rearrange("p (t e) -> p t e", e=NE), gt[:], ALU.mult))
            after(nc.vector.tensor_scalar(pos[:], pos[:], 1.0, None, ALU.subtract))
            after(nc.vector.tensor_copy(place[:, :, 0:NE], pos[:]))
            n = B[1][:, TT * NE:(TT + 1) * NE]
            after(nc.vector.tensor_scalar(extra[:], n, float(P), None, ALU.is_gt))
            for more in (2 * P, 3 * P):
                after(nc.vector.scalar_tensor_tensor(out=extra[:], in0=n, scalar=float(more), in1=extra[:],
                                                     op0=ALU.is_gt, op1=ALU.add))
            after(nc.vector.tensor_tensor_scan(upto_e[:], ones[:, 0:NE], extra[:], 0.0, ALU.mult, ALU.add))
            after(tt(before[:], upto_e[:], extra[:], ALU.subtract))
            after(tt(member[:], numbers[:], over_b(before), ALU.is_ge))
            after(tt(member2[:], numbers[:], over_b(upto_e), ALU.is_lt))
            after(tt(member[:], member[:], member2[:], ALU.mult))
            after(tt(offset[:], numbers[:], over_b(before), ALU.subtract))
            after(nc.vector.tensor_scalar(offset[:], offset[:], 1.0, float(P), ALU.add, ALU.mult))
            for t in range(TT):
                after(tt(q[:], pos[:, t:t + 1, :].to_broadcast(XH), offset[:], ALU.subtract))
                after(tt(q[:], q[:], member[:], ALU.mult))
                after(nc.vector.reduce_sum(place[:, t, NE:NE + EXTRA], q[:], AX))
                after(tt(q[:], member[:], share[:, t, 0:NE].unsqueeze(1).to_broadcast(XH), ALU.mult))
                after(nc.vector.reduce_sum(share[:, t, NE:NE + EXTRA], q[:], AX))
            after(tt(q[:], member[:], slots[:, 0:NE].unsqueeze(1).to_broadcast(XH), ALU.mult))
            after(nc.vector.reduce_sum(ids[:, NE:NE + EXTRA], q[:], AX))
            after(nc.vector.tensor_copy(ids[:, 0:NE], slots[:, 0:NE]))
            after(nc.vector.memset(ids[:, N_TABLE - 1:N_TABLE], 0.0))
            after(nc.vector.memset(place[:, :, N_TABLE - 1:N_TABLE], 0.0))
            after(nc.vector.memset(share[:, :, N_TABLE - 1:N_TABLE], 0.0))
            after(nc.vector.tensor_copy(block_expert[:], ids[0:1, :]))
            after(nc.vector.tensor_scalar(nb[:], upto_e[:, NE - 1:NE], float(NE - 1), None, ALU.add))
            after(nc.vector.tensor_copy(n_blocks[:], nb[0:1, :]))


def expert_blocks(core, htm, ident, w_gu, b_gu, w_dn, b_dn, place, share, block_expert, n_blocks, acc):
    nc = core.nc
    B = core.bank
    I32 = mybir.dt.int32
    E = D_EXPERT
    STEPS = 8
    with ExitStack() as ctx:
        (w, bgu, bdn, slots, S, Sw, SwT, xb, g, u, sig, hid, hidT, yb) = bufs(
            nc, ctx, "moe", w=[P, 6, KT, HALF], bgu=[P, 2 * E], bdn=[P, D], slots=[P, P], S=[P, TT, P],
            Sw=[P, TT, P], SwT=[P, T], xb=[P, KT, P], g=[P, HALF], u=[P, HALF], sig=[P, HALF], hid=[P, E],
            hidT=[P, KT, P], yb=[P, D])
        w_loaded = sems(nc, ctx, *(f"moe_w_loaded{c}" for c in range(6)))
        (const_loaded, bgu_loaded, bdn_loaded, product, down, hid_turned, gathered, sw_turned, scattered, slots_made,
         weighted, read_out, clipped, hid_made, yb_made, added, sig_made, xb_made, hidT_made, SwT_made, step) = sems(
            nc, ctx, *(f"moe_{s}" for s in (
                "const_loaded", "bgu_loaded", "bdn_loaded", "product", "down", "hid_turned", "gathered", "sw_turned",
                "scattered", "slots_made", "weighted", "read_out", "clipped", "hid_made", "yb_made", "added",
                "sig_made", "xb_made", "hidT_made", "SwT_made", "step")))
        block = ctx.enter_context(nc.Block())
        gu_v = w_gu.rearrange("e (k p) n -> e p k n", p=P)
        dn_v = w_dn.rearrange("e (k p) n -> e p k n", p=P)
        gu_cols = [0, E, HALF, E + HALF]

        @block.sync
        def _(sp):
            sp.dma_start(slots[:], core.const("slots")).then_inc(const_loaded, 16)

            def load(b, first):
                e = sp.value_load(block_expert[0:1, bass.ds(b, 1)], min_val=0, max_val=N_EXPERTS - 1)
                for c in range(6):
                    if not first:
                        if c < 4:
                            sp.wait_ge(product, 4 * b - 3 + c)
                        else:
                            sp.wait_ge(down, 2 * b - 5 + c)
                    src = gu_v[bass.ds(e, 1), :, :, gu_cols[c]:gu_cols[c] + HALF] if c < 4 else \
                        dn_v[bass.ds(e, 1), :, :, (c - 4) * HALF:(c - 3) * HALF]
                    sp.dma_start(w[:, c], src.rearrange("a p k n -> (a p) k n")).then_inc(w_loaded[c], 16)
                    if c == 3:
                        if not first:
                            sp.wait_ge(clipped, 2 * b)
                        sp.dma_start(bgu[:], b_gu[bass.ds(e, 1), :].to_broadcast([P, 2 * E])).then_inc(bgu_loaded, 16)
                if not first:
                    sp.wait_ge(yb_made, 2 * b)
                sp.dma_start(bdn[:], b_dn[bass.ds(e, 1), :].to_broadcast([P, D])).then_inc(bdn_loaded, 16)

            load(0, True)
            n = sp.value_load(n_blocks[0:1, 0:1], min_val=N_EXPERTS - 1, max_val=N_TABLE - 2) + 1
            with sp.Fori(1, n) as b:
                load(b, False)

        @block.tensor
        def _(pe):
            def gather(after):
                pe.wait_ge(slots_made, after)
                for half in range(2):
                    for j in range(4):
                        for t in range(TT):
                            k = 4 * half + j
                            mm = nc.tensor.matmul(B[6 + half][:, j * P:(j + 1) * P], htm[:, t, k * P:(k + 1) * P],
                                                  S[:, t, :], start=(t == 0), stop=(t == TT - 1))
                    mm.then_inc(gathered, 1)

            def gate_up(b, c):
                pe.wait_ge(w_loaded[c], 16 * b + 16)
                for k in range(KT):
                    mm = nc.tensor.matmul(B[c][:], xb[:, k, :], w[:, c, k, :], start=(k == 0), stop=(k == KT - 1))
                mm.then_inc(product, 1)

            def turn_weighted(done):
                pe.wait_ge(weighted, done)
                pe.wait_ge(hidT_made, 2 * done)
                for t in range(TT):
                    mm = nc.tensor.transpose(B[6][:, t * P:(t + 1) * P], Sw[:, t, :], ident[:])
                mm.then_inc(sw_turned, 1)

            def scatter(done):
                pe.wait_ge(SwT_made, done)
                pe.wait_ge(yb_made, 2 * done)
                for k in range(KT):
                    if k >= 2:
                        pe.wait_ge(added, KT * done - KT + k - 1)
                    nc.tensor.matmul(B[7 - k % 2][:], yb[:, k * P:(k + 1) * P], SwT[:], start=True,
                                     stop=True).then_inc(scattered, 1)

            def turn_hidden(b, half, bank):
                pe.wait_ge(hid_made, 2 * b + 1 + half)
                for j in range(4):
                    k = 4 * half + j
                    mm = nc.tensor.transpose(B[bank][:, j * P:(j + 1) * P], hid[:, k * P:(k + 1) * P], ident[:])
                mm.then_inc(hid_turned, 1)

            def down_half(b, half):
                pe.wait_ge(hidT_made, 2 * b + 1 + half)
                for n in range(2):
                    pe.wait_ge(w_loaded[4 + n], 16 * b + 16)
                    for k in range(4 * half, 4 * half + 4):
                        mm = nc.tensor.matmul(B[4 + n][:], hidT[:, k, :], w[:, 4 + n, k, :], start=(k == 0),
                                              stop=(k == KT - 1))
                    if half == 1:
                        mm.then_inc(down, 1)

            def step_block(b, first):
                pe.wait_ge(xb_made, 2 * b + 2)
                if not first:
                    pe.wait_ge(read_out, 2 * b - 1)
                gate_up(b, 0)
                if not first:
                    turn_weighted(b)
                gate_up(b, 1)
                if not first:
                    scatter(b)
                    pe.wait_ge(read_out, 2 * b)
                gate_up(b, 2)
                gate_up(b, 3)
                if not first:
                    pe.wait_ge(added, KT * b - 1)
                turn_hidden(b, 0, 7)
                down_half(b, 0)
                if not first:
                    pe.wait_ge(added, KT * b)
                gather(b + 2)
                pe.wait_ge(xb_made, 2 * b + 3)
                turn_hidden(b, 1, 6)
                down_half(b, 1)

            gather(1)
            step_block(0, True)
            n = pe.value_load(n_blocks[0:1, 0:1], min_val=N_EXPERTS - 1, max_val=N_TABLE - 2) + 1
            with pe.Fori(1, n) as b:
                step_block(b, False)
            turn_weighted(n)
            scatter(n)

        @block.scalar
        def _(act):
            def slots_out(count):
                for half in range(2):
                    act.wait_ge(gathered, count + half)
                    nc.scalar.copy(xb[:, 4 * half:4 * half + 4, :].rearrange("p k t -> p (k t)"),
                                   B[6 + half][:]).then_inc(xb_made, 1)

            def sigmoid(count):
                act.wait_ge(clipped, count)
                nc.scalar.activation(sig[:], g[:], ACT.Sigmoid, scale=SWIGLU_ALPHA).then_inc(sig_made, 1)

            def weighted_out(done):
                act.wait_ge(sw_turned, done)
                nc.scalar.copy(SwT[:], B[6][:]).then_inc(SwT_made, 1)

            def hidden_out(b, half, bank):
                act.wait_ge(hid_turned, 2 * b + 1 + half)
                nc.scalar.copy(hidT[:, 4 * half:4 * half + 4, :].rearrange("p k t -> p (k t)"),
                               B[bank][:]).then_inc(hidT_made, 1)

            def step_block(b, first):
                if not first:
                    weighted_out(b)
                sigmoid(2 * b + 1)
                hidden_out(b, 0, 7)
                sigmoid(2 * b + 2)
                slots_out(2 * b + 3)
                hidden_out(b, 1, 6)

            slots_out(1)
            step_block(0, True)
            n = act.value_load(n_blocks[0:1, 0:1], min_val=N_EXPERTS - 1, max_val=N_TABLE - 2) + 1
            with act.Fori(1, n) as b:
                step_block(b, False)
            weighted_out(n)

        @block.vector
        def _(dve):
            vec = nc.vector

            def make_slots(b):
                for t in range(TT):
                    ins = vec.tensor_scalar(S[:, t, :], slots[:], place[:, t, bass.ds(b, 1)], None, ALU.is_equal)
                ins.then_inc(slots_made, 1)

            def make_weighted(b):
                for t in range(TT):
                    ins = vec.tensor_scalar(Sw[:, t, :], slots[:], place[:, t, bass.ds(b, 1)],
                                            share[:, t, bass.ds(b, 1)], ALU.is_equal, ALU.mult)
                ins.then_inc(weighted, 1)

            def hidden(b, half, first):
                at = STEPS * b + 4 * half

                def after(instruction, n):
                    instruction.then_inc(step, 1)
                    dve.wait_ge(step, at + n)

                if half or not first:
                    dve.wait_ge(hid_made, 2 * b + half)
                dve.wait_ge(product, 4 * b + 2 + 2 * half)
                lo = half * HALF
                after(vec.tensor_tensor(g[:], B[2 * half][:], bgu[:, lo:lo + HALF], ALU.add), 1)
                after(vec.tensor_scalar(g[:], g[:], SWIGLU_LIMIT, None, ALU.min), 2)
                vec.tensor_tensor(u[:], B[2 * half + 1][:], bgu[:, E + lo:E + lo + HALF], ALU.add).then_inc(clipped, 1)
                dve.wait_ge(clipped, 2 * b + 1 + half)
                after(vec.tensor_scalar(u[:], u[:], SWIGLU_LIMIT, -SWIGLU_LIMIT, ALU.min, ALU.max), 3)
                vec.tensor_scalar(u[:], u[:], 1.0, None, ALU.add).then_inc(read_out, 1)
                dve.wait_ge(sig_made, 2 * b + 1 + half)
                after(vec.tensor_tensor(g[:], g[:], sig[:], ALU.mult), 4)
                dve.wait_ge(read_out, 2 * b + 1 + half)
                vec.tensor_tensor(hid[:, lo:lo + HALF], u[:], g[:], ALU.mult).then_inc(hid_made, 1)

            def add_back(done):
                for k in range(KT):
                    dve.wait_ge(scattered, KT * done - KT + k + 1)
                    vec.tensor_tensor(acc[:, k, :], acc[:, k, :], B[7 - k % 2][:], ALU.add).then_inc(added, 1)

            def step_block(b, first):
                dve.wait_ge(gathered, 2 * b + 2)
                make_slots(b + 1)
                dve.wait_ge(bgu_loaded, 16 * b + 16)
                hidden(b, 0, first)
                if not first:
                    add_back(b)
                    dve.wait_ge(sw_turned, b)
                make_weighted(b)
                hidden(b, 1, first)
                dve.wait_ge(bdn_loaded, 16 * b + 16)
                if not first:
                    dve.wait_ge(scattered, KT * b)
                for n in range(2):
                    dve.wait_ge(down, 2 * b + 1 + n)
                    vec.tensor_tensor(yb[:, n * HALF:(n + 1) * HALF], B[4 + n][:], bdn[:, n * HALF:(n + 1) * HALF],
                                      ALU.add).then_inc(yb_made, 1)

            vec.memset(acc[:], 0.0)
            dve.wait_ge(const_loaded, 16)
            make_slots(0)
            step_block(0, True)
            n = dve.value_load(n_blocks[0:1, 0:1], min_val=N_EXPERTS - 1, max_val=N_TABLE - 2) + 1
            with dve.Fori(1, n) as b:
                step_block(b, False)
            add_back(n)


def experts(core, a, xT, hT, ident, ones, mod, c):
    nc = core.nc
    with ExitStack() as ctx:
        (acc,) = bufs(nc, ctx, "ex", acc=[P, KT, T])
        with ExitStack() as s:
            htm, place, share = bufs(nc, s, "ex", htm=[P, TT, D], place=[P, TT, N_TABLE], share=[P, TT, N_TABLE])
            block_expert = s.enter_context(nc.sbuf_tensor("ex_block_expert", [1, N_TABLE], mybir.dt.int32))
            n_blocks = s.enter_context(nc.sbuf_tensor("ex_n_blocks", [1, 1], mybir.dt.int32))
            route(core, hT, ident, ones, a["w_router_2"][0], a["b_router_2"], htm, place, share, block_expert,
                  n_blocks)
            expert_blocks(core, htm, ident, a["w_gu_2"][0], a["b_gu_2"][0], a["w_dn_2"][0], a["b_dn_2"][0], place,
                          share, block_expert, n_blocks, acc)
        with ExitStack() as s:
            (scratch,) = bufs(nc, s, "ex", scratch=[P, KT, T])
            scale_columns(core, "g2", acc, mod[:, 40:48])
            add_tiles(core, "x2", xT, acc, ALPHA)
            norm(core, "n8", xT, xT, ones, scratch, c["post2_g"], c["post2_b"], centre=True, eps=LN_EPS)


def scale_columns(core, name, x, gain):
    nc = core.nc
    with ExitStack() as ctx:
        (scaled,) = sems(nc, ctx, f"scaled_{name}")
        block = ctx.enter_context(nc.Block())

        @block.scalar
        def _(act):
            for k in range(KT):
                nc.scalar.activation(x[:, k, :], x[:, k, :], ACT.Copy, scale=gain[:, k:k + 1]).then_inc(scaled, 1)



SSD_H, SSD_DH, SSD_N, SSD_G, SSD_CONV = 16, 64, 128, 2, 5
XBC = 1024 + 2 * SSD_G * SSD_N
XT = XBC // P
HG_H = 8
LB_FLOOR = 1e-30


def ssd_inputs(core, hT, w_in, conv_w, conv_b, zs, xbc, dt_raw):
    nc = core.nc
    B = core.bank
    PAD = SSD_CONV // 2
    w_v = w_in.rearrange("(k p) n -> p k n", p=P)
    TILES = 8 + XT
    PIECES = TILES // 4
    with ExitStack() as ctx:
        wt, wd, raw = bufs(nc, ctx, "si", w=[P, 2, KT, HALF], wd=[P, KT, SSD_H], raw=[P, XT, T + 2 * PAD])
        loaded = sems(nc, ctx, "si_loaded0", "si_loaded1")
        wd_loaded, product, copied, padded, tap, convolved, dt_product, activated = sems(
            nc, ctx, *(f"si_{s}" for s in ("wd_loaded", "product", "copied", "padded", "tap", "convolved",
                                           "dt_product", "activated")))
        block = ctx.enter_context(nc.Block())

        @block.sync
        def _(sp):
            for c in range(PIECES):
                if c >= 2:
                    sp.wait_ge(product, 4 * (c - 1))
                col = (1024 + c * HALF) if c < XT // 4 else (c - XT // 4) * HALF
                sp.dma_start(wt[:, c % 2], w_v[:, :, col:col + HALF]).then_inc(loaded[c % 2], 16)
            sp.dma_start(wd[:], w_v[:, :, 1024 + XBC:1024 + XBC + SSD_H]).then_inc(wd_loaded, 16)

        @block.tensor
        def _(pe):
            for n in range(TILES):
                c = n // 4
                pe.wait_ge(loaded[c % 2], 16 * (c // 2 + 1))
                if n >= 8:
                    pe.wait_ge(copied, n - 7)
                for k in range(KT):
                    mm = nc.tensor.matmul(B[n % 8][:], wt[:, c % 2, k, (n % 4) * P:(n % 4 + 1) * P], hT[:, k, :],
                                          start=(k == 0), stop=(k == KT - 1))
                mm.then_inc(product, 1)
            pe.wait_ge(wd_loaded, 16)
            pe.wait_ge(copied, TILES - 7)
            for k in range(KT):
                mm = nc.tensor.matmul(B[TILES % 8][0:SSD_H, :], wd[:, k, :], hT[:, k, :], start=(k == 0),
                                      stop=(k == KT - 1))
            mm.then_inc(dt_product, 1)

        @block.scalar
        def _(act):
            for n in range(TILES):
                act.wait_ge(product, n + 1)
                if n < XT:
                    nc.scalar.copy(raw[:, n, PAD:PAD + T], B[n % 8][:]).then_inc(copied, 1)
                else:
                    nc.scalar.activation(zs[:, n - XT, :], B[n % 8][:], ACT.Silu).then_inc(copied, 1)
            act.wait_ge(dt_product, 1)
            nc.scalar.copy(dt_raw[:], B[TILES % 8][0:SSD_H, :]).then_inc(activated, 1)
            for n in range(XT):
                act.wait_ge(convolved, n + 1)
                nc.scalar.activation(xbc[:, n, :], xbc[:, n, :], ACT.Silu, bias=conv_b[:, n:n + 1]).then_inc(activated, 1)

        @block.vector
        def _(dve):
            nc.vector.memset(raw[:, :, 0:PAD], 0.0).then_inc(padded, 1)
            nc.vector.memset(raw[:, :, PAD + T:], 0.0).then_inc(padded, 1)
            dve.wait_ge(padded, 2)
            for q in range(XT // 4):
                for j in range(SSD_CONV):
                    for i in range(4):
                        n = 4 * q + i
                        if j == 0:
                            dve.wait_ge(copied, n + 1)
                            nc.vector.tensor_scalar(xbc[:, n, :], raw[:, n, 0:T], conv_w[:, n, 0:1], None,
                                                    ALU.mult).then_inc(tap, 1)
                            continue
                        dve.wait_ge(tap, 4 * (4 * q + j - 1) + i + 1)
                        nc.vector.scalar_tensor_tensor(
                            out=xbc[:, n, :], in0=raw[:, n, j:j + T], scalar=conv_w[:, n, j:j + 1], in1=xbc[:, n, :],
                            op0=ALU.mult, op1=ALU.add).then_inc(convolved if j == SSD_CONV - 1 else tap, 1)


def ssd_prepare(core, xbc, x_tm, b_tm, scores, y, skip, ident):
    nc = core.nc
    B = core.bank
    with ExitStack() as ctx:
        turned, copied, skipped = sems(nc, ctx, "sp_turned", "sp_copied", "sp_skipped")
        block = ctx.enter_context(nc.Block())
        outs = [(x_tm[:, n // 2, (n % 2) * 512:(n % 2 + 1) * 512]) for n in range(8)]
        outs += [b_tm[:, 2 * n:2 * n + 2, :].rearrange("p t c -> p (t c)") for n in range(2)]
        outs += [scores[:, g, :] for g in range(SSD_G)]

        @block.tensor
        def _(pe):
            for n in range(12):
                if n >= 8:
                    pe.wait_ge(copied, n - 7)
                for j in range(4):
                    out = B[n % 8][:, j * P:(j + 1) * P]
                    if n < 8:
                        t, k = n // 2, 4 * (n % 2) + j
                        mm = nc.tensor.transpose(out, xbc[:, k, t * P:(t + 1) * P], ident[:])
                    elif n < 10:
                        t, g = 2 * (n - 8) + j // 2, j % 2
                        mm = nc.tensor.transpose(out, xbc[:, 8 + g, t * P:(t + 1) * P], ident[:])
                    else:
                        g, cols = n - 10, slice(j * P, (j + 1) * P)
                        mm = nc.tensor.matmul(out, xbc[:, 8 + g, cols], xbc[:, 10 + g, cols], start=True, stop=True)
                mm.then_inc(turned, 1)

        @block.scalar
        def _(act):
            for n in range(12):
                act.wait_ge(turned, n + 1)
                nc.scalar.copy(outs[n], B[n % 8][:]).then_inc(copied, 1)

        @block.vector
        def _(dve):
            for k in range(KT):
                nc.vector.tensor_scalar(y[:, k, :], xbc[:, k, :], skip[:, k:k + 1], None, ALU.mult).then_inc(skipped, 1)


def ssd_direction(core, d, xbc, x_tm, b_tm, scores, dt_raw, dt_bias, a_log, y, ones, ident):
    nc = core.nc
    B = core.bank
    H = SSD_H
    order = list(range(TT)) if d == 0 else list(range(TT))[::-1]
    name = f"ssd{d}"
    with ExitStack() as ctx:
        (mask, reset, sel, sel2, dt, la, G, V, I, tmp, tmp2, neg, diag, dT, GT, WT, CD, xdt, xw, gm, seg, wgt, ep, prod,
         S) = bufs(
            nc, ctx, name, mask=[P, P], reset=[H, T], sel=[H, H * P], sel2=[H, KT * P], dt=[H, T], la=[H, T],
            G=[H, T], V=[H, T], I=[H, T], tmp=[H, T], tmp2=[H, T], neg=[H, 1], diag=[H, TT, H], dT=[P, TT, H],
            GT=[P, TT, H], WT=[P, TT, H], CD=[P, TT, H], xdt=[P, TT, D], xw=[P, D], gm=[P, SSD_G, T],
            seg=[P, 2, T], wgt=[P, 2, T], ep=[P, 2, T], prod=[P, T], S=[P, TT, D])
        (loaded, step, act_step, to_act, from_act, rows_ready, turned, dec_made, cols_ready, xw_made, u_made, state,
         spread, seg_made, seg_exped, weights, pair_done, ep_spread, ep_made, y_added) = sems(
            nc, ctx, *(f"{name}_{s}" for s in (
                "loaded", "step", "act_step", "to_act", "from_act", "rows_ready", "turned", "dec_made", "cols_ready",
                "xw_made", "u_made", "state", "spread", "seg_made", "seg_exped", "weights", "pair_done", "ep_spread",
                "ep_made", "y_added")))
        block = ctx.enter_context(nc.Block())
        chunks = lambda ap: ap[:].rearrange("p (c t) -> p c t", t=P)
        ends = lambda ap: chunks(ap)[:, :, P - 1:P].to_broadcast([H, TT, P])

        @block.sync
        def _(sp):
            sp.dma_start(mask[:], core.const("upto" if d == 0 else "from")).then_inc(loaded, 16)
            sp.dma_start(reset[:], core.const("reset128", H)).then_inc(loaded, 16)
            sp.dma_start(sel[:], core.const("one_head", H)).then_inc(loaded, 16)
            sp.dma_start(sel2[:], core.const("two_heads", H)).then_inc(loaded, 16)

        @block.scalar
        def _(act):
            act.wait_ge(to_act, 1)
            nc.scalar.activation(tmp[:], dt[:], ACT.Abs).then_inc(act_step, 1)
            act.wait_ge(act_step, 1)
            nc.scalar.activation(tmp[:], tmp[:], ACT.Exp, scale=-1.0).then_inc(act_step, 1)
            nc.scalar.activation(neg[:], a_log[:, d:d + 1], ACT.Exp).then_inc(act_step, 1)
            act.wait_ge(act_step, 3)
            nc.scalar.activation(tmp2[:], tmp[:], ACT.Ln, bias=1.0).then_inc(from_act, 1)
            act.wait_ge(to_act, 2)
            nc.scalar.activation(V[:], V[:], ACT.Exp).then_inc(act_step, 1)
            nc.scalar.activation(tmp2[:, 0:TT], chunks(tmp)[:, :, P - 1], ACT.Exp).then_inc(from_act, 1)
            for k in range(KT):
                for h in (2 * k, 2 * k + 1):
                    act.wait_ge(seg_made, h + 1)
                    if h >= 2:
                        act.wait_ge(weights, h - 1)
                    nc.scalar.activation(seg[:, h % 2, :], seg[:, h % 2, :], ACT.Exp,
                                         scale=1.0 if d == 0 else -1.0).then_inc(seg_exped, 1)
                act.wait_ge(ep_spread, k + 1)
                if k >= 2:
                    act.wait_ge(y_added, k - 1)
                nc.scalar.activation(ep[:, k % 2, :], B[6][:], ACT.Exp).then_inc(ep_made, 1)

        @block.vector
        def _(dve):
            steps = Count(step)
            vec, tt = nc.vector, nc.vector.tensor_tensor

            def after(instruction):
                dve.wait_ge(step, steps.by(instruction))

            vec.tensor_scalar(dt[:], dt_raw[:], dt_bias[:, d:d + 1], None, ALU.add).then_inc(to_act, 1)
            dve.wait_ge(from_act, 1)
            after(vec.tensor_scalar(la[:], tmp[:], 1.0, -1.0, ALU.add, ALU.add))
            after(vec.tensor_scalar(V[:], la[:], 0.0, None, ALU.is_equal))
            after(tt(tmp2[:], tmp2[:], V[:], ALU.add))
            after(tt(la[:], la[:], V[:], ALU.add))
            after(vec.reciprocal(la[:], la[:]))
            after(tt(la[:], la[:], tmp2[:], ALU.mult))
            after(tt(tmp[:], tmp[:], la[:], ALU.mult))
            after(vec.scalar_tensor_tensor(out=dt[:], in0=dt[:], scalar=0.0, in1=tmp[:], op0=ALU.max, op1=ALU.add))
            after(vec.tensor_scalar(la[:], dt[:], neg[:], -1.0, ALU.mult, ALU.mult))
            dve.wait_ge(loaded, 64)
            after(vec.tensor_tensor_scan(tmp[:], reset[:], la[:], 0.0, ALU.mult, ALU.add))
            if d == 0:
                after(vec.tensor_copy(G[:], tmp[:]))
                after(vec.tensor_copy(I[:], tmp[:]))
                last = tt(chunks(V), ends(tmp), chunks(G), ALU.subtract)
            else:
                after(tt(G[:], tmp[:], la[:], ALU.subtract))
                after(tt(chunks(I), ends(tmp), chunks(G), ALU.subtract))
                last = vec.tensor_copy(V[:], G[:])
            last.then_inc(to_act, 1)
            dve.wait_ge(from_act, 2)
            tt(V[:], V[:], dt[:], ALU.mult)
            for c in range(TT):
                last = vec.tensor_scalar(diag[:, c, :], ident[0:H, 0:H], tmp2[:, c:c + 1], None, ALU.mult)
            last.then_inc(rows_ready, 1)
            for g in range(SSD_G):
                tt(gm[:, g, :].rearrange("p (c t) -> p c t", t=P), scores[:, g, :].rearrange("p (c t) -> p c t", t=P),
                   mask[:].unsqueeze(1).to_broadcast([P, TT, P]), ALU.mult).then_inc(cols_ready, 1)
            dve.wait_ge(turned, 1)
            for i, dst in enumerate((dT, GT, WT, CD)):
                last = vec.tensor_copy(dst[:].rearrange("p c h -> p (c h)"), B[0][:, i * TT * H:(i + 1) * TT * H])
            last.then_inc(cols_ready, 1)
            dve.wait_ge(cols_ready, SSD_G + 1)
            by_head = lambda ap: ap.rearrange("p (h e) -> p h e", e=SSD_DH)
            for c in range(TT):
                tt(by_head(xdt[:, c, :]), by_head(x_tm[:, c, :]),
                   dT[:, c, :].unsqueeze(2).to_broadcast([P, H, SSD_DH]), ALU.mult).then_inc(cols_ready, 1)
            vec.memset(S[:, order[0], :], 0.0).then_inc(state, 1)
            for i, c in enumerate(order[:-1]):
                if i:
                    dve.wait_ge(u_made, 2 * i)
                tt(by_head(xw[:]), by_head(x_tm[:, c, :]), WT[:, c, :].unsqueeze(2).to_broadcast([P, H, SSD_DH]),
                   ALU.mult).then_inc(xw_made, 1)
                nxt = order[i + 1]
                dve.wait_ge(state, 3 * i + 1)
                tt(by_head(S[:, nxt, :]), by_head(S[:, c, :]), CD[:, c, :].unsqueeze(2).to_broadcast([P, H, SSD_DH]),
                   ALU.mult).then_inc(state, 1)
                dve.wait_ge(state, 3 * i + 2)
                for g in range(SSD_G):
                    dve.wait_ge(u_made, 2 * i + g + 1)
                    cols = slice(g * 512, (g + 1) * 512)
                    last = tt(S[:, nxt, cols], S[:, nxt, cols], B[1 + g][:], ALU.add)
                last.then_inc(state, 2)
                dve.wait_ge(state, 3 * i + 4)
            for k in range(KT):
                for h in (2 * k, 2 * k + 1):
                    dve.wait_ge(spread, h + 1)
                    if h >= 2:
                        dve.wait_ge(weights, h - 1)
                    for c in range(TT):
                        cols = slice(c * P, (c + 1) * P)
                        last = vec.tensor_scalar(seg[:, h % 2, cols], B[h % 2][:, cols], GT[:, c, h:h + 1], 0.0,
                                                 ALU.subtract, ALU.min if d == 0 else ALU.max)
                    last.then_inc(seg_made, 1)
                for h in (2 * k, 2 * k + 1):
                    dve.wait_ge(seg_exped, h + 1)
                    if k:
                        dve.wait_ge(pair_done, k)
                    tt(wgt[:, h % 2, :], seg[:, h % 2, :], gm[:, h // 8, :], ALU.mult).then_inc(weights, 1)
                dve.wait_ge(pair_done, k + 1)
                dve.wait_ge(ep_made, k + 1)
                after(tt(prod[:], B[4 + k % 2][:], ep[:, k % 2, :], ALU.mult))
                after(tt(prod[:], prod[:], B[2 + k % 2][:], ALU.add))
                tt(y[:, k, :], y[:, k, :], prod[:], ALU.add).then_inc(y_added, 1)
                dve.wait_ge(y_added, k + 1)

        @block.tensor
        def _(pe):
            pe.wait_ge(rows_ready, 1)
            for i, rows in enumerate((dt, G, V)):
                for c in range(TT):
                    at = (i * TT + c) * H
                    nc.tensor.transpose(B[0][:, at:at + H], rows[:, c * P:(c + 1) * P], ident[0:H, 0:H])
            for c in range(TT):
                at = (3 * TT + c) * H
                mm = nc.tensor.matmul(B[0][:, at:at + H], ones[0:H, :], diag[:, c, :], start=True, stop=True)
            mm.then_inc(turned, 1)
            for i, c in enumerate(order[:-1]):
                pe.wait_ge(xw_made, i + 1)
                pe.wait_ge(state, 3 * i + 1)
                for g in range(SSD_G):
                    nc.tensor.matmul(B[1 + g][:], b_tm[:, c, g * P:(g + 1) * P], xw[:, g * 512:(g + 1) * 512],
                                     start=True, stop=True).then_inc(u_made, 1)
            pe.wait_ge(state, 3 * (TT - 1) + 1)
            pe.wait_ge(cols_ready, SSD_G + 1 + TT)

            def spread_head(h):
                if h >= 2:
                    pe.wait_ge(seg_made, h - 1)
                nc.tensor.matmul(B[h % 2][:], sel[:, h * P:(h + 1) * P], G[:], start=True, stop=True).then_inc(spread, 1)

            spread_head(0)
            spread_head(1)
            for k in range(KT):
                if k + 1 < KT:
                    spread_head(2 * k + 2)
                    spread_head(2 * k + 3)
                if k:
                    pe.wait_ge(ep_made, k)
                nc.tensor.matmul(B[6][:], sel2[:, k * P:(k + 1) * P], I[:], start=True, stop=True).then_inc(ep_spread, 1)
                if k >= 2:
                    pe.wait_ge(y_added, k - 1)
                for c in range(TT):
                    cols = slice(c * P, (c + 1) * P)
                    nc.tensor.matmul(B[4 + k % 2][:, cols], S[:, c, k * P:(k + 1) * P], xbc[:, 10 + k // 4, cols],
                                     start=True, stop=True)
                for h in (2 * k, 2 * k + 1):
                    pe.wait_ge(weights, h + 1)
                    rows = slice(SSD_DH * (h % 2), SSD_DH * (h % 2) + SSD_DH)
                    for c in range(TT):
                        cols = slice(c * P, (c + 1) * P)
                        mm = nc.tensor.matmul(B[2 + k % 2][rows, cols], xdt[:, c, h * SSD_DH:(h + 1) * SSD_DH],
                                              wgt[:, h % 2, cols], start=True, stop=True, skip_group_check=True)
                mm.then_inc(pair_done, 1)


def multiply_tiles(core, name, x, y):
    nc = core.nc
    with ExitStack() as ctx:
        (done,) = sems(nc, ctx, f"multiplied_{name}")
        block = ctx.enter_context(nc.Block())

        @block.vector
        def _(dve):
            for k in range(x.shape[1]):
                nc.vector.tensor_tensor(x[:, k, :], x[:, k, :], y[:, k, :], ALU.mult).then_inc(done, 1)


def hgrn_gates(core, d, f, kh, lower):
    nc = core.nc
    floor_log, rest_log, rest, total = lower
    name = f"hgate{d}"
    with ExitStack() as ctx:
        reset, a, b = bufs(nc, ctx, name, reset=[P, T], a=[P, 2, T], b=[P, 2, T])
        diff, = bufs(nc, ctx, name, diff=[P, KT])
        loaded, diffed, s1, s2, s3, s4, s5, d1, d2, d3, d4, done = sems(
            nc, ctx, *(f"{name}_{s}" for s in (
                "loaded", "diffed", "abs", "exp", "log", "rate", "outer_log", "sigmoid", "kept", "shifted", "joined",
                "done")))
        block = ctx.enter_context(nc.Block())

        @block.sync
        def _(sp):
            sp.dma_start(reset[:], core.const("reset128")).then_inc(loaded, 16)

        @block.scalar
        def _(act):
            for k in range(KT):
                s = k % 2
                if k >= 2:
                    act.wait_ge(d4, k - 1)
                nc.scalar.activation(a[:, s, :], f[:, k, :], ACT.Abs).then_inc(s1, 1)
                act.wait_ge(s1, k + 1)
                nc.scalar.activation(a[:, s, :], a[:, s, :], ACT.Exp, scale=-1.0).then_inc(s2, 1)
                act.wait_ge(s2, k + 1)
                nc.scalar.activation(a[:, s, :], a[:, s, :], ACT.Ln, bias=1.0).then_inc(s3, 1)
                act.wait_ge(d2, k + 1)
                nc.scalar.activation(kh[:, k, :], kh[:, k, :], ACT.Exp).then_inc(s4, 1)
                act.wait_ge(d3, k + 1)
                nc.scalar.activation(a[:, s, :], b[:, s, :], ACT.Abs).then_inc(s5, 1)
                act.wait_ge(s5, 3 * k + 1)
                nc.scalar.activation(a[:, s, :], a[:, s, :], ACT.Exp, scale=-1.0).then_inc(s5, 1)
                act.wait_ge(s5, 3 * k + 2)
                nc.scalar.activation(a[:, s, :], a[:, s, :], ACT.Ln, bias=1.0).then_inc(s5, 1)

        @block.vector
        def _(dve):
            vec = nc.vector
            cols = slice(KT * d, KT * (d + 1))
            vec.tensor_tensor(diff[:], rest_log[:, cols], floor_log[:, cols], ALU.subtract).then_inc(diffed, 1)
            dve.wait_ge(diffed, 1)
            dve.wait_ge(loaded, 16)
            for k in range(KT):
                s = k % 2
                at = KT * d + k
                dve.wait_ge(s3, k + 1)
                vec.scalar_tensor_tensor(out=b[:, s, :], in0=f[:, k, :], scalar=0.0, in1=a[:, s, :], op0=ALU.min,
                                         op1=ALU.subtract).then_inc(d1, 1)
                dve.wait_ge(d1, k + 1)
                vec.tensor_tensor(kh[:, k, :], b[:, s, :], f[:, k, :], ALU.subtract).then_inc(d2, 1)
                dve.wait_ge(d2, k + 1)
                vec.tensor_scalar(b[:, s, :], b[:, s, :], diff[:, k:k + 1], None, ALU.add).then_inc(d3, 1)
                dve.wait_ge(s5, 3 * k + 3)
                vec.scalar_tensor_tensor(out=b[:, s, :], in0=b[:, s, :], scalar=0.0, in1=a[:, s, :], op0=ALU.max,
                                         op1=ALU.add).then_inc(d4, 1)
                dve.wait_ge(d4, k + 1)
                vec.tensor_scalar(b[:, s, :], b[:, s, :], floor_log[:, at:at + 1], None, ALU.add).then_inc(done, 1)
                dve.wait_ge(done, 5 * k + 1)
                vec.tensor_tensor_scan(f[:, k, :], reset[:], b[:, s, :], 0.0, ALU.mult, ALU.add).then_inc(done, 1)
                dve.wait_ge(s4, k + 1)
                vec.tensor_scalar(kh[:, k, :], kh[:, k, :], rest[:, at:at + 1], None, ALU.mult).then_inc(done, 1)
                dve.wait_ge(done, 5 * k + 3)
                vec.tensor_copy(total[:, k, :], f[:, k, P - 1:T:P]).then_inc(done, 1)
                dve.wait_ge(done, 5 * k + 4)
                if d == 0:
                    vec.tensor_copy(a[:, s, 0:1], f[:, k, 0:1]).then_inc(done, 1)
                else:
                    vec.tensor_tensor(f[:, k, :], f[:, k, :], b[:, s, :], ALU.subtract).then_inc(done, 1)
                dve.wait_ge(done, 5 * k + 5)


def hgrn_direction(core, d, q, G, kh, total, v_tm, y, ident):
    nc = core.nc
    B = core.bank
    name = f"hg{d}"
    LEVELS = [64, 32, 16, 8, 4, 2, 1]
    NL = len(LEVELS)
    NM = NL + 1
    order = list(range(TT)) if d == 0 else list(range(TT))[::-1]
    R = 3
    with ExitStack() as ctx:
        mask, diff, qs, ks, A, qe, kd, kdT, dec, S = bufs(
            nc, ctx, name, mask=[P, NM, P], diff=[P, R, T], qs=[P, R, T], ks=[P, R, T], A=[P, 2, T], qe=[P, 2, T],
            kd=[P, 2, T], kdT=[P, T], dec=[P, KT, TT], S=[P, TT, P])
        (loaded, diffed, exped, scaled, product, picked, zeroed, decayed, end_diffed, end_exped, end_scaled, turned,
         turned_copied, u_made, state, out_made, added) = sems(
            nc, ctx, *(f"{name}_{s}" for s in (
                "loaded", "diffed", "exped", "scaled", "product", "picked", "zeroed", "decayed", "end_diffed",
                "end_exped", "end_scaled", "turned", "turned_copied", "u_made", "state", "out_made", "added")))
        block = ctx.enter_context(nc.Block())

        def halves(ap, m):
            return ap.rearrange("p (b two m) -> p b two m", two=2, m=m)

        q_half, k_half = (1, 0) if d == 0 else (0, 1)

        @block.sync
        def _(sp):
            sp.dma_start(mask[:].rearrange("p l t -> p (l t)"),
                         core.const("levels" if d == 0 else "levels_back")).then_inc(loaded, 16)

        @block.gpsimd
        def _(pool):
            nc.gpsimd.memset(qs[:], 0.0).then_inc(zeroed, 1)
            nc.gpsimd.memset(ks[:], 0.0).then_inc(zeroed, 1)
            nc.gpsimd.memset(A[:], 0.0).then_inc(zeroed, 1)
            nc.gpsimd.memset(S[:, order[0], :], 0.0).then_inc(zeroed, 1)
            for h in range(HG_H):
                g = G[:, h, :].rearrange("p (c t) -> p c t", t=P)
                if h >= 2:
                    pool.wait_ge(end_scaled, h - 1)
                e = (kd if d == 0 else qe)[:, h % 2, :].rearrange("p (c t) -> p c t", t=P)
                if h >= 2:
                    pool.wait_ge(out_made, h - 1)
                nc.gpsimd.tensor_tensor(e, total[:, h, :].unsqueeze(2).to_broadcast([P, TT, P]), g,
                                        ALU.subtract).then_inc(end_diffed, 1)
                for i, m in enumerate(LEVELS):
                    n = h * NL + i
                    if n >= R:
                        pool.wait_ge(exped, n - R + 1)
                    src = halves(G[:, h, :], m)
                    edge = src[:, :, 0, m - 1:m] if d == 0 else src[:, :, 1, 0:1]
                    nb = T // (2 * m)
                    flat = G[:, h, :].rearrange("p (b m) -> p b m", m=2 * m)
                    nc.gpsimd.tensor_tensor(diff[:, n % R, :].rearrange("p (b m) -> p b m", m=2 * m), flat,
                                            edge.to_broadcast([P, nb, 2 * m]), ALU.subtract).then_inc(diffed, 1)

        @block.scalar
        def _(act):
            nc.scalar.activation(dec[:], total[:], ACT.Exp).then_inc(decayed, 1)

            def turned_out(h):
                act.wait_ge(turned, h + 1)
                nc.scalar.copy(kdT[:], B[4][:]).then_inc(turned_copied, 1)

            for h in range(HG_H):
                act.wait_ge(end_diffed, h + 1)
                one, other = (kd, qe) if d == 0 else (qe, kd)
                nc.scalar.activation(one[:, h % 2, :], one[:, h % 2, :], ACT.Exp)
                nc.scalar.activation(other[:, h % 2, :], G[:, h, :], ACT.Exp).then_inc(end_exped, 1)
                for i, m in enumerate(LEVELS):
                    n = h * NL + i
                    act.wait_ge(diffed, n + 1)
                    if n < R:
                        act.wait_ge(zeroed, 2)
                    else:
                        act.wait_ge(product, h * NM + i - R + (0 if i >= R else 0) + 1 if i >= R else
                                    (h - 1) * NM + NL + i - R + 1)
                    src, qd, kk = (halves(x[:, n % R, :], m) for x in (diff, qs, ks))
                    nc.scalar.activation(qd[:, :, q_half, :], src[:, :, q_half, :], ACT.Exp,
                                         scale=1.0 if d == 0 else -1.0)
                    nc.scalar.activation(kk[:, :, k_half, :], src[:, :, k_half, :], ACT.Exp,
                                         scale=-1.0 if d == 0 else 1.0).then_inc(exped, 1)
                    if i == 2:
                        turned_out(h)

        @block.vector
        def _(dve):
            vec = nc.vector
            dve.wait_ge(loaded, 16)
            dve.wait_ge(zeroed, 4)
            dve.wait_ge(decayed, 1)

            def pick(h, j):
                n = h * NM + j
                dve.wait_ge(product, n + 1)
                dve.wait_ge(out_made, h - 1) if h >= 2 and j == 0 else None
                if n:
                    dve.wait_ge(picked, n)
                vec.copy_predicated(A[:, h % 2, :].rearrange("p (c t) -> p c t", t=P),
                                    mask[:, j, :].bitcast(U32).unsqueeze(1).to_broadcast([P, TT, P]),
                                    B[n % 4][:].rearrange("p (c t) -> p c t", t=P)).then_inc(picked, 1)

            def finish(h):
                dve.wait_ge(out_made, h + 1)
                vec.tensor_tensor(y[:, h, :], y[:, h, :], B[6 + h % 2][:], ALU.add).then_inc(added, 1)

            for h in range(HG_H):
                dve.wait_ge(end_exped, h + 1)
                vec.tensor_tensor(qe[:, h % 2, :], qe[:, h % 2, :], q[:, h, :], ALU.mult)
                vec.tensor_tensor(kd[:, h % 2, :], kd[:, h % 2, :], kh[:, h, :], ALU.mult).then_inc(end_scaled, 1)
                for i, m in enumerate(LEVELS):
                    n = h * NL + i
                    dve.wait_ge(exped, n + 1)
                    qd, qq, kk, kq = (halves(x, m) for x in (qs[:, n % R, :], q[:, h, :], ks[:, n % R, :], kh[:, h, :]))
                    vec.tensor_tensor(qd[:, :, q_half, :], qd[:, :, q_half, :], qq[:, :, q_half, :], ALU.mult)
                    vec.tensor_tensor(kk[:, :, k_half, :], kk[:, :, k_half, :], kq[:, :, k_half, :],
                                      ALU.mult).then_inc(scaled, 1)
                    if i >= 1:
                        pick(h, i - 1)
                    if i == 1 and h:
                        finish(h - 1)
                    if i == 4:
                        for j, c in enumerate(order[:-1]):
                            dve.wait_ge(u_made, h + 1)
                            if h or j:
                                dve.wait_ge(state, (TT - 1) * h + j)
                            if h and j == 0:
                                dve.wait_ge(out_made, h)
                            vec.scalar_tensor_tensor(out=S[:, order[j + 1], :], in0=S[:, c, :],
                                                     scalar=dec[:, h, c:c + 1], in1=B[5][:, c * P:(c + 1) * P],
                                                     op0=ALU.mult, op1=ALU.add).then_inc(state, 1)
                pick(h, NL - 1)
                pick(h, NL)
            finish(HG_H - 1)

        @block.tensor
        def _(pe):
            def pairs(h, j, right, left):
                n = h * NM + j
                if n >= 4:
                    pe.wait_ge(picked, n - 3)
                for c in range(TT):
                    cols = slice(c * P, (c + 1) * P)
                    mm = nc.tensor.matmul(B[n % 4][:, cols], left[:, cols], right[:, cols], start=True, stop=True)
                mm.then_inc(product, 1)

            def output(h):
                pe.wait_ge(picked, NM * (h + 1))
                pe.wait_ge(state, (TT - 1) * (h + 1))
                if h >= 2:
                    pe.wait_ge(added, h - 1)
                out = B[6 + h % 2]
                for c in range(TT):
                    cols = slice(c * P, (c + 1) * P)
                    nc.tensor.matmul(out[:, cols], v_tm[:, c, h * P:(h + 1) * P], A[:, h % 2, cols], start=True,
                                     stop=False)
                    mm = nc.tensor.matmul(out[:, cols], S[:, c, :], qe[:, h % 2, cols], start=False, stop=True)
                mm.then_inc(out_made, 1)

            for h in range(HG_H):
                for i in range(NL):
                    n = h * NL + i
                    pe.wait_ge(scaled, n + 1)
                    pairs(h, i, qs[:, n % R, :], ks[:, n % R, :])
                    if i == 0:
                        pe.wait_ge(end_scaled, h + 1)
                        if h:
                            pe.wait_ge(turned_copied, h)
                        for c in range(TT):
                            cols = slice(c * P, (c + 1) * P)
                            mm = nc.tensor.transpose(B[4][:, cols], kd[:, h % 2, cols], ident[:])
                        mm.then_inc(turned, 1)
                        if h:
                            output(h - 1)
                    if i == 3:
                        pe.wait_ge(turned_copied, h + 1)
                        if h:
                            pe.wait_ge(state, (TT - 1) * h)
                        for c in range(TT):
                            cols = slice(c * P, (c + 1) * P)
                            mm = nc.tensor.matmul(B[5][:, cols], kdT[:, cols], v_tm[:, c, h * P:(h + 1) * P],
                                                  start=True, stop=True)
                        mm.then_inc(u_made, 1)
                pairs(h, NL, q[:, h, :], kh[:, h, :])
            output(HG_H - 1)


def turn_out(core, iv, v_tm, ident):
    nc = core.nc
    B = core.bank
    with ExitStack() as ctx:
        turned, copied = sems(nc, ctx, "tv_turned", "tv_copied")
        block = ctx.enter_context(nc.Block())

        @block.tensor
        def _(pe):
            for n in range(8):
                for j in range(4):
                    t, k = n // 2, 4 * (n % 2) + j
                    mm = nc.tensor.transpose(B[n][:, j * P:(j + 1) * P], iv[:, k, t * P:(t + 1) * P], ident[:])
                mm.then_inc(turned, 1)

        @block.scalar
        def _(act):
            for n in range(8):
                act.wait_ge(turned, n + 1)
                nc.scalar.copy(v_tm[:, n // 2, (n % 2) * 512:(n % 2 + 1) * 512], B[n][:]).then_inc(copied, 1)


def zero_tiles(core, y):
    nc = core.nc
    with ExitStack() as ctx:
        (zeroed,) = sems(nc, ctx, "y_zeroed")
        block = ctx.enter_context(nc.Block())

        @block.vector
        def _(dve):
            nc.vector.memset(y[:], 0.0).then_inc(zeroed, 1)


def hgrn_norm(core, y, gain, gate, ones, scratch):
    nc = core.nc
    B = core.bank
    with ExitStack() as ctx:
        (eps_col,) = bufs(nc, ctx, "hn", eps=[P, 1])
        eps_set, squared, summed, rooted, inverted, normed, done = sems(
            nc, ctx, *(f"hn_{s}" for s in ("eps", "squared", "summed", "rooted", "inverted", "normed", "done")))
        block = ctx.enter_context(nc.Block())

        @block.gpsimd
        def _(pool):
            nc.gpsimd.memset(eps_col[:], EPS).then_inc(eps_set, 1)

        @block.scalar
        def _(act):
            for k in range(HG_H):
                nc.scalar.activation(scratch[:, k, :], y[:, k, :], ACT.Square).then_inc(squared, 1)
            act.wait_ge(eps_set, 1)
            for k in range(HG_H):
                act.wait_ge(summed, k + 1)
                nc.scalar.activation(scratch[:, k, :], B[k][:], ACT.Sqrt, bias=eps_col[:],
                                     scale=1.0 / P).then_inc(rooted, 1)

        @block.tensor
        def _(pe):
            for k in range(HG_H):
                pe.wait_ge(squared, k + 1)
                nc.tensor.matmul(B[k][:], ones[:], scratch[:, k, :], start=True, stop=True).then_inc(summed, 1)

        @block.vector
        def _(dve):
            for k in range(HG_H):
                dve.wait_ge(rooted, k + 1)
                nc.vector.reciprocal(scratch[:, k, :], scratch[:, k, :]).then_inc(inverted, 1)
                dve.wait_ge(inverted, k + 1)
                nc.vector.tensor_tensor(y[:, k, :], y[:, k, :], scratch[:, k, :], ALU.mult).then_inc(normed, 1)
                dve.wait_ge(normed, k + 1)
                nc.vector.scalar_tensor_tensor(out=y[:, k, :], in0=y[:, k, :], scalar=gain[:], in1=gate[:, k, :],
                                               op0=ALU.mult, op1=ALU.mult).then_inc(done, 1)


def lower_bounds(core, raw, lower, gain1, w1, s1, gain2, w2, s2):
    nc = core.nc
    floor_log, rest_log, rest, _ = lower
    SCALE = 2.0 ** 64
    with ExitStack() as ctx:
        e, s, lb = bufs(nc, ctx, "lb", e=[P, 2 * KT], s=[P, 2 * KT], lb=[P, 2 * KT])
        step, to_act, from_act = sems(nc, ctx, "lb_step", "lb_to_act", "lb_from_act")
        block = ctx.enter_context(nc.Block())

        @block.scalar
        def _(act):
            act.wait_ge(to_act, 1)
            nc.scalar.activation(e[:], e[:], ACT.Exp).then_inc(from_act, 1)
            act.wait_ge(to_act, 2)
            nc.scalar.activation(floor_log[:], lb[:], ACT.Ln, scale=SCALE)
            nc.scalar.activation(rest_log[:], rest[:], ACT.Ln).then_inc(from_act, 1)

        @block.vector
        def _(dve):
            steps = Count(step)

            def after(instruction):
                dve.wait_ge(step, steps.by(instruction))

            vec = nc.vector
            vec.tensor_tensor(e[:], raw[:], raw[:], ALU.subtract).then_inc(to_act, 1)
            dve.wait_ge(from_act, 1)
            after(vec.reciprocal(s[:], e[:]))
            after(vec.tensor_tensor(e[:], e[:], s[:], ALU.mult))
            after(vec.tensor_tensor(lb[:], e[:], e[:], ALU.subtract))
            after(vec.tensor_scalar(rest[:], lb[:], -1.0, 1.0, ALU.mult, ALU.add))
            vec.tensor_scalar(lb[:], lb[:], LB_FLOOR, None, ALU.max).then_inc(to_act, 1)
            vec.tensor_tensor(gain1[:], w1[:], s1, ALU.mult)
            vec.tensor_tensor(gain2[:], w2[:], s2, ALU.mult)
            dve.wait_ge(from_act, 2)
            after(vec.tensor_scalar(floor_log[:], floor_log[:], -64.0 * math.log(2.0), None, ALU.add))


def third_columns(core, ctx, a):
    nc = core.nc
    shapes = dict(ada_b=48, norm_mix_w=8, norm_mlp_w=8, conv_b=XT, ssd_norm_w=8, hg_norm_w=1)
    c = dict(zip(shapes, bufs(nc, ctx, "c3", **{n: [P, w] for n, w in shapes.items()})))
    more = dict(conv_w=[P, XT, SSD_CONV], cond=[P, KT], final=[P, KT], raw_lb=[P, 2 * KT], skip=[P, KT],
                dt_bias=[SSD_H, 2], a_log=[SSD_H, 2], gain1=[P, KT], gain2=[P, KT], floor_log=[P, 2 * KT],
                rest_log=[P, 2 * KT], rest=[P, 2 * KT], total=[P, KT, TT])
    c.update(zip(more, bufs(nc, ctx, "c3", **more)))
    load_columns(core, [(c[n][:], a[f"{n}_3"][0]) for n in shapes]
                 + [(c["conv_w"][:, :, j], a["conv_w_3"][0, j]) for j in range(SSD_CONV)]
                 + [(c["cond"][:], a["c_3"][0]), (c["final"][:], a["final_norm_w_3"])]
                 + [(c["raw_lb"][:, KT * d:KT * (d + 1)], a["hg_lower_bounds_3"][d, 0]) for d in range(2)])
    with ExitStack() as s:
        (loaded,) = sems(nc, s, "c3_loaded")
        block = s.enter_context(nc.Block())

        @block.sync
        def _(sp):
            with nc.allow_non_contiguous_dma("columns"):
                sp.dma_start(c["dt_bias"][:], a["dt_bias_3"][0].rearrange("d h -> h d")).then_inc(loaded, 16)
                sp.dma_start(c["a_log"][:], a["a_log_3"][0].rearrange("d h -> h d")).then_inc(loaded, 16)
                for half in range(2):
                    sp.dma_start(c["skip"][64 * half:64 * half + 64, :],
                                 bcast_rows(a["d_skip_3"][:, half:SSD_H:2], 64)).then_inc(loaded, 16)
            sp.wait_ge(loaded, 64)
    return c


def store_out(core, xT, ident, out):
    nc = core.nc
    B = core.bank
    with ExitStack() as ctx:
        (rows,) = bufs(nc, ctx, "so", rows=[P, TT, D])
        turned, copied, stored = sems(nc, ctx, "so_turned", "so_copied", "so_stored")
        block = ctx.enter_context(nc.Block())

        @block.tensor
        def _(pe):
            for n in range(8):
                for j in range(4):
                    t, k = n // 2, 4 * (n % 2) + j
                    mm = nc.tensor.transpose(B[n][:, j * P:(j + 1) * P], xT[:, k, t * P:(t + 1) * P], ident[:])
                mm.then_inc(turned, 1)

        @block.scalar
        def _(act):
            for n in range(8):
                act.wait_ge(turned, n + 1)
                nc.scalar.copy(rows[:, n // 2, (n % 2) * 512:(n % 2 + 1) * 512], B[n][:]).then_inc(copied, 1)

        @block.sync
        def _(sp):
            for t in range(TT):
                sp.wait_ge(copied, 2 * t + 2)
                sp.dma_start(out[0, t * P:(t + 1) * P, :], rows[:, t, :]).then_inc(stored, 16)
            sp.wait_ge(stored, 16 * TT)


def third_block(core, a, xT, hT, ident, ones, out):
    nc = core.nc
    w_in = a["w_in_3"][0]
    with ExitStack() as ctx:
        c = third_columns(core, ctx, a)
        (mod,) = bufs(nc, ctx, "b3", mod=[P, 48])
        modulation(core, "mod3", a["ada_w_3"][0], c["cond"], c["ada_b"], mod, (8, 32))
        lower = (c["floor_log"], c["rest_log"], c["rest"], c["total"])
        lower_bounds(core, c["raw_lb"], lower, c["gain1"], c["norm_mix_w"], mod[:, 8:16], c["gain2"],
                     c["norm_mlp_w"], mod[:, 32:40])
        with ExitStack() as s:
            (ycat,) = bufs(nc, s, "b3", ycat=[P, 2 * KT, T])
            y_ssd, y_hg = ycat[:, 0:KT, :], ycat[:, KT:2 * KT, :]
            norm(core, "n9", xT, hT, ones, y_hg, c["gain1"], mod[:, 0:8])
            with ExitStack() as r:
                zs, dt_raw = bufs(nc, r, "b3", zs=[P, KT, T], dt_raw=[SSD_H, T])
                with ExitStack() as q:
                    xbc, = bufs(nc, q, "b3", xbc=[P, XT, T])
                    ssd_inputs(core, hT, w_in, c["conv_w"], c["conv_b"], zs, xbc, dt_raw)
                    b_tm, scores = bufs(nc, q, "b3", b_tm=[P, TT, SSD_G * P], scores=[P, SSD_G, T])
                    x_tm = y_hg.rearrange("p (t a) c -> p t (a c)", a=2)
                    ssd_prepare(core, xbc, x_tm, b_tm, scores, y_ssd, c["skip"], ident)
                    for d in range(2):
                        ssd_direction(core, d, xbc, x_tm, b_tm, scores, dt_raw, c["dt_bias"], c["a_log"], y_ssd,
                                      ones, ident)
                multiply_tiles(core, "z", y_ssd, zs)
                norm(core, "n10", y_ssd, y_ssd, ones, y_hg, c["ssd_norm_w"])
            with ExitStack() as r:
                hq, ff, fb, gs = bufs(nc, r, "b3", hq=[P, KT, T], ff=[P, KT, T], fb=[P, KT, T], gs=[P, KT, T])
                dests = (hq, ff, fb, y_hg, gs)

                def emit(i, b, bank):
                    return nc.scalar.activation(dests[i][:, b, :], bank[:], ACT.Silu if i == 4 else ACT.Identity)

                linear(core, "hin", w_in[:, 1024 + XBC + SSD_H:], 5, hT, ("scalar", emit))
                v_tm = hT[:].rearrange("p (t a) c -> p t (a c)", a=2)
                turn_out(core, y_hg, v_tm, ident)
                zero_tiles(core, y_hg)
                with ExitStack() as q:
                    (kh,) = bufs(nc, q, "b3", kh=[P, KT, T])
                    for d, f in enumerate((ff, fb)):
                        hgrn_gates(core, d, f, kh, lower)
                        hgrn_direction(core, d, hq, f, kh, c["total"], v_tm, y_hg, ident)
                hgrn_norm(core, y_hg, c["hg_norm_w"], gs, ones, hq)

            def add_gated(first):
                def emit(i, b, bank):
                    return nc.vector.scalar_tensor_tensor(out=xT[:, b, :], in0=bank[:],
                                                          scalar=mod[:, first + b:first + b + 1], in1=xT[:, b, :],
                                                          op0=ALU.mult, op1=ALU.add)
                return ("vector", emit)

            linear(core, "wo3", a["w_out_3"][0], 2, ycat, add_gated(16), stacked=True)
        with ExitStack() as s:
            (up,) = bufs(nc, s, "b3", up=[P, 32, T])
            norm(core, "n11", xT, hT, ones, up[:, 0:KT, :], c["gain2"], mod[:, 24:32])
            (squared,) = sems(nc, s, "up_squared")

            def emit(i, b, bank):
                return nc.scalar.activation(up[:, 8 * i + b, :], bank[:], ACT.Relu)

            def square(block, copied):
                @block.vector
                def _(dve):
                    for n in range(32):
                        dve.wait_ge(copied, n + 1)
                        nc.vector.tensor_tensor(up[:, n, :], up[:, n, :], up[:, n, :], ALU.mult).then_inc(squared, 1)

            linear(core, "up", a["w_up_3"][0], 4, hT, ("scalar", emit), more=square)
            linear(core, "down", a["w_down_3"][0], 4, up, add_gated(40), stacked=True)
        norm(core, "n12", xT, xT, ones, hT, c["final"])
        store_out(core, xT, ident, out)


def build(nc, a, out):
    USED.clear()
    with ExitStack() as ctx:
        core = Core(nc, ctx, a["consts"])
        xT, hT, ident, ones = bufs(nc, ctx, "all", xT=[P, KT, T], hT=[P, KT, T], ident=[P, P], ones=[P, P])
        load_x(core, a["x"][0], xT, ident, ones)
        first_block(core, a, xT, hT, ident, ones)
        second_block(core, a, xT, hT, ident, ones)
        third_block(core, a, xT, hT, ident, ones, out)




def kernel(**inputs):
    import numpy as _np
    import concourse.bacc as _bacc
    from concourse import mybir as _mybir
    from concourse.bass_utils import run_bass_kernel_spmd as _run

    nc = _bacc.Bacc("TRN2", target_bir_lowering=False, num_devices=1)
    arrays, args = {}, {}
    for name, value in inputs.items():
        v = _np.ascontiguousarray(value)
        arrays[f"in_{name}_dram"] = v
        args[name] = nc.dram_tensor(f"in_{name}_dram", v.shape, _mybir.dt.from_np(v.dtype), kind="ExternalInput").ap()
    consts = _np.concatenate([_np.asarray(c, _np.float32) for c in constant_parts().values()], axis=1)
    arrays["consts_dram"] = _np.ascontiguousarray(consts)
    args["consts"] = nc.dram_tensor("consts_dram", consts.shape, _mybir.dt.float32, kind="ExternalInput").ap()
    args["bias_dram"] = nc.dram_tensor("bias_by_distance", (DSA_H, 5 * P), _mybir.dt.float32, kind="Internal").ap()
    out = nc.dram_tensor("out_0_dram", (1, T, D), _mybir.dt.float32, kind="ExternalOutput").ap()
    build(nc, args, out)
    r = _run(nc, [arrays], core_ids=[0])
    return r.results[0]["out_0_dram"]
```

```python
import math
from contextlib import ExitStack

import numpy as np

import concourse.bass as bass
from concourse import mybir

ACT = mybir.ActivationFunctionType
ALU = mybir.AluOpType
AX = mybir.AxisListType.X
F32 = mybir.dt.float32
U32 = mybir.dt.uint32

P = 128
T = 512
D = 1024
KT = D // P
TT = T // P
EPS = 1e-6
LN_EPS = 1e-5

GLA_H, GLA_DK, GLA_DV, GLA_RANK, GLA_CHUNK = 4, 48, 96, 16, 64
DSA_H, DSA_DH, IDX_H, IDX_DIM = 6, 64, 4, 32
TOPK = min(256, T // 4)
BUCKETS, MAX_DIST = 32, 128
POOL_W = 256
WINDOWS = (2, 4, 8, 16)
NEG_HIDDEN = -3.0e38
NEG_TAKEN = -3.4e38

HALF = 512



def bucket_of(rel):
    rel = np.maximum(rel, 0)
    exact = BUCKETS // 2
    relf = np.maximum(rel, 1).astype(np.float32)
    large = exact + (np.log(relf / np.float32(exact)) / np.float32(math.log(MAX_DIST / exact))
                     * np.float32(BUCKETS - exact)).astype(np.int32)
    return np.where(rel < exact, rel, np.minimum(large, BUCKETS - 1))


def constant_parts():
    i = np.arange(P)
    row, col = i[:, None], i[None, :]
    t = np.arange(T)
    parts = {}
    parts["ident"] = (row == col)
    parts["flip"] = (row + col == P - 1)
    parts["gla_pairs"] = (row <= col) & (row // GLA_CHUNK == col // GLA_CHUNK)
    parts["hidden"] = -1.0 * (col > row)
    parts["upto"] = (row <= col)
    parts["from"] = (row >= col)
    parts["reset64"] = np.broadcast_to(t % 64 != 0, (P, T))
    parts["reset128"] = np.broadcast_to(t % 128 != 0, (P, T))
    w = np.repeat(np.array(WINDOWS), P // 2).reshape(2, P)
    parts["inv_count"] = np.concatenate([1.0 / np.minimum(t[None, :] + 1, w[k][:, None]) for k in range(2)], 1)
    u = np.arange(5 * P)
    onehot = np.zeros((P, 5 * P))
    onehot[:BUCKETS] = bucket_of(T - 1 - u)[None, :] == np.arange(BUCKETS)[:, None]
    parts["bucket"] = onehot
    parts["sgu_mask"] = (col // 64 >= row // 64)
    head = np.arange(P)
    parts["one_head"] = head[:, None] == np.arange(16).repeat(P)[None, :]
    parts["two_heads"] = head[:, None] == np.arange(16).repeat(P // 2)[None, :]
    levels = [(row // (2 * m) == col // (2 * m)) & (row // m % 2 == 0) & (col // m % 2 == 1)
              for m in (64, 32, 16, 8, 4, 2, 1)]
    parts["levels"] = np.concatenate(levels + [row == col], 1)
    parts["levels_back"] = np.concatenate([a.T for a in levels] + [row == col], 1)
    parts["slots"] = np.broadcast_to(i, (P, P))
    parts["numbers"] = np.broadcast_to(np.arange(16).repeat(32), (P, 512))
    parts["tokens"] = row + P * np.arange(TT)[None, :]
    parts["row_number"] = np.broadcast_to(P * np.arange(N_TABLE), (P, N_TABLE))
    return parts


def constant_layout():
    at, where = 0, {}
    for name, a in constant_parts().items():
        where[name] = (at, a.shape[1])
        at += a.shape[1]
    return where, at


class Count:

    def __init__(self, sem):
        self.sem, self.n = sem, 0

    def by(self, instruction):
        instruction.then_inc(self.sem, 1)
        self.n += 1
        return self.n


class Core:

    def __init__(self, nc, ctx, consts):
        self.nc, self.ctx, self.consts = nc, ctx, consts
        self.where, _ = constant_layout()
        self.bank = [ctx.enter_context(nc.psum_tensor(f"bank{i}", [P, 512], F32)) for i in range(8)]
        self.stage_n = 0

    def const(self, name, rows=P):
        at, n = self.where[name]
        return self.consts[0:rows, at:at + n]


def clear_used(nc, used):
    used.sort()
    while used:
        n = 1
        while n < len(used) and used[n] == used[0] + n:
            n += 1
        nc.gpsimd.sem_clear(range(used[0], used[0] + n))
        del used[:n]
    nc.all_engine_barrier()


USED = []


def sems(nc, ctx, *names):
    if len(USED) > 80:
        clear_used(nc, USED)
    out = [ctx.enter_context(nc.semaphore(n)) for n in names]
    assert not {s.num for s in out} & set(USED)
    ctx.callback(USED.extend, [s.num for s in out])
    return out


def bufs(nc, ctx, prefix, **shapes):
    out = []
    for name, shape in shapes.items():
        out.append(ctx.enter_context(nc.sbuf_tensor(f"{prefix}_{name}", list(shape), F32)))
    return out


def columns(vector, n=P):
    return vector.rearrange("(t p) -> p t", p=n)


class Modulation:

    SLOTS = 3
    PIECES = 12

    def __init__(self, core, ctx, name, w, cond, out, bank):
        nc = core.nc
        self.nc, self.cond, self.out, self.bank = nc, cond, out, bank
        self.w_v = w.rearrange("(k p) n -> p k n", p=P)
        (self.wt,) = bufs(nc, ctx, name, w=[P, self.SLOTS, KT, HALF])
        self.loaded = sems(nc, ctx, *(f"{name}_loaded{s}" for s in range(self.SLOTS)))
        self.product, self.copied, self.activated = sems(nc, ctx, f"{name}_product", f"{name}_copied",
                                                         f"{name}_activated")

    def load(self, sp):
        for c in range(self.PIECES):
            if c >= self.SLOTS:
                sp.wait_ge(self.product, c - self.SLOTS + 1)
            s = c % self.SLOTS
            sp.dma_start(self.wt[:, s], self.w_v[:, :, c * HALF:(c + 1) * HALF]).then_inc(self.loaded[s], 16)

    def activate(self, act):
        self.nc.scalar.activation(self.cond[:], self.cond[:], ACT.Silu).then_inc(self.activated, 1)

    def multiply(self, pe, c):
        s = c % self.SLOTS
        pe.wait_ge(self.activated, 1)
        pe.wait_ge(self.loaded[s], 16 * (c // self.SLOTS + 1))
        if c:
            pe.wait_ge(self.copied, c)
        for m in range(4):
            for k in range(KT):
                mm = self.nc.tensor.matmul(self.bank[:, m:m + 1], self.wt[:, s, k, m * P:(m + 1) * P],
                                           self.cond[:, k:k + 1], start=(k == 0), stop=(k == KT - 1))
        mm.then_inc(self.product, 1)

    def copy(self, act, c):
        act.wait_ge(self.product, c + 1)
        self.nc.scalar.copy(self.out[:, 4 * c:4 * c + 4], self.bank[:, 0:4]).then_inc(self.copied, 1)


def bcast_rows(row, n=P):
    return row.to_broadcast([n, row.shape[1]])


def load_x(core, x, xT, ident, ones):
    nc = core.nc
    with ExitStack() as ctx:
        (rows,) = bufs(nc, ctx, "lx", rows=[P, TT, D])
        loaded, turned, copied, ones_set = sems(nc, ctx, "lx_loaded", "lx_turned", "lx_copied", "lx_ones")
        block = ctx.enter_context(nc.Block())

        @block.sync
        def _(sp):
            sp.dma_start(ident[:], core.const("ident")).then_inc(loaded, 16)
            sp.dma_start(rows[:], x.rearrange("(t p) d -> p t d", p=P)).then_inc(loaded, 16)

        @block.gpsimd
        def _(pool):
            nc.gpsimd.memset(ones[:], 1.0).then_inc(ones_set, 1)

        @block.tensor
        def _(pe):
            pe.wait_ge(loaded, 32)
            for k in range(KT):
                for t in range(TT):
                    mm = nc.tensor.transpose(core.bank[k][:, t * P:(t + 1) * P],
                                             rows[:, t, k * P:(k + 1) * P], ident[:])
                mm.then_inc(turned, 1)

        @block.scalar
        def _(act):
            for k in range(KT):
                act.wait_ge(turned, k + 1)
                nc.scalar.copy(xT[:, k, :], core.bank[k][:]).then_inc(copied, 1)


def norm(core, name, src, dst, ones, scratch, gain, bias=None, centre=False, func=None, eps=EPS):
    nc = core.nc
    func = func or ACT.Identity
    mean_ps, square_ps = core.bank[0], core.bank[1]
    with ExitStack() as ctx:
        part, rstd, eps_col = bufs(nc, ctx, name, part=[P, T], rstd=[P, T], eps=[P, 1])
        eps_set, part_ready, sum_ready, centred, squared, std_ready, inv_ready, normed, done = sems(
            nc, ctx, *(f"{name}_{s}" for s in ("eps", "part", "sum", "centred", "squared", "std", "inv",
                                               "normed", "done")))
        block = ctx.enter_context(nc.Block())
        middle = dst if centre else src

        @block.gpsimd
        def _(pool):
            nc.gpsimd.memset(eps_col[:], eps).then_inc(eps_set, 1)

        @block.tensor
        def _(pe):
            if centre:
                pe.wait_ge(part_ready, 1)
                nc.tensor.matmul(mean_ps[:], ones[:], part[:], start=True, stop=True).then_inc(sum_ready, 1)
            pe.wait_ge(part_ready, 1 + centre)
            nc.tensor.matmul(square_ps[:], ones[:], part[:], start=True, stop=True).then_inc(sum_ready, 1)

        @block.vector
        def _(dve):
            if centre:
                nc.vector.reduce_sum(part[:], src[:].rearrange("p k t -> p t k"), AX).then_inc(part_ready, 1)
                dve.wait_ge(sum_ready, 1)
                for k in range(KT):
                    nc.vector.scalar_tensor_tensor(out=dst[:, k, :], in0=mean_ps[:], scalar=-1.0 / D,
                                                   in1=src[:, k, :], op0=ALU.mult,
                                                   op1=ALU.add).then_inc(centred, 1)
            dve.wait_ge(squared, KT)
            nc.vector.reduce_sum(part[:], scratch[:].rearrange("p k t -> p t k"), AX).then_inc(part_ready, 1)
            dve.wait_ge(std_ready, 1)
            nc.vector.reciprocal(rstd[:], rstd[:]).then_inc(inv_ready, 1)
            dve.wait_ge(inv_ready, 1)
            for k in range(KT):
                nc.vector.tensor_tensor(scratch[:, k, :], middle[:, k, :], rstd[:],
                                        ALU.mult).then_inc(normed, 1)

        @block.scalar
        def _(act):
            for k in range(KT):
                if centre:
                    act.wait_ge(centred, k + 1)
                nc.scalar.activation(scratch[:, k, :], middle[:, k, :], ACT.Square).then_inc(squared, 1)
            act.wait_ge(eps_set, 1)
            act.wait_ge(sum_ready, 1 + centre)
            nc.scalar.activation(rstd[:], square_ps[:], ACT.Sqrt, bias=eps_col[:],
                                 scale=1.0 / D).then_inc(std_ready, 1)
            for k in range(KT):
                act.wait_ge(normed, k + 1)
                nc.scalar.activation(dst[:, k, :], scratch[:, k, :], func, scale=gain[:, k:k + 1],
                                     bias=0.0 if bias is None else bias[:, k:k + 1]).then_inc(done, 1)


OFF = {}
_at = 0
for _n, _w in (("gq", 192), ("gk", 192), ("gv", 384), ("gz", 16), ("ggate", 384), ("dq", 384), ("dk", 384),
               ("dv", 384), ("dgate", 384), ("qi", 128), ("ki", 32), ("wi", 4), ("pu", 256), ("pgate", 256)):
    OFF[_n] = _at
    _at += _w
IN_COLS = _at


def projection(core, hT, w_in, to):
    nc = core.nc
    chunks = []

    def chunk(names, tiles):
        first = OFF[names[0]]
        last = names[-1]
        width = {"gk": 192, "gv": 384, "ggate": 384, "dq": 384, "dk": 384, "dv": 384, "dgate": 384,
                 "wi": 4, "pgate": 256}[last]
        chunks.append((first, OFF[last] + width - first, tiles))

    gq, gk = to["gq"], to["gk"]
    chunk(["gq", "gk"], [("c", h * GLA_DK, GLA_DK, gq[:, h, :], ACT.Identity) for h in range(GLA_H)]
          + [("c", 192 + h * GLA_DK, GLA_DK, gk[:, h, :], ACT.Identity) for h in range(GLA_H)])
    chunk(["gv"], [("t", 0, 384, to["gv"][:, t, :], t) for t in range(TT)])
    chunk(["dq"], [("c", k * P, P, to["dq"][:, k, :], ACT.Identity) for k in range(3)])
    chunk(["dk"], [("c", k * P, P, to["dk"][:, k, :], ACT.Identity) for k in range(3)])
    chunk(["dv"], [("t", 0, 384, to["dv"][:, t, :], t) for t in range(TT)])
    chunk(["qi", "ki", "wi"], [("c", 0, P, to["qi"][:], ACT.Identity), ("r", P, P, to["ki"][:], ACT.Identity)]
          + [("t", 160, IDX_H, to["wi"][:, t, :], t) for t in range(TT)])
    chunk(["pu", "pgate"], [("c", k * P, P, to["pu"][:, k, :], ACT.Identity) for k in range(2)]
          + [("c", POOL_W + k * P, P, to["pgate"][:, k, :], ACT.Silu) for k in range(2)])
    chunk(["gz", "ggate"], [("c", 0, GLA_RANK, to["gz"][:], ACT.Identity)]
          + [("c", GLA_RANK + h * GLA_DV, GLA_DV, to["ggate"][:, h, :], ACT.Silu) for h in range(GLA_H)])
    chunk(["dgate"], [("c", k * P, P, to["dgate"][:, k, :], ACT.Silu) for k in range(3)])
    tiles_before = [sum(len(c[2]) for c in chunks[:i]) for i in range(len(chunks) + 1)]
    SLOTS = 3
    w_v = w_in.rearrange("(k p) n -> p k n", p=P)
    with ExitStack() as ctx:
        w, ki4 = bufs(nc, ctx, "proj", w=[P, SLOTS, KT, 512], ki4=[P, KT, P])
        loaded = sems(nc, ctx, *(f"proj_loaded{s}" for s in range(SLOTS)))
        product, copied, repeated = sems(nc, ctx, "proj_product", "proj_copied", "proj_repeated")
        block = ctx.enter_context(nc.Block())

        @block.sync
        def _(sp):
            for c, (first, width, _) in enumerate(chunks):
                if c >= SLOTS:
                    sp.wait_ge(product, tiles_before[c - SLOTS + 1])
                sp.dma_start(w[:, c % SLOTS, :, 0:width],
                             w_v[:, :, first:first + width]).then_inc(loaded[c % SLOTS], 16)

        @block.vector
        def _(dve):
            c = 5
            dve.wait_ge(loaded[c % SLOTS], 16 * (c // SLOTS + 1))
            for j in range(IDX_H):
                nc.vector.tensor_copy(ki4[:, :, j * IDX_DIM:(j + 1) * IDX_DIM],
                                      w[:, c % SLOTS, :, P:P + IDX_DIM]).then_inc(repeated, 1)

        @block.tensor
        def _(pe):
            n = 0
            for c, (_, _, tiles) in enumerate(chunks):
                pe.wait_ge(loaded[c % SLOTS], 16 * (c // SLOTS + 1))
                for layout, at, width, _, extra in tiles:
                    if n >= 8:
                        pe.wait_ge(copied, n - 7)
                    if layout == "r":
                        pe.wait_ge(repeated, IDX_H)
                    bank = core.bank[n % 8]
                    for k in range(KT):
                        weight = w[:, c % SLOTS, k, at:at + width]
                        if layout == "t":
                            out, left, right = bank[:, 0:width], hT[:, k, extra * P:(extra + 1) * P], weight
                        else:
                            out, right = bank[0:width, :], hT[:, k, :]
                            left = weight if layout == "c" else ki4[:, k, :]
                        mm = nc.tensor.matmul(out, left, right, start=(k == 0), stop=(k == KT - 1))
                    mm.then_inc(product, 1)
                    n += 1

        @block.scalar
        def _(act):
            n = 0
            for _, _, tiles in chunks:
                for layout, _, width, out, extra in tiles:
                    act.wait_ge(product, n + 1)
                    bank = core.bank[n % 8]
                    if layout == "t":
                        nc.scalar.activation(out, bank[:, 0:width], ACT.Identity).then_inc(copied, 1)
                    else:
                        nc.scalar.activation(out, bank[0:width, :], extra).then_inc(copied, 1)
                    n += 1


def gla(core, to, ones, ident, gate_w2, gate_b, norm_g, y):
    nc = core.nc
    B = core.bank
    CH = T // GLA_CHUNK
    C = GLA_CHUNK
    gq, gk, gv, gz, gate = (to[n] for n in ("gq", "gk", "gv", "gz", "ggate"))
    with ExitStack() as ctx:
        w2, gb, ng, mask, reset, eps_col, z, lsig, b, e, ke, kd, kdT, S, AT = bufs(
            nc, ctx, "gla", w2=[GLA_RANK, 192], gb=[GLA_DK, GLA_H], ng=[GLA_DV, 1], mask=[P, P],
            reset=[GLA_DK, GLA_H, T], eps=[P, 1], z=[GLA_DV, GLA_H, T], lsig=[GLA_DK, GLA_H, T],
            b=[GLA_DK, GLA_H, T], e=[GLA_DK, GLA_H, T], ke=[GLA_DK, GLA_H, T],
            kd=[GLA_DK, GLA_H, T], kdT=[P, GLA_H, TT, GLA_DK], S=[GLA_DK, GLA_H, CH, GLA_DV],
            AT=[P, GLA_H, T])
        qe = gq
        sq, z = z, z[0:GLA_DK]
        loaded, zeroed, pe_done, act_done, dve_done, chained = sems(
            nc, ctx, "gla_loaded", "gla_zeroed", "gla_product", "gla_scalar", "gla_vector", "gla_state")
        block = ctx.enter_context(nc.Block())
        bc = b[:].rearrange("p h (c t) -> p (h c) t", t=C)

        @block.sync
        def _(sp):
            sp.dma_start(w2[:], gate_w2).then_inc(loaded, 16)
            with nc.allow_non_contiguous_dma("a few columns"):
                sp.dma_start(gb[:], columns(gate_b, GLA_DK)).then_inc(loaded, 16)
                sp.dma_start(ng[:], columns(norm_g, GLA_DV)).then_inc(loaded, 16)
            sp.dma_start(mask[:], core.const("gla_pairs")).then_inc(loaded, 16)
            for h in range(GLA_H):
                sp.dma_start(reset[:, h, :], core.const("reset64", GLA_DK)).then_inc(loaded, 16)

        @block.gpsimd
        def _(pool):
            nc.gpsimd.memset(S[:, :, 0, :], 0.0).then_inc(zeroed, 1)
            nc.gpsimd.memset(eps_col[:], EPS).then_inc(zeroed, 1)

        PE_GATE, PE_TURN, PE_U, PE_A, PE_O, PE_NORM = 4, 8, 12, 16, 20, 24

        @block.tensor
        def _(pe):
            pe.wait_ge(loaded, 16 * 8)
            for h in range(GLA_H):
                nc.tensor.matmul(B[h][0:GLA_DK, :], w2[:, h * GLA_DK:(h + 1) * GLA_DK], gz[:],
                                 start=True, stop=True).then_inc(pe_done, 1)
            pe.wait_ge(dve_done, 5)
            for h in range(GLA_H):
                for t in range(TT):
                    mm = nc.tensor.transpose(B[4 + h][:, t * GLA_DK:(t + 1) * GLA_DK],
                                             kd[:, h, t * P:(t + 1) * P], ident[0:GLA_DK, 0:GLA_DK])
                mm.then_inc(pe_done, 1)
            for h in range(GLA_H):
                pe.wait_ge(dve_done, 9)
                for c in range(CH):
                    lo = C * (c % 2)
                    mm = nc.tensor.matmul(B[2 * h + c % 2][0:GLA_DK, (c // 2) * GLA_DV:(c // 2 + 1) * GLA_DV],
                                          kdT[lo:lo + C, h, c // 2, :],
                                          gv[lo:lo + C, c // 2, h * GLA_DV:(h + 1) * GLA_DV],
                                          start=True, stop=True)
                mm.then_inc(pe_done, 1)
            pe.wait_ge(chained, GLA_H * (CH - 1))
            for h in range(GLA_H):
                for t in range(TT):
                    cols = slice(t * P, (t + 1) * P)
                    mm = nc.tensor.matmul(B[h][:, cols], ke[:, h, cols], qe[:, h, cols], start=True, stop=True)
                mm.then_inc(pe_done, 1)
            for h in range(GLA_H):
                pe.wait_ge(dve_done, 10 + h)
                for c in range(CH):
                    cc = slice(c * C, (c + 1) * C)
                    nc.tensor.matmul(B[4 + h][0:GLA_DV, cc], gv[:, c // 2, h * GLA_DV:(h + 1) * GLA_DV],
                                     AT[:, h, cc], start=True, stop=False)
                    mm = nc.tensor.matmul(B[4 + h][0:GLA_DV, cc], S[:, h, c, :], qe[:, h, cc],
                                          start=False, stop=True)
                mm.then_inc(pe_done, 1)
            for h in range(GLA_H):
                pe.wait_ge(act_done, 11 + h)
                nc.tensor.matmul(B[h][0:GLA_DV, :], ones[0:GLA_DV, 0:GLA_DV], sq[:, h, :],
                                 start=True, stop=True).then_inc(pe_done, 1)

        @block.scalar
        def _(act):
            for h in range(GLA_H):
                act.wait_ge(loaded, 16 * 8)
                act.wait_ge(pe_done, h + 1)
                nc.scalar.activation(z[:, h, :], B[h][0:GLA_DK, :], ACT.Identity,
                                     bias=gb[:, h:h + 1]).then_inc(act_done, 1)
            act.wait_ge(act_done, 4)
            nc.scalar.activation(lsig[:], z[:], ACT.Abs).then_inc(act_done, 1)
            act.wait_ge(act_done, 5)
            nc.scalar.activation(lsig[:], lsig[:], ACT.Exp, scale=-1.0).then_inc(act_done, 1)
            act.wait_ge(act_done, 6)
            nc.scalar.activation(lsig[:], lsig[:], ACT.Ln, bias=1.0).then_inc(act_done, 1)
            act.wait_ge(dve_done, 2)
            nc.scalar.activation(e[:], b[:], ACT.Exp, scale=1 / 16).then_inc(act_done, 1)
            nc.scalar.activation(z[:], b[:], ACT.Exp, scale=-1 / 16).then_inc(act_done, 1)
            act.wait_ge(dve_done, 3)
            nc.scalar.activation(lsig[:], kd[:], ACT.Exp, scale=1 / 16).then_inc(act_done, 1)
            for h in range(GLA_H):
                act.wait_ge(pe_done, PE_A + 1 + h)
                nc.scalar.activation(sq[:, h, :], B[4 + h][0:GLA_DV, :], ACT.Square).then_inc(act_done, 1)
            act.wait_ge(zeroed, 2)
            for h in range(GLA_H):
                act.wait_ge(pe_done, PE_O + 1 + h)
                nc.scalar.activation(sq[:, h, :], B[h][0:GLA_DV, :], ACT.Sqrt, bias=eps_col[0:GLA_DV, :],
                                     scale=1.0 / GLA_DV).then_inc(act_done, 1)

        @block.vector
        def _(dve):
            dve.wait_ge(act_done, 7)
            nc.vector.scalar_tensor_tensor(out=lsig[:], in0=z[:], scalar=0.0, in1=lsig[:], op0=ALU.min,
                                           op1=ALU.subtract).then_inc(dve_done, 1)
            dve.wait_ge(dve_done, 1)
            dve.wait_ge(loaded, 16 * 8)
            flat = "p h t -> p (h t)"
            nc.vector.tensor_tensor_scan(b[:].rearrange(flat), reset[:].rearrange(flat),
                                         lsig[:].rearrange(flat), 0.0, ALU.mult, ALU.add).then_inc(dve_done, 1)
            dve.wait_ge(dve_done, 2)
            nc.vector.tensor_tensor(kd[:].rearrange("p h (c t) -> p (h c) t", t=C),
                                    bc[:, :, C - 1:C].to_broadcast([GLA_DK, GLA_H * CH, C]), bc,
                                    ALU.subtract).then_inc(dve_done, 1)
            dve.wait_ge(act_done, 9)
            nc.vector.scalar_tensor_tensor(out=qe[:], in0=gq[:], scalar=GLA_DK ** -0.5, in1=e[:],
                                           op0=ALU.mult, op1=ALU.mult)
            nc.vector.tensor_tensor(ke[:], gk[:], z[:], ALU.mult).then_inc(dve_done, 1)
            dve.wait_ge(act_done, 10)
            nc.vector.tensor_tensor(kd[:], gk[:], lsig[:], ALU.mult).then_inc(dve_done, 1)
            for h in range(GLA_H):
                dve.wait_ge(pe_done, PE_GATE + 1 + h)
                nc.vector.tensor_copy(kdT[:, h, :, :].rearrange("p t k -> p (t k)"),
                                      B[4 + h][:, 0:TT * GLA_DK]).then_inc(dve_done, 1)
            dve.wait_ge(zeroed, 1)
            for c in range(CH - 1):
                for h in range(GLA_H):
                    dve.wait_ge(pe_done, PE_TURN + 1 + h)
                    if c:
                        dve.wait_ge(chained, GLA_H * (c - 1) + h + 1)
                    at = (c // 2) * GLA_DV
                    nc.vector.scalar_tensor_tensor(
                        out=S[:, h, c + 1, :], in0=S[:, h, c, :], scalar=e[:, h, c * C + C - 1:c * C + C],
                        in1=B[2 * h + c % 2][0:GLA_DK, at:at + GLA_DV], op0=ALU.mult,
                        op1=ALU.add).then_inc(chained, 1)
            for h in range(GLA_H):
                dve.wait_ge(pe_done, PE_U + 1 + h)
                nc.vector.tensor_tensor(AT[:, h, :].rearrange("p (t q) -> p t q", q=P),
                                        B[h][:].rearrange("p (t q) -> p t q", q=P),
                                        mask[:].unsqueeze(1).to_broadcast([P, TT, P]),
                                        ALU.mult).then_inc(dve_done, 1)
            dve.wait_ge(act_done, 18)
            nc.vector.reciprocal(sq[:], sq[:]).then_inc(dve_done, 1)
            dve.wait_ge(dve_done, 14)
            for h in range(GLA_H):
                nc.vector.tensor_tensor(y[:, h, :], B[4 + h][0:GLA_DV, :], sq[:, h, :],
                                        ALU.mult).then_inc(dve_done, 1)
            dve.wait_ge(dve_done, 18)
            nc.vector.scalar_tensor_tensor(out=y[:], in0=y[:], scalar=ng[:], in1=gate[:], op0=ALU.mult,
                                           op1=ALU.mult).then_inc(dve_done, 1)


def dsa_select(core, to, ident, pick, w_mod, cond, mod):
    nc = core.nc
    B = core.bank
    qi, ki, wi = to["qi"], to["ki"], to["wi"]
    with ExitStack() as ctx:
        hidden, rl, wh, score, top = bufs(nc, ctx, "sel", hidden=[P, P], rl=[P, 2, IDX_H, T],
                                          wh=[P, TT, IDX_H], score=[P, TT, T], top=[P, 8])
        loaded, dots, relued, weighed, step = sems(nc, ctx, "sel_loaded", "sel_dots", "sel_relued",
                                                   "sel_weighed", "sel_step")
        beside = Modulation(core, ctx, "sel_mod", w_mod, cond, mod, B[0])
        block = ctx.enter_context(nc.Block())

        @block.sync
        def _(sp):
            sp.dma_start(hidden[:], core.const("hidden")).then_inc(loaded, 16)
            beside.load(sp)

        @block.tensor
        def _(pe):
            for t in range(TT):
                n = P * (t + 1)
                for j in range(IDX_H):
                    if t >= 2:
                        pe.wait_ge(relued, IDX_H * (t - 2) + j + 1)
                    rows = slice(j * IDX_DIM, (j + 1) * IDX_DIM)
                    nc.tensor.matmul(B[(IDX_H * t + j) % 8][:, 0:n], qi[rows, t * P:(t + 1) * P],
                                     ki[rows, 0:n], start=True, stop=True).then_inc(dots, 1)
            pe.wait_ge(relued, IDX_H * (TT - 2) + 1)
            for c in range(Modulation.PIECES):
                beside.multiply(pe, c)

        @block.scalar
        def _(act):
            for t in range(TT):
                n = P * (t + 1)
                for j in range(IDX_H):
                    act.wait_ge(dots, IDX_H * t + j + 1)
                    if t >= 2:
                        act.wait_ge(weighed, t - 1)
                    nc.scalar.activation(rl[:, t % 2, j, 0:n], B[(IDX_H * t + j) % 8][:, 0:n], ACT.Relu,
                                         scale=IDX_DIM ** -0.5).then_inc(relued, 1)
            beside.activate(act)
            for c in range(Modulation.PIECES):
                beside.copy(act, c)

        @block.vector
        def _(dve):
            steps = Count(step)

            def after(instruction):
                dve.wait_ge(step, steps.by(instruction))

            after(nc.vector.tensor_scalar(wh[:], wi[:], IDX_H ** -0.5, None, ALU.mult))
            dve.wait_ge(loaded, 16)
            for t in range(TT):
                n = P * (t + 1)
                dve.wait_ge(relued, IDX_H * (t + 1))
                s = score[:, t, 0:n]
                after(nc.vector.tensor_scalar(s, rl[:, t % 2, 0, 0:n], wh[:, t, 0:1], None, ALU.mult))
                for j in range(1, IDX_H):
                    last = nc.vector.scalar_tensor_tensor(out=s, in0=rl[:, t % 2, j, 0:n],
                                                          scalar=wh[:, t, j:j + 1], in1=s, op0=ALU.mult,
                                                          op1=ALU.add)
                    if j < IDX_H - 1:
                        after(last)
                last.then_inc(weighed, 1)
                dve.wait_ge(weighed, t + 1)
                diag = score[:, t, t * P:n]
                after(nc.vector.scalar_tensor_tensor(out=diag, in0=hidden[:], scalar=-NEG_HIDDEN, in1=diag,
                                                     op0=ALU.mult, op1=ALU.add))
                if t == 0:
                    nc.vector.tensor_copy(pick[:, 0, 0:P], hidden[:])
                    continue
                for _ in range(TOPK // 8):
                    after(nc.vector.max(top[:], s))
                    after(nc.vector.match_replace(s, top[:], s, NEG_TAKEN))
                after(nc.vector.tensor_scalar(pick[:, t, 0:n], s, NEG_TAKEN, 1.0, ALU.is_equal, ALU.subtract))


def dsa_attend(core, to, ident, rel_bias, bias_dram, pick, y, w_mod, cond, mod):
    nc = core.nc
    B = core.bank
    dq, dk, dv, gate = (to[n] for n in ("dq", "dk", "dv", "dgate"))
    units = [(t, h) for t in range(TT) for h in range(DSA_H)]
    N = len(units)
    U = 5 * P
    with ExitStack() as ctx:
        rb, onehot, by_distance, bias, L, pr, prT, peak, total, flip = bufs(
            nc, ctx, "att", rb=[BUCKETS, DSA_H], onehot=[BUCKETS, U], by_distance=[DSA_H, U],
            bias=[P, DSA_H, T], L=[P, 2, T], pr=[P, 2, T], prT=[P, 2, T], peak=[P, 2], total=[P, 2], flip=[P, P])
        (loaded, table, table_copied, stored, windows, logits, peaked, exped, weights, turned, turned_copied,
         attended, step, gated, flipped, flip_copied) = sems(
            nc, ctx, *(f"att_{s}" for s in ("loaded", "table", "table_copied", "stored", "windows", "logits",
                                            "peaked", "exped", "weights", "turned", "turned_copied",
                                            "attended", "step", "gated", "flipped",
                                            "flip_copied")))
        beside = Modulation(core, ctx, "att_mod", w_mod, cond, mod, B[7])
        block = ctx.enter_context(nc.Block())

        @block.sync
        def _(sp):
            sp.dma_start(rb[:], rel_bias).then_inc(loaded, 16)
            sp.dma_start(onehot[:], core.const("bucket", BUCKETS)).then_inc(loaded, 16)
            sp.wait_ge(table_copied, 2)
            sp.dma_start(bias_dram, by_distance[:]).then_inc(stored, 16)
            sp.wait_ge(stored, 16)
            for h in range(DSA_H):
                window = bass.AP(tensor=bias_dram.tensor, offset=h * U, ap=[[1, P], [1, T]])
                sp.dma_start(bias[:, h, :], window).then_inc(windows, 16)
            sp.dma_start(flip[:], core.const("flip")).then_inc(windows, 16)
            beside.load(sp)

        @block.tensor
        def _(pe):
            pe.wait_ge(loaded, 32)
            nc.tensor.matmul(B[6][0:DSA_H, :], rb[:], onehot[:, 0:512], start=True, stop=True).then_inc(table, 1)
            nc.tensor.matmul(B[7][0:DSA_H, 0:U - 512], rb[:], onehot[:, 512:U], start=True,
                             stop=True).then_inc(table, 1)
            pe.wait_ge(windows, 16 * (DSA_H + 1))
            pe.wait_ge(table_copied, 2)
            for h in range(DSA_H):
                nc.tensor.matmul(B[2 + h][:], flip[:], bias[:, h, :], start=True, stop=True).then_inc(flipped, 1)
            pe.wait_ge(flip_copied, DSA_H)
            for i in range(N + 1):
                if i < N:
                    t, h = units[i]
                    n = P * (t + 1)
                    rows = slice(DSA_DH * (h % 2), DSA_DH * (h % 2) + DSA_DH)
                    if i >= 2:
                        pe.wait_ge(peaked, i - 1)
                    nc.tensor.matmul(B[i % 2][:, 0:n], dq[rows, h // 2, t * P:(t + 1) * P],
                                     dk[rows, h // 2, 0:n], start=True, stop=True).then_inc(logits, 1)
                if i >= 1:
                    j = i - 1
                    t, h = units[j]
                    pe.wait_ge(weights, j + 1)
                    if j >= 2:
                        pe.wait_ge(turned_copied, j - 1)
                    for s in range(t + 1):
                        mm = nc.tensor.transpose(B[2 + j % 2][:, s * P:(s + 1) * P],
                                                 pr[:, j % 2, s * P:(s + 1) * P], ident[:])
                    mm.then_inc(turned, 1)
                    pe.wait_ge(turned_copied, j + 1)
                    rows = slice(DSA_DH * (h % 2), DSA_DH * (h % 2) + DSA_DH)
                    for s in range(t + 1):
                        mm = nc.tensor.matmul(B[4 + h // 2][rows, t * P:(t + 1) * P],
                                              dv[:, s, h * DSA_DH:(h + 1) * DSA_DH],
                                              prT[:, j % 2, s * P:(s + 1) * P], start=(s == 0), stop=(s == t),
                                              skip_group_check=True)
                    mm.then_inc(attended, 1)
                    if j % 2:
                        beside.multiply(pe, j // 2)

        @block.vector
        def _(dve):
            steps = Count(step)

            def after(instruction):
                dve.wait_ge(step, steps.by(instruction))

            for i in range(2):
                dve.wait_ge(table, i + 1)
                cols = slice(0, 512) if i == 0 else slice(512, U)
                nc.vector.tensor_copy(by_distance[:, cols],
                                      B[6 + i][0:DSA_H, 0:cols.stop - cols.start]).then_inc(table_copied, 1)
            for h in range(DSA_H):
                dve.wait_ge(flipped, h + 1)
                nc.vector.tensor_copy(bias[:, h, :], B[2 + h][:]).then_inc(flip_copied, 1)
            dve.wait_ge(flip_copied, DSA_H)
            for i in range(N + 1):
                if i < N:
                    t, h = units[i]
                    n = P * (t + 1)
                    x = L[:, i % 2, 0:n]
                    dve.wait_ge(logits, i + 1)
                    if i >= 2:
                        dve.wait_ge(exped, i - 1)
                    after(nc.vector.scalar_tensor_tensor(out=x, in0=B[i % 2][:, 0:n], scalar=DSA_DH ** -0.5,
                                                         in1=bias[:, h, T - n:T], op0=ALU.mult, op1=ALU.add))
                    after(nc.vector.scalar_tensor_tensor(out=x, in0=pick[:, t, 0:n], scalar=1e30, in1=x,
                                                         op0=ALU.mult, op1=ALU.add))
                    after(nc.vector.reduce_max(peak[:, i % 2:i % 2 + 1], x, AX))
                    nc.vector.tensor_scalar(peak[:, i % 2:i % 2 + 1], peak[:, i % 2:i % 2 + 1], -1.0, None,
                                            ALU.mult).then_inc(peaked, 1)
                if i >= 1:
                    j = i - 1
                    n = P * (units[j][0] + 1)
                    dve.wait_ge(exped, j + 1)
                    after(nc.vector.reciprocal(total[:, j % 2:j % 2 + 1], total[:, j % 2:j % 2 + 1]))
                    nc.vector.tensor_scalar(pr[:, j % 2, 0:n], pr[:, j % 2, 0:n], total[:, j % 2:j % 2 + 1],
                                            None, ALU.mult).then_inc(weights, 1)
            for k in range(3):
                dve.wait_ge(attended, N)
                nc.vector.tensor_tensor(y[:, k, :], B[4 + k][:], gate[:, k, :], ALU.mult).then_inc(gated, 1)

        @block.scalar
        def _(act):
            beside.activate(act)
            for i in range(N + 1):
                if i >= 3 and i % 2:
                    beside.copy(act, (i - 3) // 2)
                if i < N:
                    n = P * (units[i][0] + 1)
                    act.wait_ge(peaked, i + 1)
                    if i >= 2:
                        act.wait_ge(turned, i - 1)
                    nc.scalar.activation(pr[:, i % 2, 0:n], L[:, i % 2, 0:n], ACT.Exp, bias=peak[:, i % 2:i % 2 + 1],
                                         accum_out=total[:, i % 2:i % 2 + 1]).then_inc(exped, 1)
                if i >= 1:
                    j = i - 1
                    n = P * (units[j][0] + 1)
                    act.wait_ge(turned, j + 1)
                    if j >= 2:
                        act.wait_ge(attended, j - 1)
                    nc.scalar.copy(prT[:, j % 2, 0:n], B[2 + j % 2][:, 0:n]).then_inc(turned_copied, 1)
            beside.copy(act, Modulation.PIECES - 1)


def pool_mix(core, to, pool_w, pool_scale, y):
    nc = core.nc
    B = core.bank
    pu, gate = to["pu"], to["pgate"]
    PAD = max(WINDOWS)
    with ExitStack() as ctx:
        inv, w, sc, a, b = bufs(nc, ctx, "pool", inv=[P, 2, T], w=[P, 2, 64], sc=[P, 2], a=[P, 2, PAD + T],
                                b=[P, 2, PAD + T])
        loaded, step, pooled, mixed, scaled = sems(nc, ctx, "pool_loaded", "pool_step", "pool_pooled",
                                                   "pool_mixed", "pool_scaled")
        block = ctx.enter_context(nc.Block())

        @block.sync
        def _(sp):
            sp.dma_start(inv[:].rearrange("p k t -> p (k t)"), core.const("inv_count")).then_inc(loaded, 16)
            sp.dma_start(w[:], pool_w.rearrange("(k g) c d -> (g c) k d", g=2)).then_inc(loaded, 16)
            with nc.allow_non_contiguous_dma("two columns"):
                sp.dma_start(sc[:], columns(pool_scale)).then_inc(loaded, 16)

        @block.vector
        def _(dve):
            steps = Count(step)

            def after(instruction):
                dve.wait_ge(step, steps.by(instruction))

            nc.vector.memset(b[:, :, 0:PAD], 0.0)
            nc.vector.memset(a[:, :, 0:PAD], 0.0)
            after(nc.vector.tensor_copy(a[:, :, PAD:], pu[:]))
            src, dst = a, b
            for k, window in enumerate(WINDOWS):
                tile, row = k // 2, 64 * (k % 2)
                half = window // 2
                after(nc.vector.tensor_tensor(dst[:, :, PAD:], src[:, :, PAD:],
                                              src[:, :, PAD - half:PAD + T - half], ALU.add))
                after(nc.vector.tensor_copy(y[row:row + 64, tile, :], dst[row:row + 64, tile, PAD:]))
                src, dst = dst, src
            dve.wait_ge(loaded, 48)
            after(nc.vector.tensor_tensor(y[:], y[:], inv[:], ALU.mult))
            nc.vector.tensor_tensor(y[:], y[:], pu[:], ALU.subtract).then_inc(pooled, 1)
            for tile in range(2):
                dve.wait_ge(mixed, 4)
                nc.vector.scalar_tensor_tensor(out=y[:, tile, :], in0=B[tile][:], scalar=sc[:, tile:tile + 1],
                                               in1=gate[:, tile, :], op0=ALU.mult,
                                               op1=ALU.mult).then_inc(scaled, 1)

        @block.tensor
        def _(pe):
            pe.wait_ge(loaded, 48)
            pe.wait_ge(pooled, 1)
            for g in range(4):
                rows = slice(64 * (g % 2), 64 * (g % 2) + 64)
                nc.tensor.matmul(B[g // 2][rows, :], w[rows, g // 2, :], y[rows, g // 2, :], start=True,
                                 stop=True, skip_group_check=True).then_inc(mixed, 1)


def mix_out(core, xT, y_gla, y_dsa, y_pool, w_out):
    nc = core.nc
    B = core.bank
    parts = [(y_gla, h, GLA_DV) for h in range(4)] + [(y_dsa, k, P) for k in range(3)] + [(y_pool, k, P) for k in range(2)]
    with ExitStack() as ctx:
        wg, wd = bufs(nc, ctx, "mo", wg=[GLA_DV, 4, D], wd=[P, 5, D])
        loaded, product, added = sems(nc, ctx, "mo_loaded", "mo_product", "mo_added")
        block = ctx.enter_context(nc.Block())

        @block.sync
        def _(sp):
            sp.dma_start(wg[:], w_out[0:384].rearrange("(k p) n -> p k n", p=GLA_DV)).then_inc(loaded, 16)
            sp.dma_start(wd[:], w_out[384:D].rearrange("(k p) n -> p k n", p=P)).then_inc(loaded, 16)

        @block.tensor
        def _(pe):
            pe.wait_ge(loaded, 32)
            for m in range(KT):
                for i, (y, k, rows) in enumerate(parts):
                    w = wg[:, i, m * P:(m + 1) * P] if i < 4 else wd[:, i - 4, m * P:(m + 1) * P]
                    mm = nc.tensor.matmul(B[m][:], w, y[0:rows, k, :], start=(i == 0), stop=(i == len(parts) - 1))
                mm.then_inc(product, 1)

        @block.vector
        def _(dve):
            for m in range(KT):
                dve.wait_ge(product, m + 1)
                nc.vector.tensor_tensor(xT[:, m, :], xT[:, m, :], B[m][:], ALU.add).then_inc(added, 1)


def load_columns(core, pairs):
    nc = core.nc
    with ExitStack() as ctx:
        (loaded,) = sems(nc, ctx, f"columns_loaded{core.stage_n}")
        core.stage_n += 1
        block = ctx.enter_context(nc.Block())

        @block.sync
        def _(sp):
            with nc.allow_non_contiguous_dma("columns"):
                for dst, vector in pairs:
                    sp.dma_start(dst, columns(vector)).then_inc(loaded, 16)
            sp.wait_ge(loaded, 16 * len(pairs))


def first_block(core, a, xT, hT, ident, ones):
    nc = core.nc
    with ExitStack() as ctx:
        ng, fg, cond2, cond3, y_gla, y_dsa, y_pool = bufs(
            nc, ctx, "b1", ng=[P, KT], fg=[P, KT], cond2=[P, KT], cond3=[P, KT], y_gla=[GLA_DV, GLA_H, T], y_dsa=[P, 3, T], y_pool=[P, 2, T])
        load_columns(core, [(ng[:], a["norm_g"][0]), (fg[:], a["final_norm_g"]), (cond2[:], a["c_2"][0]),
                            (cond3[:], a["c_3"][0])])
        with ExitStack() as inner:
            names = dict(gq=[GLA_DK, GLA_H, T], gk=[GLA_DK, GLA_H, T], gz=[GLA_RANK, T], ggate=[GLA_DV, GLA_H, T],
                         dq=[P, 3, T], dk=[P, 3, T], dgate=[P, 3, T], qi=[P, T], ki=[P, T], pu=[P, 2, T],
                         pgate=[P, 2, T], gv=[P, TT, 384], dv=[P, TT, 384], wi=[P, TT, IDX_H])
            to = dict(zip(names, bufs(nc, inner, "b1", **names)))
            with ExitStack() as s:
                (scratch,) = bufs(nc, s, "b1n", scratch=[P, KT, T])
                norm(core, "n1", xT, hT, ones, scratch, ng)
            projection(core, hT, a["w_in"][0], to)
            gla(core, to, ones, ident, a["gla_gate_w2"][0], a["gla_gate_b"][0], a["gla_norm_g"][0], y_gla)
            with ExitStack() as s:
                (pick,) = bufs(nc, s, "b1s", pick=[P, TT, T])
                dsa_select(core, to, ident, pick, a["w_mod_2"][0], cond2, core.mod2)
                dsa_attend(core, to, ident, a["rel_bias"], a["bias_dram"], pick, y_dsa,
                           a["ada_w_3"][0], cond3, core.mod3)
            pool_mix(core, to, a["pool_w"][0], a["pool_scale"][0], y_pool)
        mix_out(core, xT, y_gla, y_dsa, y_pool, a["w_out"][0])
        with ExitStack() as s:
            (scratch,) = bufs(nc, s, "b1f", scratch=[P, KT, T])
            norm(core, "n2", xT, xT, ones, scratch, fg)



CONV_W, SGU_G = 31, 8
ALPHA = 2.0 ** 0.25
N_EXPERTS, TOP_K, D_EXPERT = 32, 4, 1024
SWIGLU_LIMIT, SWIGLU_ALPHA = 7.0, 1.702
EXTRA = T * TOP_K // P
N_TABLE = N_EXPERTS + EXTRA + 1


def linear(core, name, w, passes, src, evict, stacked=False, more=None):
    nc = core.nc
    B = core.bank
    w_v = w.rearrange("(k p) n -> p k n", p=P)
    engine_name, emit = evict
    with ExitStack() as ctx:
        (wt,) = bufs(nc, ctx, name, w=[P, 2, KT, HALF])
        loaded = sems(nc, ctx, f"{name}_loaded0", f"{name}_loaded1")
        product, copied = sems(nc, ctx, f"{name}_product", f"{name}_copied")
        block = ctx.enter_context(nc.Block())

        def piece(i, s):
            if stacked:
                return w_v[:, bass.ds(i * KT, KT), s * HALF:(s + 1) * HALF]
            return w_v[:, :, bass.ds(i * D + s * HALF, HALF)]

        @block.sync
        def _(sp):
            for s in range(2):
                sp.dma_start(wt[:, s], piece(0, s)).then_inc(loaded[s], 16)
            if passes > 1:
                with sp.Fori(1, passes) as i:
                    for s in range(2):
                        sp.wait_ge(product, 8 * i - 4 + 4 * s)
                        sp.dma_start(wt[:, s], piece(i, s)).then_inc(loaded[s], 16)

        def products(pe, i, first):
            for s in range(2):
                pe.wait_ge(loaded[s], 16 * i + 16)
                for m in range(4):
                    b = 4 * s + m
                    if not first:
                        pe.wait_ge(copied, 8 * i - 7 + b)
                    for k in range(KT):
                        right = src[:, k, :]
                        if stacked and not first:
                            right = src[:, bass.ds(i * KT + k, 1), :].rearrange("p a t -> p (a t)")
                        mm = nc.tensor.matmul(B[b][:], wt[:, s, k, m * P:(m + 1) * P], right,
                                              start=(k == 0), stop=(k == KT - 1))
                    mm.then_inc(product, 1)

        @block.tensor
        def _(pe):
            products(pe, 0, True)
            if passes > 1:
                with pe.Fori(1, passes) as i:
                    products(pe, i, False)

        def evictions(eng):
            for i in range(passes):
                for b in range(8):
                    eng.wait_ge(product, 8 * i + b + 1)
                    emit(i, b, B[b]).then_inc(copied, 1)

        if engine_name == "scalar":
            @block.scalar
            def _(act):
                evictions(act)
        else:
            @block.vector
            def _(dve):
                evictions(dve)

        if more is not None:
            more(block, copied)


def finish_modulation(core, name, mod, bias):
    nc = core.nc
    with ExitStack() as ctx:
        biased, done = sems(nc, ctx, f"{name}_biased", f"{name}_done")
        block = ctx.enter_context(nc.Block())

        @block.vector
        def _(dve):
            nc.vector.tensor_tensor(mod[:], mod[:], bias[:], ALU.add).then_inc(biased, 1)
            dve.wait_ge(biased, 1)
            for lo in (8, 32):
                nc.vector.tensor_scalar(mod[:, lo:lo + KT], mod[:, lo:lo + KT], 1.0, None, ALU.add).then_inc(done, 1)


def mixer_in(core, hT, w_in, b_in, conv_w, conv_b, z, conv):
    nc = core.nc
    funcs = (ACT.Identity, ACT.Sigmoid, ACT.Gelu, ACT.Gelu, ACT.Sigmoid, ACT.Sigmoid)
    PAD = CONV_W - 1
    with ExitStack() as ctx:
        (ya,) = bufs(nc, ctx, "conv", ya=[P, KT, PAD + T])
        gated, tap = sems(nc, ctx, "conv_gated", "conv_tap")

        def emit(i, b, bank):
            return nc.scalar.activation(z[:, 8 * i + b, :], bank[:], funcs[i], bias=b_in[:, 8 * i + b:8 * i + b + 1])

        def convolve(block, copied):
            @block.vector
            def _(dve):
                nc.vector.memset(ya[:, :, 0:PAD], 0.0)
                for k in range(KT):
                    dve.wait_ge(copied, 9 + k)
                    nc.vector.tensor_tensor(ya[:, k, PAD:], z[:, k, :], z[:, 8 + k, :], ALU.mult).then_inc(gated, 1)
                dve.wait_ge(gated, KT)
                for k in range(KT):
                    nc.vector.tensor_scalar(conv[:, k, :], ya[:, k, 0:T], conv_w[:, k, 0:1], conv_b[:, k:k + 1],
                                            ALU.mult, ALU.add).then_inc(tap, 1)
                with dve.Fori(1, CONV_W) as j:
                    for k in range(KT):
                        dve.wait_ge(tap, KT * j - KT + k + 1)
                        nc.vector.scalar_tensor_tensor(
                            out=conv[:, k, :], in0=ya[:, k, bass.ds(j, T)], scalar=conv_w[:, k, bass.ds(j, 1)],
                            in1=conv[:, k, :], op0=ALU.mult, op1=ALU.add).then_inc(tap, 1)

        linear(core, "min", w_in, 6, hT, ("scalar", emit), more=convolve)


def spatial_gating(core, u, v, w_s, b_s, ident):
    nc = core.nc
    B = core.bank
    with ExitStack() as ctx:
        ws, wsT, mask, bs, vT, mixed = bufs(nc, ctx, "sgu", ws=[P, SGU_G, P], wsT=[P, SGU_G, P], mask=[P, P],
                                            bs=[P, SGU_G, P], vT=[P, TT, D], mixed=[P, 2, T])
        loaded, w_turned, w_masked, v_turned, v_copied, product, biased, gated = sems(
            nc, ctx, *(f"sgu_{s}" for s in ("loaded", "w_turned", "w_masked", "v_turned", "v_copied", "product",
                                            "biased", "gated")))
        block = ctx.enter_context(nc.Block())

        @block.sync
        def _(sp):
            sp.dma_start(ws[:], w_s.rearrange("g i j -> i g j")).then_inc(loaded, 16)
            sp.dma_start(mask[:], core.const("sgu_mask")).then_inc(loaded, 16)
            sp.dma_start(bs[:].rearrange("p g i -> p (g i)"),
                         bcast_rows(b_s.rearrange("(a g) i -> a (g i)", a=1))).then_inc(loaded, 16)

        @block.tensor
        def _(pe):
            pe.wait_ge(loaded, 48)
            for g in range(SGU_G):
                mm = nc.tensor.transpose(B[g // 4][:, (g % 4) * P:(g % 4 + 1) * P], ws[:, g, :], ident[:])
                mm.then_inc(w_turned, 1)
            for n in range(8):
                t, half = n // 2, n % 2
                if n >= 6:
                    pe.wait_ge(w_masked, 4 * (n - 5))
                for q in range(4):
                    k = 4 * half + q
                    mm = nc.tensor.transpose(B[(2 + n) % 8][:, q * P:(q + 1) * P], v[:, k, t * P:(t + 1) * P],
                                             ident[:])
                mm.then_inc(v_turned, 1)
            for g in range(SGU_G):
                pe.wait_ge(w_masked, SGU_G)
                pe.wait_ge(v_copied, 8)
                if g >= 2:
                    pe.wait_ge(biased, g - 1)
                for t in range(TT):
                    mm = nc.tensor.matmul(B[g % 2][:, t * P:(t + 1) * P], vT[:, t, g * P:(g + 1) * P],
                                          wsT[:, g, :], start=True, stop=True)
                mm.then_inc(product, 1)

        @block.scalar
        def _(act):
            for n in range(8):
                act.wait_ge(v_turned, n + 1)
                nc.scalar.copy(vT[:, n // 2, (n % 2) * 512:(n % 2 + 1) * 512], B[(2 + n) % 8][:]).then_inc(v_copied, 1)

        @block.vector
        def _(dve):
            dve.wait_ge(loaded, 48)
            for g in range(SGU_G):
                dve.wait_ge(w_turned, 4 * (g // 4 + 1))
                nc.vector.tensor_tensor(wsT[:, g, :], B[g // 4][:, (g % 4) * P:(g % 4 + 1) * P], mask[:],
                                        ALU.mult).then_inc(w_masked, 1)
            for g in range(SGU_G):
                dve.wait_ge(product, g + 1)
                nc.vector.tensor_tensor(mixed[:, g % 2, :].rearrange("p (t i) -> p t i", i=P),
                                        B[g % 2][:].rearrange("p (t i) -> p t i", i=P),
                                        bs[:, g, :].unsqueeze(1).to_broadcast([P, TT, P]), ALU.add).then_inc(biased, 1)
                dve.wait_ge(biased, g + 1)
                nc.vector.tensor_tensor(u[:, g, :], u[:, g, :], mixed[:, g % 2, :], ALU.mult).then_inc(gated, 1)


def second_mixer(core, a, xT, hT, ident, ones, mod, c):
    nc = core.nc
    with ExitStack() as ctx:
        (z,) = bufs(nc, ctx, "b2", z=[P, 48, T])
        tile = lambda i: z[:, 8 * i:8 * i + 8, :]
        norm(core, "n3", xT, hT, ones, tile(0), mod[:, 8:16], mod[:, 0:8], centre=True, eps=LN_EPS)
        with ExitStack() as s:
            (conv,) = bufs(nc, s, "b2", conv=[P, KT, T])
            mixer_in(core, hT, a["w_in_2"][0], c["b_in"], c["conv_w"], c["conv_b"], z, conv)
            norm(core, "n4", conv, hT, ones, tile(0), c["ln_a_g"], c["ln_a_b"], centre=True, func=ACT.Silu,
                 eps=LN_EPS)

        def gated_product(gate, bias, add_to=None):
            def emit(i, b, bank):
                return nc.vector.scalar_tensor_tensor(out=tile(gate)[:, b, :], in0=bank[:], scalar=bias[:, b:b + 1],
                                                      in1=tile(gate)[:, b, :], op0=ALU.add, op1=ALU.mult)
            return ("vector", emit)

        linear(core, "wa", a["w_a_2"][0], 1, hT, gated_product(4, c["b_a"]))
        norm(core, "n5", tile(3), tile(3), ones, tile(0), c["ln_v_g"], c["ln_v_b"], centre=True, eps=LN_EPS)
        spatial_gating(core, tile(2), tile(3), a["w_s_2"][0], a["b_s_2"][0], ident)
        linear(core, "wb", a["w_b_2"][0], 1, tile(2), gated_product(5, c["b_b"]))
        add_tiles(core, "m", tile(4), tile(5))

        def emit(i, b, bank):
            return nc.vector.tensor_scalar(tile(0)[:, b, :], bank[:], c["b_out"][:, b:b + 1], mod[:, 16 + b:17 + b],
                                           ALU.add, ALU.mult)

        linear(core, "wo", a["w_out_2"][0], 1, tile(4), ("vector", emit))
        add_tiles(core, "r", xT, tile(0), ALPHA)
        norm(core, "n6", xT, xT, ones, tile(0), c["post1_g"], c["post1_b"], centre=True, eps=LN_EPS)
        norm(core, "n7", xT, hT, ones, tile(0), mod[:, 32:40], mod[:, 24:32], centre=True, eps=LN_EPS)


def add_tiles(core, name, x, y, scale=1.0):
    nc = core.nc
    with ExitStack() as ctx:
        (added,) = sems(nc, ctx, f"add_{name}")
        block = ctx.enter_context(nc.Block())

        @block.vector
        def _(dve):
            for k in range(KT):
                nc.vector.scalar_tensor_tensor(out=x[:, k, :], in0=x[:, k, :], scalar=scale, in1=y[:, k, :],
                                               op0=ALU.mult, op1=ALU.add).then_inc(added, 1)


def second_columns(core, ctx, a):
    nc = core.nc
    shapes = dict(b_mod=48, b_in=48, conv_b=8, ln_a_g=8, ln_a_b=8, b_a=8, ln_v_g=8, ln_v_b=8, b_b=8, b_out=8,
                  post1_g=8, post1_b=8, post2_g=8, post2_b=8)
    c = dict(zip(shapes, bufs(nc, ctx, "c2", **{n: [P, w] for n, w in shapes.items()})))
    (conv_w,) = bufs(nc, ctx, "c2", conv_w=[P, KT, CONV_W])
    load_columns(core, [(c[n][:], a[f"{n}_2"][0]) for n in shapes]
                 + [(conv_w[:, :, j], a["conv_w_2"][0, j]) for j in range(CONV_W)])
    c["conv_w"] = conv_w
    return c


def second_block(core, a, xT, hT, ident, ones):
    nc = core.nc
    with ExitStack() as ctx:
        c = second_columns(core, ctx, a)
        mod = core.mod2
        finish_modulation(core, "mod2", mod, c["b_mod"])
        second_mixer(core, a, xT, hT, ident, ones, mod, c)
        experts(core, a, xT, hT, ident, ones, mod, c)


def route(core, hT, ident, ones, w_router, b_router, h_dram, y_dram, place, row, weight, block_expert, n_blocks):
    nc = core.nc
    B = core.bank
    NE = N_EXPERTS
    SH = [P, TT, NE]
    XH = [P, EXTRA, NE]
    BH = [P, TT, N_TABLE]
    with ExitStack() as ctx:
        (wr, br, slots, numbers, upto, lg, top, gt, eq, rank, need, ex, tot, pos, extra, upto_e, before, member,
         member2, offset, q, ids, nb, htm, share, here, nth, inside, rows, chosen_row, number,
         zeros) = bufs(
            nc, ctx, "route", wr=[P, KT, NE], br=[P, NE], slots=[P, P], numbers=XH, upto=[P, P], lg=SH,
            top=[P, TT, 8], gt=SH, eq=SH, rank=SH, need=[P, TT, 1], ex=SH, tot=[P, TT, 1], pos=SH, extra=[P, NE],
            upto_e=[P, NE], before=[P, NE], member=XH, member2=XH, offset=XH, q=XH, ids=[P, N_TABLE], nb=[P, 1],
            htm=[P, TT, D], share=BH, here=BH, nth=BH, inside=BH, rows=BH, chosen_row=[P, TT, TOP_K],
            number=[P, N_TABLE], zeros=[P, D])
        loaded, logits, turned, copied, step, shifted, exped, chosen, counted, stored, zeroed = sems(
            nc, ctx, *(f"route_{s}" for s in ("loaded", "logits", "turned", "copied", "step", "shifted", "exped",
                                              "chosen", "counted", "stored", "zeroed")))
        block = ctx.enter_context(nc.Block())

        @block.sync
        def _(sp):
            sp.dma_start(wr[:], w_router.rearrange("(k p) e -> p k e", p=P)).then_inc(loaded, 16)
            sp.dma_start(br[:], bcast_rows(b_router)).then_inc(loaded, 16)
            sp.dma_start(slots[:], core.const("slots")).then_inc(loaded, 16)
            sp.dma_start(numbers[:].rearrange("p b e -> p (b e)"), core.const("numbers")).then_inc(loaded, 16)
            sp.dma_start(upto[:], core.const("upto")).then_inc(loaded, 16)
            sp.dma_start(number[:], core.const("row_number")).then_inc(loaded, 16)
            sp.wait_ge(copied, 8)
            sp.dma_start(h_dram.rearrange("(t p) d -> p t d", p=P), htm[:]).then_inc(stored, 16)
            sp.wait_ge(zeroed, 1)
            for b in range(NE, N_TABLE):
                sp.dma_start(y_dram[b * P:(b + 1) * P, :], zeros[:]).then_inc(stored, 16)
            sp.wait_ge(stored, 16 * (1 + N_TABLE - NE))

        @block.gpsimd
        def _(pool):
            nc.gpsimd.memset(zeros[:], 0.0).then_inc(zeroed, 1)

        @block.tensor
        def _(pe):
            pe.wait_ge(loaded, 96)
            for t in range(TT):
                for k in range(KT):
                    mm = nc.tensor.matmul(B[0][:, t * NE:(t + 1) * NE], hT[:, k, t * P:(t + 1) * P], wr[:, k, :],
                                          start=(k == 0), stop=(k == KT - 1))
            mm.then_inc(logits, 1)
            for n in range(8):
                if n >= 6:
                    pe.wait_ge(copied, n - 5)
                for j in range(4):
                    k = 4 * (n % 2) + j
                    mm = nc.tensor.transpose(B[2 + n % 6][:, j * P:(j + 1) * P],
                                             hT[:, k, (n // 2) * P:(n // 2 + 1) * P], ident[:])
                mm.then_inc(turned, 1)
            pe.wait_ge(chosen, 1)
            for t in range(TT):
                for s in range(t + 1):
                    nc.tensor.matmul(B[1][:, t * NE:(t + 1) * NE], upto[:] if s == t else ones[:], gt[:, s, :],
                                     start=(s == 0), stop=(s == t))
            for s in range(TT):
                mm = nc.tensor.matmul(B[1][:, TT * NE:(TT + 1) * NE], ones[:], gt[:, s, :], start=(s == 0),
                                      stop=(s == TT - 1))
            mm.then_inc(counted, 1)

        @block.scalar
        def _(act):
            for n in range(8):
                act.wait_ge(turned, n + 1)
                nc.scalar.copy(htm[:, n // 2, (n % 2) * 512:(n % 2 + 1) * 512], B[2 + n % 6][:]).then_inc(copied, 1)
            act.wait_ge(shifted, 1)
            nc.scalar.activation(ex[:], lg[:], ACT.Exp).then_inc(exped, 1)

        @block.vector
        def _(dve):
            steps = Count(step)

            def after(instruction):
                dve.wait_ge(step, steps.by(instruction))

            tt, wide = nc.vector.tensor_tensor, lambda ap, shape: ap.to_broadcast(shape)
            over_b = lambda ap: ap[:].unsqueeze(1).to_broadcast(XH)
            dve.wait_ge(loaded, 96)
            dve.wait_ge(logits, 1)
            after(tt(lg[:], B[0][:, 0:TT * NE].rearrange("p (t e) -> p t e", e=NE),
                     br[:].unsqueeze(1).to_broadcast(SH), ALU.add))
            for t in range(TT):
                after(nc.vector.max(top[:, t, :], lg[:, t, :]))
            least = wide(top[:, :, TOP_K - 1:TOP_K], SH)
            after(tt(gt[:], lg[:], least, ALU.is_gt))
            after(tt(eq[:], lg[:], least, ALU.is_equal))
            after(nc.vector.reduce_sum(need[:], gt[:], AX))
            after(nc.vector.tensor_scalar(need[:], need[:], -1.0, float(TOP_K), ALU.mult, ALU.add))
            for t in range(TT):
                after(nc.vector.tensor_tensor_scan(rank[:, t, :], ones[:, 0:NE], eq[:, t, :], 0.0, ALU.mult, ALU.add))
            after(tt(rank[:], rank[:], wide(need[:], SH), ALU.is_le))
            after(tt(eq[:], eq[:], rank[:], ALU.mult))
            nc.vector.tensor_tensor(gt[:], gt[:], eq[:], ALU.add).then_inc(chosen, 1)
            tt(lg[:], lg[:], wide(top[:, :, 0:1], SH), ALU.subtract).then_inc(shifted, 1)
            dve.wait_ge(exped, 1)
            dve.wait_ge(chosen, 1)
            after(tt(ex[:], ex[:], gt[:], ALU.mult))
            after(nc.vector.reduce_sum(tot[:], ex[:], AX))
            after(nc.vector.reciprocal(tot[:], tot[:]))
            after(tt(share[:, :, 0:NE], ex[:], wide(tot[:], SH), ALU.mult))
            dve.wait_ge(counted, 1)
            after(tt(pos[:], B[1][:, 0:TT * NE].rearrange("p (t e) -> p t e", e=NE), gt[:], ALU.mult))
            after(nc.vector.tensor_scalar(pos[:], pos[:], 1.0, None, ALU.subtract))
            after(nc.vector.tensor_copy(place[:, :, 0:NE], pos[:]))
            n = B[1][:, TT * NE:(TT + 1) * NE]
            after(nc.vector.tensor_scalar(extra[:], n, float(P), None, ALU.is_gt))
            for more in (2 * P, 3 * P):
                after(nc.vector.scalar_tensor_tensor(out=extra[:], in0=n, scalar=float(more), in1=extra[:],
                                                     op0=ALU.is_gt, op1=ALU.add))
            after(nc.vector.tensor_tensor_scan(upto_e[:], ones[:, 0:NE], extra[:], 0.0, ALU.mult, ALU.add))
            after(tt(before[:], upto_e[:], extra[:], ALU.subtract))
            after(tt(member[:], numbers[:], over_b(before), ALU.is_ge))
            after(tt(member2[:], numbers[:], over_b(upto_e), ALU.is_lt))
            after(tt(member[:], member[:], member2[:], ALU.mult))
            after(tt(offset[:], numbers[:], over_b(before), ALU.subtract))
            after(nc.vector.tensor_scalar(offset[:], offset[:], 1.0, float(P), ALU.add, ALU.mult))
            after(nc.vector.tensor_scalar(offset[:], offset[:], 1.0, None, ALU.subtract))
            for t in range(TT):
                after(tt(q[:], pos[:, t:t + 1, :].to_broadcast(XH), offset[:], ALU.subtract))
                after(tt(q[:], q[:], member[:], ALU.mult))
                after(nc.vector.reduce_sum(place[:, t, NE:NE + EXTRA], q[:], AX))
                after(tt(q[:], member[:], share[:, t, 0:NE].unsqueeze(1).to_broadcast(XH), ALU.mult))
                after(nc.vector.reduce_sum(share[:, t, NE:NE + EXTRA], q[:], AX))
            after(nc.vector.tensor_scalar(place[:, :, NE:NE + EXTRA], place[:, :, NE:NE + EXTRA], 1.0, None,
                                          ALU.subtract))
            after(tt(q[:], member[:], slots[:, 0:NE].unsqueeze(1).to_broadcast(XH), ALU.mult))
            after(nc.vector.reduce_sum(ids[:, NE:NE + EXTRA], q[:], AX))
            after(nc.vector.tensor_copy(ids[:, 0:NE], slots[:, 0:NE]))
            after(nc.vector.memset(ids[:, N_TABLE - 1:N_TABLE], 0.0))
            after(nc.vector.memset(place[:, :, N_TABLE - 1:N_TABLE], -1.0))
            after(nc.vector.memset(share[:, :, N_TABLE - 1:N_TABLE], 0.0))
            after(nc.vector.tensor_scalar(here[:], share[:], 0.0, None, ALU.is_gt))
            after(nc.vector.tensor_scalar(inside[:], place[:], 0.0, None, ALU.is_ge))
            after(tt(here[:], here[:], inside[:], ALU.mult))
            after(nc.vector.tensor_scalar(inside[:], place[:], float(P), None, ALU.is_lt))
            after(tt(here[:], here[:], inside[:], ALU.mult))
            for t in range(TT):
                after(nc.vector.tensor_tensor_scan(nth[:, t, :], ones[:, 0:N_TABLE], here[:, t, :], 0.0, ALU.mult,
                                                   ALU.add))
            after(tt(nth[:], nth[:], here[:], ALU.mult))
            after(tt(rows[:], place[:], number[:].unsqueeze(1).to_broadcast(BH), ALU.add))
            for j in range(TOP_K):
                after(nc.vector.tensor_scalar(here[:], nth[:], float(j + 1), None, ALU.is_equal))
                after(tt(inside[:], here[:], rows[:], ALU.mult))
                after(nc.vector.reduce_sum(chosen_row[:, :, j:j + 1], inside[:], AX))
                after(tt(inside[:], here[:], share[:], ALU.mult))
                after(nc.vector.reduce_sum(weight[:, :, j:j + 1], inside[:], AX))
            for t in range(TT):
                for j in range(TOP_K):
                    after(nc.vector.tensor_copy(row[TOP_K * t + j][:], chosen_row[:, t, j:j + 1]))
            after(nc.vector.tensor_copy(block_expert[:], ids[0:1, :]))
            after(nc.vector.tensor_scalar(nb[:], upto_e[:, NE - 1:NE], float(NE - 1), None, ALU.add))
            after(nc.vector.tensor_copy(n_blocks[:], nb[0:1, :]))


def expert_blocks(core, h_dram, ident, w_gu, b_gu, w_dn, b_dn, place, block_expert, n_blocks, y_dram):
    nc = core.nc
    B = core.bank
    I32 = mybir.dt.int32
    E = D_EXPERT
    STEPS = 8
    with ExitStack() as ctx:
        (w, bgu, bdn, slots, tokens, S, rows, xb, g, u, sig, hid, hidT, yb) = bufs(
            nc, ctx, "moe", w=[P, 6, KT, HALF], bgu=[P, 2 * E], bdn=[P, D], slots=[P, P], tokens=[P, TT],
            S=[P, TT, P], rows=[P, D], xb=[P, KT, P], g=[P, HALF], u=[P, HALF], sig=[P, HALF], hid=[P, E],
            hidT=[P, KT, P], yb=[P, D])
        row_of_slot = ctx.enter_context(nc.sbuf_tensor("moe_row_of_slot", [P, 1], mybir.dt.uint32))
        w_loaded = sems(nc, ctx, *(f"moe_w_loaded{c}" for c in range(6)))
        (const_loaded, bgu_loaded, bdn_loaded, product, down, hid_turned, slots_made, numbered, rows_known,
         rows_turned, read_out, clipped, hid_made, yb_made, stored, sig_made, xb_made, hidT_made, may_gather, all_stored,
         step) = sems(
            nc, ctx, *(f"moe_{s}" for s in (
                "const_loaded", "bgu_loaded", "bdn_loaded", "product", "down", "hid_turned", "slots_made", "numbered",
                "rows_known", "rows_turned", "read_out", "clipped", "hid_made", "yb_made", "stored",
                "sig_made", "xb_made", "hidT_made", "may_gather", "all_stored",
                "step")))
        gathered = core.block_gathered
        block = ctx.enter_context(nc.Block())
        gu_v = w_gu.rearrange("e (k p) n -> e p k n", p=P)
        dn_v = w_dn.rearrange("e (k p) n -> e p k n", p=P)
        y_v = y_dram.rearrange("(b p) d -> b p d", p=P)
        gu_cols = [0, E, HALF, E + HALF]

        @block.sync
        def _(sp):
            sp.dma_start(slots[:], core.const("slots")).then_inc(const_loaded, 16)
            sp.dma_start(tokens[:], core.const("tokens")).then_inc(const_loaded, 16)

            def store(b):
                sp.dma_start(y_v[bass.ds(b, 1), :, :].rearrange("a p d -> (a p) d"), yb[:]).then_inc(stored, 16)

            def load(b, first):
                e = sp.value_load(block_expert[0:1, bass.ds(b, 1)], min_val=0, max_val=N_EXPERTS - 1)
                for c in range(6):
                    if not first:
                        if c < 4:
                            sp.wait_ge(product, 4 * b - 3 + c)
                        else:
                            sp.wait_ge(down, 2 * b - 5 + c)
                    src = gu_v[bass.ds(e, 1), :, :, gu_cols[c]:gu_cols[c] + HALF] if c < 4 else \
                        dn_v[bass.ds(e, 1), :, :, (c - 4) * HALF:(c - 3) * HALF]
                    sp.dma_start(w[:, c], src.rearrange("a p k n -> (a p) k n")).then_inc(w_loaded[c], 16)
                    if c == 3:
                        if not first:
                            sp.wait_ge(clipped, 2 * b)
                        sp.dma_start(bgu[:], b_gu[bass.ds(e, 1), :].to_broadcast([P, 2 * E])).then_inc(bgu_loaded, 16)
                if not first:
                    sp.wait_ge(yb_made, 2 * b)
                sp.dma_start(bdn[:], b_dn[bass.ds(e, 1), :].to_broadcast([P, D])).then_inc(bdn_loaded, 16)
                if not first:
                    store(b - 1)

            load(0, True)
            n = sp.value_load(n_blocks[0:1, 0:1], min_val=N_EXPERTS - 1, max_val=N_TABLE - 2) + 1
            with sp.Fori(1, n) as b:
                load(b, False)
            sp.wait_ge(yb_made, 2 * n)
            store(n - 1)
            sp.wait_ge(stored, 16 * n)
            sp.sem_inc(all_stored, 1)

        @block.gpsimd
        def _(pool):
            def gather(b, first):
                pool.wait_ge(rows_known, b + 1)
                if not first:
                    pool.wait_ge(rows_turned, 2 * b)
                pool.sem_inc(may_gather, 1)
                pool.indirect_dma_start(rows[:], None, h_dram,
                                        bass.IndirectOffsetOnAxis(ap=row_of_slot[:], axis=0)).then_inc(gathered, 16)

            gather(0, True)
            n = pool.value_load(n_blocks[0:1, 0:1], min_val=N_EXPERTS - 1, max_val=N_TABLE - 2) + 1
            with pool.Fori(1, n + 1) as b:
                gather(b, False)

        @block.tensor
        def _(pe):
            def number_slots(count):
                pe.wait_ge(slots_made, count)
                for t in range(TT):
                    mm = nc.tensor.matmul(B[7][:, 0:1], S[:, t, :], tokens[:, t:t + 1], start=(t == 0),
                                          stop=(t == TT - 1))
                mm.then_inc(numbered, 1)

            def turn_rows(count):
                pe.wait_ge(gathered, 16 * count)
                for half in range(2):
                    for j in range(4):
                        k = 4 * half + j
                        mm = nc.tensor.transpose(B[6 + half][:, j * P:(j + 1) * P], rows[:, k * P:(k + 1) * P],
                                                 ident[:])
                    mm.then_inc(rows_turned, 1)

            def gate_up(b, c):
                pe.wait_ge(w_loaded[c], 16 * b + 16)
                for k in range(KT):
                    mm = nc.tensor.matmul(B[c][:], xb[:, k, :], w[:, c, k, :], start=(k == 0), stop=(k == KT - 1))
                mm.then_inc(product, 1)

            def turn_hidden(b, half, bank):
                pe.wait_ge(hid_made, 2 * b + 1 + half)
                for j in range(4):
                    k = 4 * half + j
                    mm = nc.tensor.transpose(B[bank][:, j * P:(j + 1) * P], hid[:, k * P:(k + 1) * P], ident[:])
                mm.then_inc(hid_turned, 1)

            def down_half(b, half):
                pe.wait_ge(hidT_made, 2 * b + 1 + half)
                for n in range(2):
                    pe.wait_ge(w_loaded[4 + n], 16 * b + 16)
                    for k in range(4 * half, 4 * half + 4):
                        mm = nc.tensor.matmul(B[4 + n][:], hidT[:, k, :], w[:, 4 + n, k, :], start=(k == 0),
                                              stop=(k == KT - 1))
                    if half == 1:
                        mm.then_inc(down, 1)

            def step_block(b, first):
                pe.wait_ge(xb_made, 2 * b + 2)
                if not first:
                    pe.wait_ge(read_out, 2 * b - 1)
                gate_up(b, 0)
                number_slots(b + 2)
                gate_up(b, 1)
                if not first:
                    pe.wait_ge(read_out, 2 * b)
                gate_up(b, 2)
                gate_up(b, 3)
                pe.wait_ge(rows_known, b + 2)
                turn_hidden(b, 0, 7)
                if not first:
                    pe.wait_ge(yb_made, 2 * b)
                down_half(b, 0)
                turn_rows(b + 2)
                pe.wait_ge(xb_made, 2 * b + 3)
                turn_hidden(b, 1, 6)
                down_half(b, 1)

            number_slots(1)
            turn_rows(1)
            step_block(0, True)
            n = pe.value_load(n_blocks[0:1, 0:1], min_val=N_EXPERTS - 1, max_val=N_TABLE - 2) + 1
            with pe.Fori(1, n) as b:
                step_block(b, False)

        @block.scalar
        def _(act):
            def numbers_out(count):
                act.wait_ge(numbered, count)
                nc.scalar.copy(row_of_slot[:], B[7][:, 0:1]).then_inc(rows_known, 1)

            def rows_out(count):
                for half in range(2):
                    act.wait_ge(rows_turned, count + half)
                    nc.scalar.copy(xb[:, 4 * half:4 * half + 4, :].rearrange("p k t -> p (k t)"),
                                   B[6 + half][:]).then_inc(xb_made, 1)

            def sigmoid(count):
                act.wait_ge(clipped, count)
                nc.scalar.activation(sig[:], g[:], ACT.Sigmoid, scale=SWIGLU_ALPHA).then_inc(sig_made, 1)

            def hidden_out(b, half, bank):
                act.wait_ge(hid_turned, 2 * b + 1 + half)
                nc.scalar.copy(hidT[:, 4 * half:4 * half + 4, :].rearrange("p k t -> p (k t)"),
                               B[bank][:]).then_inc(hidT_made, 1)

            def step_block(b):
                act.wait_ge(gathered, 16 * b + 16)
                numbers_out(b + 2)
                sigmoid(2 * b + 1)
                hidden_out(b, 0, 7)
                sigmoid(2 * b + 2)
                rows_out(2 * b + 3)
                hidden_out(b, 1, 6)

            numbers_out(1)
            rows_out(1)
            step_block(0)
            n = act.value_load(n_blocks[0:1, 0:1], min_val=N_EXPERTS - 1, max_val=N_TABLE - 2) + 1
            with act.Fori(1, n) as b:
                step_block(b)

        @block.vector
        def _(dve):
            vec = nc.vector

            def make_slots(b):
                for t in range(TT):
                    ins = vec.tensor_scalar(S[:, t, :], slots[:], place[:, t, bass.ds(b, 1)], None, ALU.is_equal)
                ins.then_inc(slots_made, 1)

            def hidden(b, half, first):
                at = STEPS * b + 4 * half

                def after(instruction, n):
                    instruction.then_inc(step, 1)
                    dve.wait_ge(step, at + n)

                if half or not first:
                    dve.wait_ge(hid_made, 2 * b + half)
                dve.wait_ge(product, 4 * b + 2 + 2 * half)
                lo = half * HALF
                after(vec.tensor_tensor(g[:], B[2 * half][:], bgu[:, lo:lo + HALF], ALU.add), 1)
                after(vec.tensor_scalar(g[:], g[:], SWIGLU_LIMIT, None, ALU.min), 2)
                vec.tensor_tensor(u[:], B[2 * half + 1][:], bgu[:, E + lo:E + lo + HALF], ALU.add).then_inc(clipped, 1)
                dve.wait_ge(clipped, 2 * b + 1 + half)
                after(vec.tensor_scalar(u[:], u[:], SWIGLU_LIMIT, -SWIGLU_LIMIT, ALU.min, ALU.max), 3)
                vec.tensor_scalar(u[:], u[:], 1.0, None, ALU.add).then_inc(read_out, 1)
                dve.wait_ge(sig_made, 2 * b + 1 + half)
                after(vec.tensor_tensor(g[:], g[:], sig[:], ALU.mult), 4)
                dve.wait_ge(read_out, 2 * b + 1 + half)
                vec.tensor_tensor(hid[:, lo:lo + HALF], u[:], g[:], ALU.mult).then_inc(hid_made, 1)

            def step_block(b, first):
                dve.wait_ge(numbered, b + 1)
                make_slots(b + 1)
                dve.wait_ge(bgu_loaded, 16 * b + 16)
                hidden(b, 0, first)
                hidden(b, 1, first)
                dve.wait_ge(bdn_loaded, 16 * b + 16)
                if not first:
                    dve.wait_ge(stored, 16 * b)
                for n in range(2):
                    dve.wait_ge(down, 2 * b + 1 + n)
                    vec.tensor_tensor(yb[:, n * HALF:(n + 1) * HALF], B[4 + n][:], bdn[:, n * HALF:(n + 1) * HALF],
                                      ALU.add).then_inc(yb_made, 1)

            dve.wait_ge(const_loaded, 32)
            make_slots(0)
            step_block(0, True)
            n = dve.value_load(n_blocks[0:1, 0:1], min_val=N_EXPERTS - 1, max_val=N_TABLE - 2) + 1
            with dve.Fori(1, n) as b:
                step_block(b, False)


def combine(core, y_dram, row, weight, ident, gain, acc):
    nc = core.nc
    B = core.bank
    SLOTS = len(core.combine_gathered)
    N = TT * TOP_K
    with ExitStack() as ctx:
        rows, total = bufs(nc, ctx, "combine", rows=[P, SLOTS, D], total=[P, TT, D])
        gathered = core.combine_gathered
        used, turned, copied = sems(nc, ctx, "combine_used", "combine_turned", "combine_copied")
        block = ctx.enter_context(nc.Block())

        @block.gpsimd
        def _(pool):
            for n in range(N):
                if n >= SLOTS:
                    pool.wait_ge(used, n - SLOTS + 1)
                pool.indirect_dma_start(rows[:, n % SLOTS, :], None, y_dram,
                                        bass.IndirectOffsetOnAxis(ap=row[n][:], axis=0)).then_inc(
                                            gathered[n % SLOTS], 16)

        @block.vector
        def _(dve):
            for n in range(N):
                t, j = n // TOP_K, n % TOP_K
                dve.wait_ge(gathered[n % SLOTS], 16 * (n // SLOTS + 1))
                if j == 0:
                    nc.vector.tensor_scalar(total[:, t, :], rows[:, n % SLOTS, :], weight[:, t, j:j + 1], None,
                                            ALU.mult).then_inc(used, 1)
                else:
                    dve.wait_ge(used, n)
                    nc.vector.scalar_tensor_tensor(out=total[:, t, :], in0=rows[:, n % SLOTS, :],
                                                   scalar=weight[:, t, j:j + 1], in1=total[:, t, :], op0=ALU.mult,
                                                   op1=ALU.add).then_inc(used, 1)

        @block.tensor
        def _(pe):
            for t in range(TT):
                pe.wait_ge(used, TOP_K * (t + 1))
                for k in range(KT):
                    nc.tensor.transpose(B[k][:, t * P:(t + 1) * P], total[:, t, k * P:(k + 1) * P],
                                        ident[:]).then_inc(turned, 1)

        @block.scalar
        def _(act):
            for k in range(KT):
                act.wait_ge(turned, KT * (TT - 1) + k + 1)
                nc.scalar.activation(acc[:, k, :], B[k][:], ACT.Copy, scale=gain[:, k:k + 1]).then_inc(copied, 1)


def experts(core, a, xT, hT, ident, ones, mod, c):
    nc = core.nc
    with ExitStack() as s:
        place, weight = bufs(nc, s, "ex", place=[P, TT, N_TABLE], weight=[P, TT, TOP_K])
        block_expert = s.enter_context(nc.sbuf_tensor("ex_block_expert", [1, N_TABLE], mybir.dt.int32))
        n_blocks = s.enter_context(nc.sbuf_tensor("ex_n_blocks", [1, 1], mybir.dt.int32))
        row = [s.enter_context(nc.sbuf_tensor(f"ex_row{n}", [P, 1], mybir.dt.uint32)) for n in range(TT * TOP_K)]
        route(core, hT, ident, ones, a["w_router_2"][0], a["b_router_2"], a["h_dram"], a["y_dram"], place, row, weight,
              block_expert, n_blocks)
        expert_blocks(core, a["h_dram"], ident, a["w_gu_2"][0], a["b_gu_2"][0], a["w_dn_2"][0], a["b_dn_2"][0], place,
                      block_expert, n_blocks, a["y_dram"])
        (acc,) = bufs(nc, s, "ex", acc=[P, KT, T])
        combine(core, a["y_dram"], row, weight, ident, mod[:, 40:48], acc)
        (scratch,) = bufs(nc, s, "ex", scratch=[P, KT, T])
        add_tiles(core, "x2", xT, acc, ALPHA)
        norm(core, "n8", xT, xT, ones, scratch, c["post2_g"], c["post2_b"], centre=True, eps=LN_EPS)





SSD_H, SSD_DH, SSD_N, SSD_G, SSD_CONV = 16, 64, 128, 2, 5
XBC = 1024 + 2 * SSD_G * SSD_N
XT = XBC // P
HG_H = 8
LB_FLOOR = 1e-30


def ssd_inputs(core, hT, w_in, conv_w, conv_b, zs, xbc, dt_raw):
    nc = core.nc
    B = core.bank
    PAD = SSD_CONV // 2
    w_v = w_in.rearrange("(k p) n -> p k n", p=P)
    TILES = 8 + XT
    PIECES = TILES // 4
    with ExitStack() as ctx:
        wt, wd, raw = bufs(nc, ctx, "si", w=[P, 2, KT, HALF], wd=[P, KT, SSD_H], raw=[P, XT, T + 2 * PAD])
        loaded = sems(nc, ctx, "si_loaded0", "si_loaded1")
        wd_loaded, product, copied, padded, tap, convolved, dt_product, activated = sems(
            nc, ctx, *(f"si_{s}" for s in ("wd_loaded", "product", "copied", "padded", "tap", "convolved",
                                           "dt_product", "activated")))
        block = ctx.enter_context(nc.Block())

        @block.sync
        def _(sp):
            for c in range(PIECES):
                if c >= 2:
                    sp.wait_ge(product, 4 * (c - 1))
                col = (1024 + c * HALF) if c < XT // 4 else (c - XT // 4) * HALF
                sp.dma_start(wt[:, c % 2], w_v[:, :, col:col + HALF]).then_inc(loaded[c % 2], 16)
            sp.dma_start(wd[:], w_v[:, :, 1024 + XBC:1024 + XBC + SSD_H]).then_inc(wd_loaded, 16)

        @block.tensor
        def _(pe):
            for n in range(TILES):
                c = n // 4
                pe.wait_ge(loaded[c % 2], 16 * (c // 2 + 1))
                if n >= 8:
                    pe.wait_ge(copied, n - 7)
                for k in range(KT):
                    mm = nc.tensor.matmul(B[n % 8][:], wt[:, c % 2, k, (n % 4) * P:(n % 4 + 1) * P], hT[:, k, :],
                                          start=(k == 0), stop=(k == KT - 1))
                mm.then_inc(product, 1)
            pe.wait_ge(wd_loaded, 16)
            pe.wait_ge(copied, TILES - 7)
            for k in range(KT):
                mm = nc.tensor.matmul(B[TILES % 8][0:SSD_H, :], wd[:, k, :], hT[:, k, :], start=(k == 0),
                                      stop=(k == KT - 1))
            mm.then_inc(dt_product, 1)

        @block.scalar
        def _(act):
            for n in range(TILES):
                act.wait_ge(product, n + 1)
                if n < XT:
                    nc.scalar.copy(raw[:, n, PAD:PAD + T], B[n % 8][:]).then_inc(copied, 1)
                else:
                    nc.scalar.activation(zs[:, n - XT, :], B[n % 8][:], ACT.Silu).then_inc(copied, 1)
            act.wait_ge(dt_product, 1)
            nc.scalar.copy(dt_raw[:], B[TILES % 8][0:SSD_H, :]).then_inc(activated, 1)
            for n in range(XT):
                act.wait_ge(convolved, n + 1)
                nc.scalar.activation(xbc[:, n, :], xbc[:, n, :], ACT.Silu, bias=conv_b[:, n:n + 1]).then_inc(activated, 1)

        @block.vector
        def _(dve):
            nc.vector.memset(raw[:, :, 0:PAD], 0.0).then_inc(padded, 1)
            nc.vector.memset(raw[:, :, PAD + T:], 0.0).then_inc(padded, 1)
            dve.wait_ge(padded, 2)
            for q in range(XT // 4):
                for j in range(SSD_CONV):
                    for i in range(4):
                        n = 4 * q + i
                        if j == 0:
                            dve.wait_ge(copied, n + 1)
                            nc.vector.tensor_scalar(xbc[:, n, :], raw[:, n, 0:T], conv_w[:, n, 0:1], None,
                                                    ALU.mult).then_inc(tap, 1)
                            continue
                        dve.wait_ge(tap, 4 * (4 * q + j - 1) + i + 1)
                        nc.vector.scalar_tensor_tensor(
                            out=xbc[:, n, :], in0=raw[:, n, j:j + T], scalar=conv_w[:, n, j:j + 1], in1=xbc[:, n, :],
                            op0=ALU.mult, op1=ALU.add).then_inc(convolved if j == SSD_CONV - 1 else tap, 1)


def ssd_prepare(core, xbc, x_tm, b_tm, scores, y, skip, ident):
    nc = core.nc
    B = core.bank
    with ExitStack() as ctx:
        turned, copied, skipped = sems(nc, ctx, "sp_turned", "sp_copied", "sp_skipped")
        block = ctx.enter_context(nc.Block())
        outs = [(x_tm[:, n // 2, (n % 2) * 512:(n % 2 + 1) * 512]) for n in range(8)]
        outs += [b_tm[:, 2 * n:2 * n + 2, :].rearrange("p t c -> p (t c)") for n in range(2)]
        outs += [scores[:, g, :] for g in range(SSD_G)]

        @block.tensor
        def _(pe):
            for n in range(12):
                if n >= 8:
                    pe.wait_ge(copied, n - 7)
                for j in range(4):
                    out = B[n % 8][:, j * P:(j + 1) * P]
                    if n < 8:
                        t, k = n // 2, 4 * (n % 2) + j
                        mm = nc.tensor.transpose(out, xbc[:, k, t * P:(t + 1) * P], ident[:])
                    elif n < 10:
                        t, g = 2 * (n - 8) + j // 2, j % 2
                        mm = nc.tensor.transpose(out, xbc[:, 8 + g, t * P:(t + 1) * P], ident[:])
                    else:
                        g, cols = n - 10, slice(j * P, (j + 1) * P)
                        mm = nc.tensor.matmul(out, xbc[:, 8 + g, cols], xbc[:, 10 + g, cols], start=True, stop=True)
                mm.then_inc(turned, 1)

        @block.scalar
        def _(act):
            for n in range(12):
                act.wait_ge(turned, n + 1)
                nc.scalar.copy(outs[n], B[n % 8][:]).then_inc(copied, 1)

        @block.vector
        def _(dve):
            for k in range(KT):
                nc.vector.tensor_scalar(y[:, k, :], xbc[:, k, :], skip[:, k:k + 1], None, ALU.mult).then_inc(skipped, 1)


def ssd_direction(core, d, xbc, x_tm, b_tm, scores, dt_raw, dt_bias, a_log, y, ones, ident):
    nc = core.nc
    B = core.bank
    H = SSD_H
    order = list(range(TT)) if d == 0 else list(range(TT))[::-1]
    name = f"ssd{d}"
    with ExitStack() as ctx:
        (mask, reset, sel, sel2, dt, la, G, V, I, tmp, tmp2, neg, diag, dT, GT, WT, CD, xdt, xw, gm, seg, wgt, ep, prod,
         S) = bufs(
            nc, ctx, name, mask=[P, P], reset=[H, T], sel=[H, H * P], sel2=[H, KT * P], dt=[H, T], la=[H, T],
            G=[H, T], V=[H, T], I=[H, T], tmp=[H, T], tmp2=[H, T], neg=[H, 1], diag=[H, TT, H], dT=[P, TT, H],
            GT=[P, TT, H], WT=[P, TT, H], CD=[P, TT, H], xdt=[P, TT, D], xw=[P, D], gm=[P, SSD_G, T],
            seg=[P, 2, T], wgt=[P, 2, T], ep=[P, 2, T], prod=[P, T], S=[P, TT, D])
        (loaded, step, act_step, to_act, from_act, rows_ready, turned, dec_made, cols_ready, xw_made, u_made, state,
         spread, seg_made, seg_exped, weights, pair_done, ep_spread, ep_made, y_added) = sems(
            nc, ctx, *(f"{name}_{s}" for s in (
                "loaded", "step", "act_step", "to_act", "from_act", "rows_ready", "turned", "dec_made", "cols_ready",
                "xw_made", "u_made", "state", "spread", "seg_made", "seg_exped", "weights", "pair_done", "ep_spread",
                "ep_made", "y_added")))
        block = ctx.enter_context(nc.Block())
        chunks = lambda ap: ap[:].rearrange("p (c t) -> p c t", t=P)
        ends = lambda ap: chunks(ap)[:, :, P - 1:P].to_broadcast([H, TT, P])

        @block.sync
        def _(sp):
            sp.dma_start(mask[:], core.const("upto" if d == 0 else "from")).then_inc(loaded, 16)
            sp.dma_start(reset[:], core.const("reset128", H)).then_inc(loaded, 16)
            sp.dma_start(sel[:], core.const("one_head", H)).then_inc(loaded, 16)
            sp.dma_start(sel2[:], core.const("two_heads", H)).then_inc(loaded, 16)

        @block.scalar
        def _(act):
            act.wait_ge(to_act, 1)
            nc.scalar.activation(tmp[:], dt[:], ACT.Abs).then_inc(act_step, 1)
            act.wait_ge(act_step, 1)
            nc.scalar.activation(tmp[:], tmp[:], ACT.Exp, scale=-1.0).then_inc(act_step, 1)
            nc.scalar.activation(neg[:], a_log[:, d:d + 1], ACT.Exp).then_inc(act_step, 1)
            act.wait_ge(act_step, 3)
            nc.scalar.activation(tmp2[:], tmp[:], ACT.Ln, bias=1.0).then_inc(from_act, 1)
            act.wait_ge(to_act, 2)
            nc.scalar.activation(V[:], V[:], ACT.Exp).then_inc(act_step, 1)
            nc.scalar.activation(tmp2[:, 0:TT], chunks(tmp)[:, :, P - 1], ACT.Exp).then_inc(from_act, 1)
            for k in range(KT):
                for h in (2 * k, 2 * k + 1):
                    act.wait_ge(seg_made, h + 1)
                    if h >= 2:
                        act.wait_ge(weights, h - 1)
                    nc.scalar.activation(seg[:, h % 2, :], seg[:, h % 2, :], ACT.Exp,
                                         scale=1.0 if d == 0 else -1.0).then_inc(seg_exped, 1)
                act.wait_ge(ep_spread, k + 1)
                if k >= 2:
                    act.wait_ge(y_added, k - 1)
                nc.scalar.activation(ep[:, k % 2, :], B[6][:], ACT.Exp).then_inc(ep_made, 1)

        @block.vector
        def _(dve):
            steps = Count(step)
            vec, tt = nc.vector, nc.vector.tensor_tensor

            def after(instruction):
                dve.wait_ge(step, steps.by(instruction))

            vec.tensor_scalar(dt[:], dt_raw[:], dt_bias[:, d:d + 1], None, ALU.add).then_inc(to_act, 1)
            dve.wait_ge(from_act, 1)
            after(vec.tensor_scalar(la[:], tmp[:], 1.0, -1.0, ALU.add, ALU.add))
            after(vec.tensor_scalar(V[:], la[:], 0.0, None, ALU.is_equal))
            after(tt(tmp2[:], tmp2[:], V[:], ALU.add))
            after(tt(la[:], la[:], V[:], ALU.add))
            after(vec.reciprocal(la[:], la[:]))
            after(tt(la[:], la[:], tmp2[:], ALU.mult))
            after(tt(tmp[:], tmp[:], la[:], ALU.mult))
            after(vec.scalar_tensor_tensor(out=dt[:], in0=dt[:], scalar=0.0, in1=tmp[:], op0=ALU.max, op1=ALU.add))
            after(vec.tensor_scalar(la[:], dt[:], neg[:], -1.0, ALU.mult, ALU.mult))
            dve.wait_ge(loaded, 64)
            after(vec.tensor_tensor_scan(tmp[:], reset[:], la[:], 0.0, ALU.mult, ALU.add))
            if d == 0:
                after(vec.tensor_copy(G[:], tmp[:]))
                after(vec.tensor_copy(I[:], tmp[:]))
                last = tt(chunks(V), ends(tmp), chunks(G), ALU.subtract)
            else:
                after(tt(G[:], tmp[:], la[:], ALU.subtract))
                after(tt(chunks(I), ends(tmp), chunks(G), ALU.subtract))
                last = vec.tensor_copy(V[:], G[:])
            last.then_inc(to_act, 1)
            dve.wait_ge(from_act, 2)
            tt(V[:], V[:], dt[:], ALU.mult)
            for c in range(TT):
                last = vec.tensor_scalar(diag[:, c, :], ident[0:H, 0:H], tmp2[:, c:c + 1], None, ALU.mult)
            last.then_inc(rows_ready, 1)
            for g in range(SSD_G):
                tt(gm[:, g, :].rearrange("p (c t) -> p c t", t=P), scores[:, g, :].rearrange("p (c t) -> p c t", t=P),
                   mask[:].unsqueeze(1).to_broadcast([P, TT, P]), ALU.mult).then_inc(cols_ready, 1)
            dve.wait_ge(turned, 1)
            for i, dst in enumerate((dT, GT, WT, CD)):
                last = vec.tensor_copy(dst[:].rearrange("p c h -> p (c h)"), B[0][:, i * TT * H:(i + 1) * TT * H])
            last.then_inc(cols_ready, 1)
            dve.wait_ge(cols_ready, SSD_G + 1)
            by_head = lambda ap: ap.rearrange("p (h e) -> p h e", e=SSD_DH)
            for c in range(TT):
                tt(by_head(xdt[:, c, :]), by_head(x_tm[:, c, :]),
                   dT[:, c, :].unsqueeze(2).to_broadcast([P, H, SSD_DH]), ALU.mult).then_inc(cols_ready, 1)
            vec.memset(S[:, order[0], :], 0.0).then_inc(state, 1)
            for i, c in enumerate(order[:-1]):
                if i:
                    dve.wait_ge(u_made, 2 * i)
                tt(by_head(xw[:]), by_head(x_tm[:, c, :]), WT[:, c, :].unsqueeze(2).to_broadcast([P, H, SSD_DH]),
                   ALU.mult).then_inc(xw_made, 1)
                nxt = order[i + 1]
                dve.wait_ge(state, 3 * i + 1)
                tt(by_head(S[:, nxt, :]), by_head(S[:, c, :]), CD[:, c, :].unsqueeze(2).to_broadcast([P, H, SSD_DH]),
                   ALU.mult).then_inc(state, 1)
                dve.wait_ge(state, 3 * i + 2)
                for g in range(SSD_G):
                    dve.wait_ge(u_made, 2 * i + g + 1)
                    cols = slice(g * 512, (g + 1) * 512)
                    last = tt(S[:, nxt, cols], S[:, nxt, cols], B[1 + g][:], ALU.add)
                last.then_inc(state, 2)
                dve.wait_ge(state, 3 * i + 4)
            for k in range(KT):
                for h in (2 * k, 2 * k + 1):
                    dve.wait_ge(spread, h + 1)
                    if h >= 2:
                        dve.wait_ge(weights, h - 1)
                    for c in range(TT):
                        cols = slice(c * P, (c + 1) * P)
                        last = vec.tensor_scalar(seg[:, h % 2, cols], B[h % 2][:, cols], GT[:, c, h:h + 1], 0.0,
                                                 ALU.subtract, ALU.min if d == 0 else ALU.max)
                    last.then_inc(seg_made, 1)
                for h in (2 * k, 2 * k + 1):
                    dve.wait_ge(seg_exped, h + 1)
                    if k:
                        dve.wait_ge(pair_done, k)
                    tt(wgt[:, h % 2, :], seg[:, h % 2, :], gm[:, h // 8, :], ALU.mult).then_inc(weights, 1)
                dve.wait_ge(pair_done, k + 1)
                dve.wait_ge(ep_made, k + 1)
                after(tt(prod[:], B[4 + k % 2][:], ep[:, k % 2, :], ALU.mult))
                after(tt(prod[:], prod[:], B[2 + k % 2][:], ALU.add))
                tt(y[:, k, :], y[:, k, :], prod[:], ALU.add).then_inc(y_added, 1)
                dve.wait_ge(y_added, k + 1)

        @block.tensor
        def _(pe):
            pe.wait_ge(rows_ready, 1)
            for i, rows in enumerate((dt, G, V)):
                for c in range(TT):
                    at = (i * TT + c) * H
                    nc.tensor.transpose(B[0][:, at:at + H], rows[:, c * P:(c + 1) * P], ident[0:H, 0:H])
            for c in range(TT):
                at = (3 * TT + c) * H
                mm = nc.tensor.matmul(B[0][:, at:at + H], ones[0:H, :], diag[:, c, :], start=True, stop=True)
            mm.then_inc(turned, 1)
            for i, c in enumerate(order[:-1]):
                pe.wait_ge(xw_made, i + 1)
                pe.wait_ge(state, 3 * i + 1)
                for g in range(SSD_G):
                    nc.tensor.matmul(B[1 + g][:], b_tm[:, c, g * P:(g + 1) * P], xw[:, g * 512:(g + 1) * 512],
                                     start=True, stop=True).then_inc(u_made, 1)
            pe.wait_ge(state, 3 * (TT - 1) + 1)
            pe.wait_ge(cols_ready, SSD_G + 1 + TT)

            def spread_head(h):
                if h >= 2:
                    pe.wait_ge(seg_made, h - 1)
                nc.tensor.matmul(B[h % 2][:], sel[:, h * P:(h + 1) * P], G[:], start=True, stop=True).then_inc(spread, 1)

            spread_head(0)
            spread_head(1)
            for k in range(KT):
                if k + 1 < KT:
                    spread_head(2 * k + 2)
                    spread_head(2 * k + 3)
                if k:
                    pe.wait_ge(ep_made, k)
                nc.tensor.matmul(B[6][:], sel2[:, k * P:(k + 1) * P], I[:], start=True, stop=True).then_inc(ep_spread, 1)
                if k >= 2:
                    pe.wait_ge(y_added, k - 1)
                for c in range(TT):
                    cols = slice(c * P, (c + 1) * P)
                    nc.tensor.matmul(B[4 + k % 2][:, cols], S[:, c, k * P:(k + 1) * P], xbc[:, 10 + k // 4, cols],
                                     start=True, stop=True)
                for h in (2 * k, 2 * k + 1):
                    pe.wait_ge(weights, h + 1)
                    rows = slice(SSD_DH * (h % 2), SSD_DH * (h % 2) + SSD_DH)
                    for c in range(TT):
                        cols = slice(c * P, (c + 1) * P)
                        mm = nc.tensor.matmul(B[2 + k % 2][rows, cols], xdt[:, c, h * SSD_DH:(h + 1) * SSD_DH],
                                              wgt[:, h % 2, cols], start=True, stop=True, skip_group_check=True)
                mm.then_inc(pair_done, 1)


def multiply_tiles(core, name, x, y):
    nc = core.nc
    with ExitStack() as ctx:
        (done,) = sems(nc, ctx, f"multiplied_{name}")
        block = ctx.enter_context(nc.Block())

        @block.vector
        def _(dve):
            for k in range(x.shape[1]):
                nc.vector.tensor_tensor(x[:, k, :], x[:, k, :], y[:, k, :], ALU.mult).then_inc(done, 1)


def hgrn_gates(core, d, f, kh, lower):
    nc = core.nc
    floor_log, rest_log, rest, total = lower
    name = f"hgate{d}"
    with ExitStack() as ctx:
        reset, a, b, diff = bufs(nc, ctx, name, reset=[P, T], a=[P, KT, T], b=[P, KT, T], diff=[P, KT])
        (loaded, diffed, magnitude, rate, log_term, kept, outer_magnitude, outer_rate, outer_term, log_sig, kept_log,
         apart, joined, logged, summed, kept_scaled, totalled, done) = sems(
            nc, ctx, *(f"{name}_{s}" for s in (
                "loaded", "diffed", "magnitude", "rate", "log_term", "kept", "outer_magnitude", "outer_rate",
                "outer_term", "log_sig", "kept_log", "apart", "joined", "logged", "summed", "kept_scaled",
                "totalled", "done")))
        block = ctx.enter_context(nc.Block())

        @block.sync
        def _(sp):
            sp.dma_start(reset[:], core.const("reset128")).then_inc(loaded, 16)

        @block.scalar
        def _(act):
            func = nc.scalar.activation
            for k in range(KT):
                func(a[:, k, :], f[:, k, :], ACT.Abs).then_inc(magnitude, 1)
            for k in range(KT):
                act.wait_ge(magnitude, k + 1)
                func(a[:, k, :], a[:, k, :], ACT.Exp, scale=-1.0).then_inc(rate, 1)
            for k in range(KT):
                act.wait_ge(rate, k + 1)
                func(a[:, k, :], a[:, k, :], ACT.Ln, bias=1.0).then_inc(log_term, 1)
            for k in range(KT):
                act.wait_ge(apart, k + 1)
                func(a[:, k, :], b[:, k, :], ACT.Abs).then_inc(outer_magnitude, 1)
            for k in range(KT):
                act.wait_ge(outer_magnitude, k + 1)
                func(a[:, k, :], a[:, k, :], ACT.Exp, scale=-1.0).then_inc(outer_rate, 1)
                func(kh[:, k, :], kh[:, k, :], ACT.Exp).then_inc(kept, 1)
            for k in range(KT):
                act.wait_ge(outer_rate, k + 1)
                func(a[:, k, :], a[:, k, :], ACT.Ln, bias=1.0).then_inc(outer_term, 1)

        @block.vector
        def _(dve):
            vec = nc.vector
            cols = slice(KT * d, KT * (d + 1))
            vec.tensor_tensor(diff[:], rest_log[:, cols], floor_log[:, cols], ALU.subtract).then_inc(diffed, 1)
            dve.wait_ge(diffed, 1)
            for k in range(KT):
                dve.wait_ge(log_term, k + 1)
                vec.scalar_tensor_tensor(out=b[:, k, :], in0=f[:, k, :], scalar=0.0, in1=a[:, k, :], op0=ALU.min,
                                         op1=ALU.subtract).then_inc(log_sig, 1)
                dve.wait_ge(log_sig, k + 1)
                vec.tensor_tensor(kh[:, k, :], b[:, k, :], f[:, k, :], ALU.subtract).then_inc(kept_log, 1)
                dve.wait_ge(kept_log, k + 1)
                vec.tensor_scalar(b[:, k, :], b[:, k, :], diff[:, k:k + 1], None, ALU.add).then_inc(apart, 1)
            dve.wait_ge(loaded, 16)
            for k in range(KT):
                at = KT * d + k
                dve.wait_ge(outer_term, k + 1)
                vec.scalar_tensor_tensor(out=b[:, k, :], in0=b[:, k, :], scalar=0.0, in1=a[:, k, :], op0=ALU.max,
                                         op1=ALU.add).then_inc(joined, 1)
                vec.tensor_scalar(kh[:, k, :], kh[:, k, :], rest[:, at:at + 1], None, ALU.mult).then_inc(kept_scaled, 1)
                dve.wait_ge(joined, k + 1)
                vec.tensor_scalar(b[:, k, :], b[:, k, :], floor_log[:, at:at + 1], None, ALU.add).then_inc(logged, 1)
                dve.wait_ge(logged, k + 1)
                vec.tensor_tensor_scan(f[:, k, :], reset[:], b[:, k, :], 0.0, ALU.mult, ALU.add).then_inc(summed, 1)
                dve.wait_ge(summed, k + 1)
                vec.tensor_copy(total[:, k, :], f[:, k, P - 1:T:P]).then_inc(totalled, 1)
                if d == 1:
                    dve.wait_ge(totalled, k + 1)
                    vec.tensor_tensor(f[:, k, :], f[:, k, :], b[:, k, :], ALU.subtract).then_inc(done, 1)


def hgrn_direction(core, d, q, G, kh, total, v_tm, y, ident):
    nc = core.nc
    B = core.bank
    name = f"hg{d}"
    LEVELS = [64, 32, 16, 8, 4, 2, 1]
    NL = len(LEVELS)
    NM = NL + 1
    order = list(range(TT)) if d == 0 else list(range(TT))[::-1]
    R = 3
    with ExitStack() as ctx:
        mask, diff, qs, ks, A, qe, kd, kdT, dec, S = bufs(
            nc, ctx, name, mask=[P, NM, P], diff=[P, R, T], qs=[P, R, T], ks=[P, R, T], A=[P, 2, T], qe=[P, 2, T],
            kd=[P, 2, T], kdT=[P, T], dec=[P, KT, TT], S=[P, TT, P])
        (loaded, diffed, exped, scaled, product, picked, zeroed, decayed, end_diffed, end_exped, end_scaled, turned,
         turned_copied, u_made, state, out_made, added) = sems(
            nc, ctx, *(f"{name}_{s}" for s in (
                "loaded", "diffed", "exped", "scaled", "product", "picked", "zeroed", "decayed", "end_diffed",
                "end_exped", "end_scaled", "turned", "turned_copied", "u_made", "state", "out_made", "added")))
        block = ctx.enter_context(nc.Block())

        def halves(ap, m):
            return ap.rearrange("p (b two m) -> p b two m", two=2, m=m)

        q_half, k_half = (1, 0) if d == 0 else (0, 1)

        @block.sync
        def _(sp):
            sp.dma_start(mask[:].rearrange("p l t -> p (l t)"),
                         core.const("levels" if d == 0 else "levels_back")).then_inc(loaded, 16)

        @block.gpsimd
        def _(pool):
            nc.gpsimd.memset(qs[:], 0.0).then_inc(zeroed, 1)
            nc.gpsimd.memset(ks[:], 0.0).then_inc(zeroed, 1)
            nc.gpsimd.memset(A[:], 0.0).then_inc(zeroed, 1)
            nc.gpsimd.memset(S[:, order[0], :], 0.0).then_inc(zeroed, 1)
            for h in range(HG_H):
                g = G[:, h, :].rearrange("p (c t) -> p c t", t=P)
                if h >= 2:
                    pool.wait_ge(end_scaled, h - 1)
                e = (kd if d == 0 else qe)[:, h % 2, :].rearrange("p (c t) -> p c t", t=P)
                if h >= 2:
                    pool.wait_ge(out_made, h - 1)
                nc.gpsimd.tensor_tensor(e, total[:, h, :].unsqueeze(2).to_broadcast([P, TT, P]), g,
                                        ALU.subtract).then_inc(end_diffed, 1)
                for i, m in enumerate(LEVELS):
                    n = h * NL + i
                    if n >= R:
                        pool.wait_ge(exped, n - R + 1)
                    src = halves(G[:, h, :], m)
                    edge = src[:, :, 0, m - 1:m] if d == 0 else src[:, :, 1, 0:1]
                    nb = T // (2 * m)
                    flat = G[:, h, :].rearrange("p (b m) -> p b m", m=2 * m)
                    nc.gpsimd.tensor_tensor(diff[:, n % R, :].rearrange("p (b m) -> p b m", m=2 * m), flat,
                                            edge.to_broadcast([P, nb, 2 * m]), ALU.subtract).then_inc(diffed, 1)

        @block.scalar
        def _(act):
            nc.scalar.activation(dec[:], total[:], ACT.Exp).then_inc(decayed, 1)

            def turned_out(h):
                act.wait_ge(turned, h + 1)
                nc.scalar.copy(kdT[:], B[4][:]).then_inc(turned_copied, 1)

            for h in range(HG_H):
                act.wait_ge(end_diffed, h + 1)
                one, other = (kd, qe) if d == 0 else (qe, kd)
                nc.scalar.activation(one[:, h % 2, :], one[:, h % 2, :], ACT.Exp)
                nc.scalar.activation(other[:, h % 2, :], G[:, h, :], ACT.Exp).then_inc(end_exped, 1)
                for i, m in enumerate(LEVELS):
                    n = h * NL + i
                    act.wait_ge(diffed, n + 1)
                    if n < R:
                        act.wait_ge(zeroed, 2)
                    else:
                        act.wait_ge(product, h * NM + i - R + (0 if i >= R else 0) + 1 if i >= R else
                                    (h - 1) * NM + NL + i - R + 1)
                    src, qd, kk = (halves(x[:, n % R, :], m) for x in (diff, qs, ks))
                    nc.scalar.activation(qd[:, :, q_half, :], src[:, :, q_half, :], ACT.Exp,
                                         scale=1.0 if d == 0 else -1.0)
                    nc.scalar.activation(kk[:, :, k_half, :], src[:, :, k_half, :], ACT.Exp,
                                         scale=-1.0 if d == 0 else 1.0).then_inc(exped, 1)
                    if i == 2:
                        turned_out(h)

        @block.vector
        def _(dve):
            vec = nc.vector
            dve.wait_ge(loaded, 16)
            dve.wait_ge(zeroed, 4)
            dve.wait_ge(decayed, 1)

            def pick(h, j):
                n = h * NM + j
                dve.wait_ge(product, n + 1)
                dve.wait_ge(out_made, h - 1) if h >= 2 and j == 0 else None
                if n:
                    dve.wait_ge(picked, n)
                vec.copy_predicated(A[:, h % 2, :].rearrange("p (c t) -> p c t", t=P),
                                    mask[:, j, :].bitcast(U32).unsqueeze(1).to_broadcast([P, TT, P]),
                                    B[n % 4][:].rearrange("p (c t) -> p c t", t=P)).then_inc(picked, 1)

            def finish(h):
                dve.wait_ge(out_made, h + 1)
                vec.tensor_tensor(y[:, h, :], y[:, h, :], B[6 + h % 2][:], ALU.add).then_inc(added, 1)

            for h in range(HG_H):
                dve.wait_ge(end_exped, h + 1)
                vec.tensor_tensor(qe[:, h % 2, :], qe[:, h % 2, :], q[:, h, :], ALU.mult)
                vec.tensor_tensor(kd[:, h % 2, :], kd[:, h % 2, :], kh[:, h, :], ALU.mult).then_inc(end_scaled, 1)
                for i, m in enumerate(LEVELS):
                    n = h * NL + i
                    dve.wait_ge(exped, n + 1)
                    qd, qq, kk, kq = (halves(x, m) for x in (qs[:, n % R, :], q[:, h, :], ks[:, n % R, :], kh[:, h, :]))
                    vec.tensor_tensor(qd[:, :, q_half, :], qd[:, :, q_half, :], qq[:, :, q_half, :], ALU.mult)
                    vec.tensor_tensor(kk[:, :, k_half, :], kk[:, :, k_half, :], kq[:, :, k_half, :],
                                      ALU.mult).then_inc(scaled, 1)
                    if i >= 1:
                        pick(h, i - 1)
                    if i == 1 and h:
                        finish(h - 1)
                    if i == 4:
                        for j, c in enumerate(order[:-1]):
                            dve.wait_ge(u_made, h + 1)
                            if h or j:
                                dve.wait_ge(state, (TT - 1) * h + j)
                            if h and j == 0:
                                dve.wait_ge(out_made, h)
                            vec.scalar_tensor_tensor(out=S[:, order[j + 1], :], in0=S[:, c, :],
                                                     scalar=dec[:, h, c:c + 1], in1=B[5][:, c * P:(c + 1) * P],
                                                     op0=ALU.mult, op1=ALU.add).then_inc(state, 1)
                pick(h, NL - 1)
                pick(h, NL)
            finish(HG_H - 1)

        @block.tensor
        def _(pe):
            def pairs(h, j, right, left):
                n = h * NM + j
                if n >= 4:
                    pe.wait_ge(picked, n - 3)
                for c in range(TT):
                    cols = slice(c * P, (c + 1) * P)
                    mm = nc.tensor.matmul(B[n % 4][:, cols], left[:, cols], right[:, cols], start=True, stop=True)
                mm.then_inc(product, 1)

            def output(h):
                pe.wait_ge(picked, NM * (h + 1))
                pe.wait_ge(state, (TT - 1) * (h + 1))
                if h >= 2:
                    pe.wait_ge(added, h - 1)
                out = B[6 + h % 2]
                for c in range(TT):
                    cols = slice(c * P, (c + 1) * P)
                    nc.tensor.matmul(out[:, cols], v_tm[:, c, h * P:(h + 1) * P], A[:, h % 2, cols], start=True,
                                     stop=False)
                    mm = nc.tensor.matmul(out[:, cols], S[:, c, :], qe[:, h % 2, cols], start=False, stop=True)
                mm.then_inc(out_made, 1)

            for h in range(HG_H):
                for i in range(NL):
                    n = h * NL + i
                    pe.wait_ge(scaled, n + 1)
                    pairs(h, i, qs[:, n % R, :], ks[:, n % R, :])
                    if i == 0:
                        pe.wait_ge(end_scaled, h + 1)
                        if h:
                            pe.wait_ge(turned_copied, h)
                        for c in range(TT):
                            cols = slice(c * P, (c + 1) * P)
                            mm = nc.tensor.transpose(B[4][:, cols], kd[:, h % 2, cols], ident[:])
                        mm.then_inc(turned, 1)
                        if h:
                            output(h - 1)
                    if i == 3:
                        pe.wait_ge(turned_copied, h + 1)
                        if h:
                            pe.wait_ge(state, (TT - 1) * h)
                        for c in range(TT):
                            cols = slice(c * P, (c + 1) * P)
                            mm = nc.tensor.matmul(B[5][:, cols], kdT[:, cols], v_tm[:, c, h * P:(h + 1) * P],
                                                  start=True, stop=True)
                        mm.then_inc(u_made, 1)
                pairs(h, NL, q[:, h, :], kh[:, h, :])
            output(HG_H - 1)


def turn_out(core, iv, v_tm, ident):
    nc = core.nc
    B = core.bank
    with ExitStack() as ctx:
        turned, copied = sems(nc, ctx, "tv_turned", "tv_copied")
        block = ctx.enter_context(nc.Block())

        @block.tensor
        def _(pe):
            for n in range(8):
                for j in range(4):
                    t, k = n // 2, 4 * (n % 2) + j
                    mm = nc.tensor.transpose(B[n][:, j * P:(j + 1) * P], iv[:, k, t * P:(t + 1) * P], ident[:])
                mm.then_inc(turned, 1)

        @block.scalar
        def _(act):
            for n in range(8):
                act.wait_ge(turned, n + 1)
                nc.scalar.copy(v_tm[:, n // 2, (n % 2) * 512:(n % 2 + 1) * 512], B[n][:]).then_inc(copied, 1)


def zero_tiles(core, y):
    nc = core.nc
    with ExitStack() as ctx:
        (zeroed,) = sems(nc, ctx, "y_zeroed")
        block = ctx.enter_context(nc.Block())

        @block.vector
        def _(dve):
            nc.vector.memset(y[:], 0.0).then_inc(zeroed, 1)


def hgrn_norm(core, y, gain, gate, ones, scratch):
    nc = core.nc
    B = core.bank
    with ExitStack() as ctx:
        (eps_col,) = bufs(nc, ctx, "hn", eps=[P, 1])
        eps_set, squared, summed, rooted, inverted, normed, done = sems(
            nc, ctx, *(f"hn_{s}" for s in ("eps", "squared", "summed", "rooted", "inverted", "normed", "done")))
        block = ctx.enter_context(nc.Block())

        @block.gpsimd
        def _(pool):
            nc.gpsimd.memset(eps_col[:], EPS).then_inc(eps_set, 1)

        @block.scalar
        def _(act):
            for k in range(HG_H):
                nc.scalar.activation(scratch[:, k, :], y[:, k, :], ACT.Square).then_inc(squared, 1)
            act.wait_ge(eps_set, 1)
            for k in range(HG_H):
                act.wait_ge(summed, k + 1)
                nc.scalar.activation(scratch[:, k, :], B[k][:], ACT.Sqrt, bias=eps_col[:],
                                     scale=1.0 / P).then_inc(rooted, 1)

        @block.tensor
        def _(pe):
            for k in range(HG_H):
                pe.wait_ge(squared, k + 1)
                nc.tensor.matmul(B[k][:], ones[:], scratch[:, k, :], start=True, stop=True).then_inc(summed, 1)

        @block.vector
        def _(dve):
            for k in range(HG_H):
                dve.wait_ge(rooted, k + 1)
                nc.vector.reciprocal(scratch[:, k, :], scratch[:, k, :]).then_inc(inverted, 1)
                dve.wait_ge(inverted, k + 1)
                nc.vector.tensor_tensor(y[:, k, :], y[:, k, :], scratch[:, k, :], ALU.mult).then_inc(normed, 1)
                dve.wait_ge(normed, k + 1)
                nc.vector.scalar_tensor_tensor(out=y[:, k, :], in0=y[:, k, :], scalar=gain[:], in1=gate[:, k, :],
                                               op0=ALU.mult, op1=ALU.mult).then_inc(done, 1)


def lower_bounds(core, raw, lower, gain1, w1, s1, gain2, w2, s2):
    nc = core.nc
    floor_log, rest_log, rest, _ = lower
    SCALE = 2.0 ** 64
    with ExitStack() as ctx:
        e, s, lb = bufs(nc, ctx, "lb", e=[P, 2 * KT], s=[P, 2 * KT], lb=[P, 2 * KT])
        step, to_act, from_act = sems(nc, ctx, "lb_step", "lb_to_act", "lb_from_act")
        block = ctx.enter_context(nc.Block())

        @block.scalar
        def _(act):
            act.wait_ge(to_act, 1)
            nc.scalar.activation(e[:], e[:], ACT.Exp).then_inc(from_act, 1)
            act.wait_ge(to_act, 2)
            nc.scalar.activation(floor_log[:], lb[:], ACT.Ln, scale=SCALE)
            nc.scalar.activation(rest_log[:], rest[:], ACT.Ln).then_inc(from_act, 1)

        @block.vector
        def _(dve):
            steps = Count(step)

            def after(instruction):
                dve.wait_ge(step, steps.by(instruction))

            vec = nc.vector
            vec.tensor_tensor(e[:], raw[:], raw[:], ALU.subtract).then_inc(to_act, 1)
            dve.wait_ge(from_act, 1)
            after(vec.reciprocal(s[:], e[:]))
            after(vec.tensor_tensor(e[:], e[:], s[:], ALU.mult))
            after(vec.tensor_tensor(lb[:], e[:], e[:], ALU.subtract))
            after(vec.tensor_scalar(rest[:], lb[:], -1.0, 1.0, ALU.mult, ALU.add))
            vec.tensor_scalar(lb[:], lb[:], LB_FLOOR, None, ALU.max).then_inc(to_act, 1)
            vec.tensor_tensor(gain1[:], w1[:], s1, ALU.mult)
            vec.tensor_tensor(gain2[:], w2[:], s2, ALU.mult)
            dve.wait_ge(from_act, 2)
            after(vec.tensor_scalar(floor_log[:], floor_log[:], -64.0 * math.log(2.0), None, ALU.add))


def third_columns(core, ctx, a):
    nc = core.nc
    shapes = dict(ada_b=48, norm_mix_w=8, norm_mlp_w=8, conv_b=XT, ssd_norm_w=8, hg_norm_w=1)
    c = dict(zip(shapes, bufs(nc, ctx, "c3", **{n: [P, w] for n, w in shapes.items()})))
    more = dict(conv_w=[P, XT, SSD_CONV], final=[P, KT], raw_lb=[P, 2 * KT], skip=[P, KT],
                dt_bias=[SSD_H, 2], a_log=[SSD_H, 2], gain1=[P, KT], gain2=[P, KT], floor_log=[P, 2 * KT],
                rest_log=[P, 2 * KT], rest=[P, 2 * KT], total=[P, KT, TT])
    c.update(zip(more, bufs(nc, ctx, "c3", **more)))
    load_columns(core, [(c[n][:], a[f"{n}_3"][0]) for n in shapes]
                 + [(c["conv_w"][:, :, j], a["conv_w_3"][0, j]) for j in range(SSD_CONV)]
                 + [(c["final"][:], a["final_norm_w_3"])]
                 + [(c["raw_lb"][:, KT * d:KT * (d + 1)], a["hg_lower_bounds_3"][d, 0]) for d in range(2)])
    with ExitStack() as s:
        (loaded,) = sems(nc, s, "c3_loaded")
        block = s.enter_context(nc.Block())

        @block.sync
        def _(sp):
            with nc.allow_non_contiguous_dma("columns"):
                sp.dma_start(c["dt_bias"][:], a["dt_bias_3"][0].rearrange("d h -> h d")).then_inc(loaded, 16)
                sp.dma_start(c["a_log"][:], a["a_log_3"][0].rearrange("d h -> h d")).then_inc(loaded, 16)
                for half in range(2):
                    sp.dma_start(c["skip"][64 * half:64 * half + 64, :],
                                 bcast_rows(a["d_skip_3"][:, half:SSD_H:2], 64)).then_inc(loaded, 16)
            sp.wait_ge(loaded, 64)
    return c


def store_out(core, xT, ident, out):
    nc = core.nc
    B = core.bank
    with ExitStack() as ctx:
        (rows,) = bufs(nc, ctx, "so", rows=[P, TT, D])
        turned, copied, stored = sems(nc, ctx, "so_turned", "so_copied", "so_stored")
        block = ctx.enter_context(nc.Block())

        @block.tensor
        def _(pe):
            for n in range(8):
                for j in range(4):
                    t, k = n // 2, 4 * (n % 2) + j
                    mm = nc.tensor.transpose(B[n][:, j * P:(j + 1) * P], xT[:, k, t * P:(t + 1) * P], ident[:])
                mm.then_inc(turned, 1)

        @block.scalar
        def _(act):
            for n in range(8):
                act.wait_ge(turned, n + 1)
                nc.scalar.copy(rows[:, n // 2, (n % 2) * 512:(n % 2 + 1) * 512], B[n][:]).then_inc(copied, 1)

        @block.sync
        def _(sp):
            for t in range(TT):
                sp.wait_ge(copied, 2 * t + 2)
                sp.dma_start(out[0, t * P:(t + 1) * P, :], rows[:, t, :]).then_inc(stored, 16)
            sp.wait_ge(stored, 16 * TT)


def third_block(core, a, xT, hT, ident, ones, out):
    nc = core.nc
    w_in = a["w_in_3"][0]
    with ExitStack() as ctx:
        c = third_columns(core, ctx, a)
        mod = core.mod3
        finish_modulation(core, "mod3", mod, c["ada_b"])
        lower = (c["floor_log"], c["rest_log"], c["rest"], c["total"])
        lower_bounds(core, c["raw_lb"], lower, c["gain1"], c["norm_mix_w"], mod[:, 8:16], c["gain2"],
                     c["norm_mlp_w"], mod[:, 32:40])
        with ExitStack() as s:
            (ycat,) = bufs(nc, s, "b3", ycat=[P, 2 * KT, T])
            y_ssd, y_hg = ycat[:, 0:KT, :], ycat[:, KT:2 * KT, :]
            norm(core, "n9", xT, hT, ones, y_hg, c["gain1"], mod[:, 0:8])
            with ExitStack() as r:
                zs, dt_raw = bufs(nc, r, "b3", zs=[P, KT, T], dt_raw=[SSD_H, T])
                with ExitStack() as q:
                    xbc, = bufs(nc, q, "b3", xbc=[P, XT, T])
                    ssd_inputs(core, hT, w_in, c["conv_w"], c["conv_b"], zs, xbc, dt_raw)
                    b_tm, scores = bufs(nc, q, "b3", b_tm=[P, TT, SSD_G * P], scores=[P, SSD_G, T])
                    x_tm = y_hg.rearrange("p (t a) c -> p t (a c)", a=2)
                    ssd_prepare(core, xbc, x_tm, b_tm, scores, y_ssd, c["skip"], ident)
                    for d in range(2):
                        ssd_direction(core, d, xbc, x_tm, b_tm, scores, dt_raw, c["dt_bias"], c["a_log"], y_ssd,
                                      ones, ident)
                multiply_tiles(core, "z", y_ssd, zs)
                norm(core, "n10", y_ssd, y_ssd, ones, y_hg, c["ssd_norm_w"])
            with ExitStack() as r:
                hq, ff, fb, gs = bufs(nc, r, "b3", hq=[P, KT, T], ff=[P, KT, T], fb=[P, KT, T], gs=[P, KT, T])
                dests = (hq, ff, fb, y_hg, gs)

                def emit(i, b, bank):
                    return nc.scalar.activation(dests[i][:, b, :], bank[:], ACT.Silu if i == 4 else ACT.Identity)

                linear(core, "hin", w_in[:, 1024 + XBC + SSD_H:], 5, hT, ("scalar", emit))
                v_tm = hT[:].rearrange("p (t a) c -> p t (a c)", a=2)
                turn_out(core, y_hg, v_tm, ident)
                zero_tiles(core, y_hg)
                with ExitStack() as q:
                    (kh,) = bufs(nc, q, "b3", kh=[P, KT, T])
                    for d, f in enumerate((ff, fb)):
                        hgrn_gates(core, d, f, kh, lower)
                        hgrn_direction(core, d, hq, f, kh, c["total"], v_tm, y_hg, ident)
                hgrn_norm(core, y_hg, c["hg_norm_w"], gs, ones, hq)

            def add_gated(first):
                def emit(i, b, bank):
                    return nc.vector.scalar_tensor_tensor(out=xT[:, b, :], in0=bank[:],
                                                          scalar=mod[:, first + b:first + b + 1], in1=xT[:, b, :],
                                                          op0=ALU.mult, op1=ALU.add)
                return ("vector", emit)

            linear(core, "wo3", a["w_out_3"][0], 2, ycat, add_gated(16), stacked=True)
        with ExitStack() as s:
            (up,) = bufs(nc, s, "b3", up=[P, 32, T])
            norm(core, "n11", xT, hT, ones, up[:, 0:KT, :], c["gain2"], mod[:, 24:32])
            (squared,) = sems(nc, s, "up_squared")

            def emit(i, b, bank):
                return nc.scalar.activation(up[:, 8 * i + b, :], bank[:], ACT.Relu)

            def square(block, copied):
                @block.vector
                def _(dve):
                    for n in range(32):
                        dve.wait_ge(copied, n + 1)
                        nc.vector.tensor_tensor(up[:, n, :], up[:, n, :], up[:, n, :], ALU.mult).then_inc(squared, 1)

            linear(core, "up", a["w_up_3"][0], 4, hT, ("scalar", emit), more=square)
            linear(core, "down", a["w_down_3"][0], 4, up, add_gated(40), stacked=True)
        norm(core, "n12", xT, xT, ones, hT, c["final"])
        store_out(core, xT, ident, out)


def build(nc, a, out):
    USED.clear()
    with ExitStack() as ctx:
        core = Core(nc, ctx, a["consts"])
        xT, hT, ident, ones = bufs(nc, ctx, "all", xT=[P, KT, T], hT=[P, KT, T], ident=[P, P], ones=[P, P])
        core.mod2, core.mod3 = bufs(nc, ctx, "all", mod2=[P, 48], mod3=[P, 48])
        core.block_gathered = ctx.enter_context(nc.semaphore("moe_gathered"))
        core.combine_gathered = [ctx.enter_context(nc.semaphore(f"combine_gathered{s}")) for s in range(4)]
        load_x(core, a["x"][0], xT, ident, ones)
        first_block(core, a, xT, hT, ident, ones)
        second_block(core, a, xT, hT, ident, ones)
        third_block(core, a, xT, hT, ident, ones, out)




def kernel(**inputs):
    import numpy as _np
    import concourse.bacc as _bacc
    from concourse import mybir as _mybir
    from concourse.bass_utils import run_bass_kernel_spmd as _run

    nc = _bacc.Bacc("TRN2", target_bir_lowering=False, num_devices=1)
    arrays, args = {}, {}
    for name, value in inputs.items():
        v = _np.ascontiguousarray(value)
        arrays[f"in_{name}_dram"] = v
        args[name] = nc.dram_tensor(f"in_{name}_dram", v.shape, _mybir.dt.from_np(v.dtype), kind="ExternalInput").ap()
    consts = _np.concatenate([_np.asarray(c, _np.float32) for c in constant_parts().values()], axis=1)
    arrays["consts_dram"] = _np.ascontiguousarray(consts)
    args["consts"] = nc.dram_tensor("consts_dram", consts.shape, _mybir.dt.float32, kind="ExternalInput").ap()
    args["bias_dram"] = nc.dram_tensor("bias_by_distance", (DSA_H, 5 * P), _mybir.dt.float32, kind="Internal").ap()
    args["h_dram"] = nc.dram_tensor("h_rows", (T, D), _mybir.dt.float32, kind="Internal").ap()
    args["y_dram"] = nc.dram_tensor("expert_rows", (N_TABLE * P, D), _mybir.dt.float32, kind="Internal").ap()
    out = nc.dram_tensor("out_0_dram", (1, T, D), _mybir.dt.float32, kind="ExternalOutput").ap()
    build(nc, args, out)
    r = _run(nc, [arrays], core_ids=[0])
    return r.results[0]["out_0_dram"]
```
